# Optimizing a Trainium2 kernel written in Bass

```python
import math
import jax, jax.numpy as jnp
from jax import lax
import numpy as np

D_MODEL = 2048
BATCH = 1
SEQ = 256
DEPTH = 1
DEC_BATCH = 8
DEC_SEQ = 4
PAST_LEN = 2048
PAGE_SIZE = 128

N_HEADS = 16
HEAD_DIM = 64
ATTN_WIDTH = N_HEADS * HEAD_DIM
POOL_WIDTH = D_MODEL - ATTN_WIDTH
IN_WIDTH = 3 * ATTN_WIDTH + POOL_WIDTH
POOL_WINDOWS = (2, 4, 8, 16)
N_POOL_GROUPS = len(POOL_WINDOWS)
POOL_GROUP_WIDTH = POOL_WIDTH // N_POOL_GROUPS
POOL_BUF = max(POOL_WINDOWS) - 1
DILATED = ((128, 1), (512, 4), (2048, 16))
MAX_WINDOW = max(w for w, _ in DILATED)
QBLOCK = 128
NUM_BUCKETS = 32
MAX_DISTANCE = MAX_WINDOW
N_GROUPS = 4
EXPERTS_PER_GROUP = 4
N_EXPERTS = N_GROUPS * EXPERTS_PER_GROUP
TOP_K_INNER = 2
D_EXPERT = 512
EPS = 1e-6
SCALE = HEAD_DIM ** -0.5
NEG_INF = -1e30

kernel_name = 'hymba_pool_dilated_hmoe_step'

def _rms_norm(x, g):
    xf = x.astype(jnp.float32)
    y = xf * lax.rsqrt(jnp.mean(xf * xf, axis=-1, keepdims=True) + EPS)
    return (y * g.astype(jnp.float32)).astype(x.dtype)

def _rel_bucket(dist):
    max_exact = NUM_BUCKETS // 2
    df = jnp.maximum(dist, 1).astype(jnp.float32)
    large = max_exact + (jnp.log(df / max_exact) / math.log(MAX_DISTANCE / max_exact)
                         * (NUM_BUCKETS - max_exact)).astype(jnp.int32)
    large = jnp.minimum(large, NUM_BUCKETS - 1)
    return jnp.where(dist < max_exact, dist, large)

def _branch_bias(rel_bias, dilation, n_steps):
    j = jnp.arange(n_steps + 1, dtype=jnp.int32)
    return rel_bias[_rel_bucket(j * dilation)].astype(jnp.float32)

def _mixer_inputs(x, ln1_w, w_in, q_norm_w, k_norm_w):
    n, L, _ = x.shape
    z = _rms_norm(x, ln1_w) @ w_in
    q = z[..., :ATTN_WIDTH].reshape(n, L, N_HEADS, HEAD_DIM)
    k = z[..., ATTN_WIDTH:2 * ATTN_WIDTH].reshape(n, L, N_HEADS, HEAD_DIM)
    v = z[..., 2 * ATTN_WIDTH:3 * ATTN_WIDTH].reshape(n, L, N_HEADS, HEAD_DIM)
    u = z[..., 3 * ATTN_WIDTH:]
    return _rms_norm(q, q_norm_w), _rms_norm(k, k_norm_w), v, u

def _softmax_stats(scores, valid):
    s = jnp.where(valid, scores, NEG_INF)
    m = jnp.max(s, axis=-1, keepdims=True)
    p = jnp.exp(s - m)
    den = jnp.sum(p, axis=-1, keepdims=True)
    return p / den, m[..., 0] + jnp.log(den[..., 0])

def _dilated_prompt(q, k, v, bias_j, dilation, n_steps):
    b, s, h, hd = q.shape
    L = s // dilation
    n = b * dilation
    nb = -(-L // QBLOCK)
    lp = nb * QBLOCK

    def to_res(t):
        return t.reshape(b, L, dilation, h, hd).transpose(0, 2, 1, 3, 4).reshape(n, L, h, hd)

    qb = jnp.pad(to_res(q), ((0, 0), (0, lp - L), (0, 0), (0, 0))).reshape(n, nb, QBLOCK, h, hd)

    def key_windows(t):
        tp = jnp.pad(to_res(t), ((0, 0), (QBLOCK, lp - L), (0, 0), (0, 0)))
        tp = tp.reshape(n, nb + 1, QBLOCK, h, hd)
        return jnp.concatenate([tp[:, :-1], tp[:, 1:]], axis=2)

    kw, vw = key_windows(k), key_windows(v)
    qi = jnp.arange(QBLOCK)[:, None]
    kk = jnp.arange(2 * QBLOCK)[None, :]
    j = qi + QBLOCK - kk
    key_pos = jnp.arange(nb)[:, None, None] * QBLOCK - QBLOCK + kk[None]
    valid = ((j >= 0) & (j <= n_steps))[None] & (key_pos >= 0)
    bias = bias_j[jnp.clip(j, 0, n_steps)].transpose(2, 0, 1)
    scores = jnp.einsum('nbqhd,nbkhd->nbhqk', qb, kw,
                        preferred_element_type=jnp.float32) * SCALE + bias[None, None]
    p, lse = _softmax_stats(scores, valid[None, :, None])
    o = jnp.einsum('nbhqk,nbkhd->nbqhd', p, vw.astype(jnp.float32))
    lse = lse.transpose(0, 1, 3, 2)

    def from_res(t):
        t = t.reshape((n, lp) + t.shape[3:])[:, :L]
        t = t.reshape((b, dilation, L) + t.shape[2:]).swapaxes(1, 2)
        return t.reshape((b, s) + t.shape[3:])

    return from_res(o), from_res(lse)

def _dilated_sample(q, k_all, v_all, bias_j, dilation, n_steps, q_offset):
    T = q.shape[1]
    steps = jnp.arange(n_steps + 1)
    idx = (q_offset + jnp.arange(T))[:, None] - steps[None, :] * dilation
    valid = idx >= 0
    idx = jnp.maximum(idx, 0)
    kg = k_all[:, idx]
    vg = v_all[:, idx]
    scores = jnp.einsum('bthd,btjhd->bhtj', q, kg,
                        preferred_element_type=jnp.float32) * SCALE + bias_j.T[None, :, None, :]
    p, lse = _softmax_stats(scores, valid[None, None])
    o = jnp.einsum('bhtj,btjhd->bthd', p, vg.astype(jnp.float32))
    return o, lse.transpose(0, 2, 1)

def _merge_branches(results):
    o = jnp.stack([r[0] for r in results])
    lse = jnp.stack([r[1] for r in results])
    w = jax.nn.softmax(lse, axis=0)
    return jnp.sum(w[..., None] * o, axis=0)

def _pool_mix(u, prefix, start, w_pool, pool_scale):
    n, L, C = u.shape
    comb = jnp.concatenate([prefix.astype(u.dtype), u], axis=1)
    cs = jnp.cumsum(comb.astype(jnp.float32), axis=1)
    cs = jnp.concatenate([jnp.zeros((n, 1, C), jnp.float32), cs], axis=1)
    uf = u.astype(jnp.float32)
    pos = start + jnp.arange(L)
    parts = []
    for gi, w in enumerate(POOL_WINDOWS):
        sl = slice(gi * POOL_GROUP_WIDTH, (gi + 1) * POOL_GROUP_WIDTH)
        win_sum = cs[:, POOL_BUF + 1:POOL_BUF + 1 + L, sl] - cs[:, POOL_BUF + 1 - w:POOL_BUF + 1 - w + L, sl]
        cnt = jnp.minimum(pos + 1, w).astype(jnp.float32)[None, :, None]
        parts.append(win_sum / cnt - uf[..., sl])
    d = jnp.stack(parts, axis=2)
    y = jnp.einsum('nlgc,gce->nlge', d, w_pool.astype(jnp.float32)).reshape(n, L, C)
    y = y * pool_scale.astype(jnp.float32)
    return y.astype(u.dtype), comb[:, -POOL_BUF:]

def _hier_moe(h, w_rg, b_rg, w_re, b_re, w_gate, w_up, w_down):
    n, L, D = h.shape
    hf = h.reshape(n * L, D)
    lg = (hf @ w_rg).astype(jnp.float32) + b_rg.astype(jnp.float32)
    pg = jax.nn.softmax(lg, axis=-1)
    g_top = jnp.argmax(lg, axis=-1)
    p_top = jnp.take_along_axis(pg, g_top[:, None], axis=-1)[:, 0]
    le = ((hf @ w_re).astype(jnp.float32) + b_re.astype(jnp.float32)).reshape(-1, N_GROUPS, EXPERTS_PER_GROUP)
    le_g = jnp.take_along_axis(le, g_top[:, None, None], axis=1)[:, 0]
    top_v, top_i = lax.top_k(le_g, TOP_K_INNER)
    pe = jax.nn.softmax(top_v, axis=-1)
    eidx = g_top[:, None] * EXPERTS_PER_GROUP + top_i
    gates = jnp.sum(jax.nn.one_hot(eidx, N_EXPERTS, dtype=jnp.float32)
                    * (p_top[:, None] * pe)[..., None], axis=1)
    a = jnp.einsum('nd,edf->nef', hf, w_gate)
    b = jnp.einsum('nd,edf->nef', hf, w_up)
    hid = jax.nn.silu(a) * b * gates[..., None].astype(a.dtype)
    y = jnp.einsum('nef,efd->nd', hid, w_down)
    return y.reshape(n, L, D)

def _block_output(x, attn, pool, w_o, ln2_w, w_rg, b_rg, w_re, b_re, w_gate, w_up, w_down):
    n, L, _ = x.shape
    mix = jnp.concatenate([attn.reshape(n, L, ATTN_WIDTH).astype(x.dtype), pool.astype(x.dtype)], axis=-1)
    x = x + mix @ w_o
    return x + _hier_moe(_rms_norm(x, ln2_w), w_rg, b_rg, w_re, b_re, w_gate, w_up, w_down)

def setup_inputs(seed: int = 0) -> dict:
    key = jax.random.key(seed)
    ks = jax.random.split(key, 24)
    win_buf = min(MAX_WINDOW, PAST_LEN)
    nrm = jax.random.normal

    def w(k, shape, fan_in):
        return nrm(k, shape, jnp.float32) * fan_in ** -0.5

    return {
        'x_prompt': nrm(ks[0], (BATCH, SEQ, D_MODEL), jnp.float32),
        'x_sample': nrm(ks[1], (DEC_BATCH, DEC_SEQ, D_MODEL), jnp.float32),
        'cache_k': nrm(ks[2], (DEPTH, DEC_BATCH, win_buf, N_HEADS, HEAD_DIM), jnp.float32),
        'cache_v': nrm(ks[3], (DEPTH, DEC_BATCH, win_buf, N_HEADS, HEAD_DIM), jnp.float32),
        'state_pool': nrm(ks[4], (DEPTH, DEC_BATCH, POOL_BUF, POOL_WIDTH), jnp.float32),
        'rel_bias': 0.5 * nrm(ks[5], (NUM_BUCKETS, N_HEADS), jnp.float32),
        'ln1_w': 1.0 + 0.1 * nrm(ks[6], (DEPTH, D_MODEL), jnp.float32),
        'w_in': w(ks[7], (DEPTH, D_MODEL, IN_WIDTH), D_MODEL),
        'q_norm_w': 1.0 + 0.1 * nrm(ks[8], (DEPTH, HEAD_DIM), jnp.float32),
        'k_norm_w': 1.0 + 0.1 * nrm(ks[9], (DEPTH, HEAD_DIM), jnp.float32),
        'w_pool': w(ks[10], (DEPTH, N_POOL_GROUPS, POOL_GROUP_WIDTH, POOL_GROUP_WIDTH), POOL_GROUP_WIDTH),
        'pool_scale': 1.0 + 0.1 * nrm(ks[11], (DEPTH, POOL_WIDTH), jnp.float32),
        'w_o': w(ks[12], (DEPTH, D_MODEL, D_MODEL), D_MODEL),
        'ln2_w': 1.0 + 0.1 * nrm(ks[13], (DEPTH, D_MODEL), jnp.float32),
        'w_router_group': w(ks[14], (DEPTH, D_MODEL, N_GROUPS), D_MODEL),
        'b_router_group': 0.01 * nrm(ks[15], (DEPTH, N_GROUPS), jnp.float32),
        'w_router_expert': w(ks[16], (DEPTH, D_MODEL, N_EXPERTS), D_MODEL),
        'b_router_expert': 0.01 * nrm(ks[17], (DEPTH, N_EXPERTS), jnp.float32),
        'w_gate': w(ks[18], (DEPTH, N_EXPERTS, D_MODEL, D_EXPERT), D_MODEL),
        'w_up': w(ks[19], (DEPTH, N_EXPERTS, D_MODEL, D_EXPERT), D_MODEL),
        'w_down': w(ks[20], (DEPTH, N_EXPERTS, D_EXPERT, D_MODEL), D_EXPERT),
    }

def reference(x_prompt, x_sample, cache_k, cache_v, state_pool, rel_bias, ln1_w, w_in,
              q_norm_w, k_norm_w, w_pool, pool_scale, w_o, ln2_w, w_router_group,
              b_router_group, w_router_expert, b_router_expert, w_gate, w_up, w_down):
    biases = [_branch_bias(rel_bias, d, w // d) for (w, d) in DILATED]
    xp, xs = x_prompt, x_sample
    kp_l, vp_l, pp_l, ks_l, vs_l, ps_l = [], [], [], [], [], []
    for l in range(DEPTH):
        moe_w = (w_router_group[l], b_router_group[l], w_router_expert[l], b_router_expert[l],
                 w_gate[l], w_up[l], w_down[l])
        q, k, v, u = _mixer_inputs(xp, ln1_w[l], w_in[l], q_norm_w[l], k_norm_w[l])
        attn = _merge_branches([_dilated_prompt(q, k, v, bj, d, w // d)
                                for (w, d), bj in zip(DILATED, biases)])
        zeros_prefix = jnp.zeros((u.shape[0], POOL_BUF, u.shape[2]), u.dtype)
        pool, pbuf = _pool_mix(u, zeros_prefix, 0, w_pool[l], pool_scale[l])
        keep = min(MAX_WINDOW, xp.shape[1])
        kp_l.append(k[:, -keep:])
        vp_l.append(v[:, -keep:])
        pp_l.append(pbuf)
        xp = _block_output(xp, attn, pool, w_o[l], ln2_w[l], *moe_w)
        q, k, v, u = _mixer_inputs(xs, ln1_w[l], w_in[l], q_norm_w[l], k_norm_w[l])
        k_all = jnp.concatenate([cache_k[l].astype(k.dtype), k], axis=1)
        v_all = jnp.concatenate([cache_v[l].astype(v.dtype), v], axis=1)
        q_offset = cache_k.shape[2]
        attn = _merge_branches([_dilated_sample(q, k_all, v_all, bj, d, w // d, q_offset)
                                for (w, d), bj in zip(DILATED, biases)])
        pool, sbuf = _pool_mix(u, state_pool[l], PAST_LEN, w_pool[l], pool_scale[l])
        ks_l.append(k)
        vs_l.append(v)
        ps_l.append(sbuf)
        xs = _block_output(xs, attn, pool, w_o[l], ln2_w[l], *moe_w)
    return (xp, xs, jnp.stack(kp_l), jnp.stack(vp_l), jnp.stack(pp_l),
            jnp.stack(ks_l), jnp.stack(vs_l), jnp.stack(ps_l))


_drawn_inputs = setup_inputs


def setup_inputs(seed=0):
    import zlib

    import numpy as np

    out = dict(_drawn_inputs(seed))
    spreads = {}
    factors = {'q_norm_w': 2.925, 'b_router_group': 64.0, 'b_router_expert': 9.675}
    for name, (base, spread) in spreads.items():
        noise = np.random.default_rng([zlib.crc32(name.encode()), seed]).standard_normal(out[name].shape)
        drawn = base * np.exp(spread * noise) if base else spread * noise
        out[name] = __import__('jax').numpy.asarray(drawn.astype(out[name].dtype))
    for name, factor in factors.items():
        out[name] = (out[name] * factor).astype(out[name].dtype)
    return out
```

```python
from contextlib import ExitStack
import math

import numpy as np

import concourse.bass as bass
from concourse import mybir
from concourse.alu_op_type import AluOpType as ALU

F32 = mybir.dt.float32
I32 = mybir.dt.int32
ACT = mybir.ActivationFunctionType
AX = mybir.AxisListType

P = 128
D = 2048
DC = D // P
SEQ, DEC_B, DEC_T, PAST = 256, 8, 4, 2048
NS = DEC_B * DEC_T
TOK = SEQ + NS
CHUNKS = [(0, 128), (128, 128), (256, 32)]
H, HD = 16, 64
PAIRS = H // 2
AW = H * HD
PW = D - AW
IN_W = 3 * AW + PW
TILE = 512
POOL_W = (2, 4, 8, 16)
BUF = 15
GW = PW // 4
NB = 32
EPS = 1e-6
SCALE = HD ** -0.5
NEG = -1e30
FE = 512
NG, EPG = 4, 4
NE = NG * EPG
SLOTS = 6
SLOT = 4096
NEAR = 512
FAR = 96
ROWG = D + 8
KEYS = NEAR + 4 * FAR + NS
PASSES = 3


def counted(dist):
    d = np.asarray(dist)
    n = ((d <= 128).astype(int) + ((d <= 512) & (d % 4 == 0)) + ((d <= 2048) & (d % 16 == 0)))
    return np.where(d >= 0, n, 0)


def bucket(dist):
    d = np.maximum(np.asarray(dist), 1)
    df = d.astype(np.float32)
    large = 16 + (np.log(df / np.float32(16)) / np.float32(math.log(2048 / 16)) * np.float32(16)).astype(np.int32)
    return np.where(np.asarray(dist) < 16, np.maximum(dist, 0), np.minimum(large, NB - 1))


def log_count(dist):
    n = counted(dist)
    return np.where(n > 0, np.log(np.maximum(n, 1)), NEG).astype(np.float32)


def shape_constants():
    out = {}
    y = np.arange(384)
    dist = 255 - y
    one = np.zeros((33, 384), np.float32)
    one[np.clip(bucket(dist), 0, NB - 1), y] = 1.0
    one[32] = log_count(dist)
    cols = KEYS - NS + DEC_B * NS
    hot = np.zeros((4, NB, cols), np.float32)
    mask = np.full((4, 16, cols), NEG, np.float32)
    for t in range(4):
        near = np.array([[NEAR + t - 4 * p - j for p in range(128)] for j in range(4)]).ravel()
        far = np.array([[PAST + t - 16 * p - j for p in range(FAR)] for j in range(4)]).ravel()
        new = np.array([[t - k % 4 if k // 4 == b else -1 for k in range(NS)] for b in range(DEC_B)]).ravel()
        d = np.concatenate([near, far, new])
        hot[t, np.clip(bucket(d), 0, NB - 1), np.arange(cols)] = 1.0
        mask[t] = log_count(d)[None]
    bias = np.zeros((P, 384 + 2 * cols), np.float32)
    bias[:33, :384] = one
    bias[:, 384:384 + cols] = hot.reshape(P, cols)
    bias[:64, 384 + cols:] = mask.reshape(64, cols)
    out["c_bias"] = bias
    rows, l = np.arange(SEQ)[:, None], np.arange(SEQ)[None]
    pool = np.zeros((P, 4 * 256 + 4 * 128 + 2 * 4 * 32), np.float32)
    for g, w in enumerate(POOL_W):
        full = ((rows <= l) & (rows > l - w)) / np.minimum(l + 1, w) - (rows == l)
        pool[:, g * 256:(g + 1) * 256] = full[:128]
        pool[:, 1024 + g * 128:1024 + (g + 1) * 128] = full[128:, 128:]
        for b in range(DEC_B):
            for t in range(DEC_T):
                at = BUF + t
                for r in range(at - w + 1, at + 1):
                    if r < BUF:
                        pool[b * BUF + r, 1536 + g * 32 + b * 4 + t] = 1.0 / w
                    else:
                        pool[b * 4 + r - BUF, 1664 + g * 32 + b * 4 + t] = 1.0 / w
                pool[b * 4 + t, 1664 + g * 32 + b * 4 + t] -= 1.0
    out["c_pool"] = pool
    eye = np.eye(P, dtype=np.float32)
    out["c_eye"] = np.concatenate([eye, eye[::-1]], axis=1).copy()
    r = np.zeros((P, 2 * P + 3 * P + 3 + 3 + 3), np.float32)
    r[:, :P] = np.triu(np.ones((P, P), np.float32), 1)
    r[:, P:2 * P] = 1.0
    r[:, 2 * P:5 * P] = np.arange(3 * P)[None]
    for k, (t0, n) in enumerate(CHUNKS):
        r[:, 5 * P + k] = t0 + np.arange(P)
        r[:n, 5 * P + 3 + k] = 1.0
        r[:, 5 * P + 6 + k] = TOK + np.arange(P)
    out["c_route"] = r
    return out


class Steps:

    def __init__(self, eng, sem):
        self.eng, self.sem, self.n = eng, sem, 0
        self.turn = None

    def did(self, ins):
        ins.then_inc(self.sem, 1)
        self.n += 1

    def settle(self):
        self.eng.wait_ge(self.sem, self.n if self.turn is None else self.turn + self.n)

    def begin(self, turn, per):
        self.outer, self.per = self.n, per
        self.turn, self.n = turn * per, self.n

    def end(self, turns):
        assert self.n - self.outer == self.per, (self.n - self.outer, self.per)
        self.turn, self.n = None, self.outer + self.per * turns


def hybrid_layer(nc, a, o):
    ctx = ExitStack()
    with ctx:
        build(nc, a, o, ctx)


def build(nc, a, o, ctx):
    def sb(name, shape, dt=F32):
        return ctx.enter_context(nc.sbuf_tensor(name, shape, dt))

    def sem(name):
        return ctx.enter_context(nc.semaphore(name))

    ring = sb("ring", [P, SLOTS, SLOT])
    HT = sb("HT", [P, DC * TOK])
    X = sb("X", [P, 3 * D])
    Z = sb("Z", [P, 3 * IN_W])
    eye2 = sb("eye2", [P, 2 * P])
    small = sb("small", [P, 16 + 16 + 128 + 8 + 16 * 20 + 1 + 64 + 16])
    E = sb("E", [64, KEYS - NS + DEC_B * NS])
    Qbd = sb("Qbd", [P, 520])
    qkTs = sb("qkTs", [P, 2, PAIRS, NS])
    stage = sb("stage", [P, 6, 256])
    stat = sb("stat", [P, 160])
    pidx = sb("pidx", [P, 32], I32)
    gS = sb("gS", [H, 384])
    PS = ctx.enter_context(nc.psum_tensor("PS", [P, 8, TILE], F32))

    hT = HT[:, :].rearrange("p (c t) -> p c t", t=TOK)
    x_rows = X[:, :].rearrange("p (c d) -> p c d", d=D)
    z = Z[:, :].rearrange("p (c n) -> p c n", n=IN_W)
    eye, flip = eye2[:, 0:P], eye2[:, P:2 * P]
    ln1T, ln2T = small[:, 0:16], small[:, 16:32]
    qkw = small[:, 32:160].rearrange("p (w d) -> p w d", d=HD)
    pscale = small[:, 160:168]
    wr = small[:, 168:488].rearrange("p (c n) -> p c n", n=20)
    rb = small[0:20, 488:489]
    relS = small[:, 489:553]
    relP = small[0:33, 553:569]
    SM = 569

    sq_tmp = X[:, 0:2048]
    state = X[0:DEC_B * BUF, 2048:3072]
    dT = X[:, 3072:3072 + 4 * TOK].rearrange("p (b c t) -> p b c t", b=2, t=TOK)
    KT = X[:, 0:1792].rearrange("p (b n) -> p b n", b=2)
    PTs = X[:, 1792:2368].rearrange("p (c n) -> p c n", n=64)
    SB = X[0:64, 2368:2368 + KEYS]
    OS = X[0:64, 3296:4320]
    PP = X[:, 4320:5088].rearrange("p (b n) -> p b n", b=2)
    PPT = X[:, 5088:5856].rearrange("p (b n) -> p b n", b=2)
    st_q, st_k, st_v = (stage[:, n, :].rearrange("p (c n) -> p c n", c=2) for n in range(3))
    qTz = [stage[:, 3, :], stage[:, 4, :]]
    kTp = stage[:, 5, :]
    T = ring[:, 4, :].rearrange("p (h n) -> p h n", h=H)
    EC = KEYS - NS + DEC_B * NS
    c_one = ring[0:33, 5, 0:384]
    c_hot = ring[:, 5, 384:384 + EC]
    c_mask = ring[0:64, 5, 384 + EC:384 + 2 * EC]
    c_pool = ring[:, 5, 0:1792]
    wpool = ring[:, 5, 1792:3840].rearrange("p (g c e) -> p g c e", g=4, c=2)
    route = Z[:, 2100:2100 + 649]
    Pm = X[:, 0:1152].rearrange("p (c k n) -> p c k n", c=3, k=3)
    R = X[:, 1152:1152 + 400]
    LG = X[0:20, 1600:1600 + TOK]
    HTG = [HT[:, n * 2048:(n + 1) * 2048].rearrange("p (c t) -> p c t", t=P) for n in range(2)]
    XG = [X[:, n * ROWG:(n + 1) * ROWG] for n in range(2)]
    HN = Z[:, 0:2048]
    SIL, HID = Z[:, 2048:2560], Z[:, 2560:3072]
    HIDT = Z[:, 3072:3584].rearrange("p (f t) -> p f t", t=P)

    g_scr = nc.dram_tensor("g_scr", (H, 384), F32).ap()
    x1_scr = nc.dram_tensor("x1_scr", (TOK, ROWG), F32).ap()

    landed = [sem(f"landed{s}") for s in range(SLOTS)]
    used = [sem(f"used{s}") for s in range(SLOTS)]
    x_in, const_in, state_in = sem("x_in"), sem("const_in"), sem("state_in")
    g_stored, x_again, route_in, x1_stored = sem("g_stored"), sem("x_again"), sem("route_in"), sem("x1_stored")
    stored, pstored = sem("stored"), sem("pstored")
    dve_step, act_step = sem("dve_step"), sem("act_step")
    squares, root_in, roots = sem("squares"), sem("root_in"), sem("roots")
    h_rows, h_turned, h_moved = sem("h_rows"), sem("h_turned"), sem("h_moved")
    bias_mm, bias_moved, g_ready = sem("bias_mm"), sem("bias_moved"), sem("g_ready")
    proj_done, z_moved = sem("proj_done"), sem("z_moved")
    normed = sem("normed")
    sT_done, sT_moved = sem("sT_done"), sem("sT_moved")
    d_done, d_moved, y_done, y_moved = sem("d_done"), sem("d_moved"), sem("y_done"), sem("y_moved")
    stage_ready = sem("stage_ready")
    pT, kt_turned, s_pair = sem("pT"), sem("kt_turned"), sem("s_pair")
    pS, pPT, pO, sPT, sO, sOT = (sem(n) for n in ("pS", "pPT", "pO", "sPT", "sO", "sOT"))
    qk_moved, ktn, ktf, p_exp, ppt_moved = (sem(n) for n in ("qk_moved", "ktn", "ktf", "p_exp", "ppt_moved"))
    s_exp, pts_n, pts_f, os_a, os_b, po_moved = (sem(n) for n in ("s_exp", "pts_n", "pts_f", "os_a", "os_b", "po_moved"))
    qbd_ready, p_negmax, p_norm, s_negmax, s_inv, diag = (
        sem(n) for n in ("qbd_ready", "p_negmax", "p_norm", "s_negmax", "s_inv", "diag"))
    wo_done, wo_moved, s_sum = sem("wo_done"), sem("wo_moved"), sem("s_sum")
    rl_done, rl_moved, lgT_done, expd = sem("rl_done"), sem("rl_moved"), sem("lgT_done"), sem("expd")
    exp_in, oh_ready, rank_done, pm_ready, idx_done, idx_ready, gates_ready = (
        sem(n) for n in ("exp_in", "oh_ready", "rank_done", "pm_ready", "idx_done", "idx_ready", "gates_ready"))
    idx_copied, pool_turn = sem("idx_copied"), sem("pool_turn")
    gathered = [sem(f"gathered{n}") for n in range(2)]
    scattered = [sem(f"scattered{n}") for n in range(2)]
    hn_ready, htg_turned, htg_moved = sem("hn_ready"), sem("htg_turned"), sem("htg_moved")
    gate_done, up_done, sil_ready, hid_ready = sem("gate_done"), sem("up_done"), sem("sil_ready"), sem("hid_ready")
    hidT_done, hidT_moved, down_done, out_rows = sem("hidT_done"), sem("hidT_moved"), sem("down_done"), sem("out_rows")

    w_in_t = a["w_in"][0].rearrange("(c p) n -> p c n", p=P)
    w_o_t = a["w_o"][0].rearrange("(c p) n -> p c n", p=P)
    xp_t = a["x_prompt"][0].rearrange("(c p) d -> p c d", p=P)
    xs_t = a["x_sample"].rearrange("b t d -> (b t) d")

    def near_rows(cache, b):
        return cache[0, b, PAST - NEAR:PAST].rearrange("(p j) h d -> p (j h d)", j=4)

    def far_rows(cache, b):
        return cache[0, b, 0:PAST - NEAR].rearrange("(p j) h d -> p j (h d)", j=16)[:, 0:4, :]

    def load_columns(sp, w_t, col, par):
        for half in range(2):
            s = 2 * par + half
            sp.dma_start(ring[:, s, :].rearrange("p (c n) -> p c n", n=TILE),
                         w_t[:, half * 8:half * 8 + 8, bass.ds(col, TILE)]).then_inc(landed[s], 16)

    block = ctx.enter_context(nc.Block())

    LOADS_P1, LOADS_AT, LOADS_WO = 4, 8, 2
    BASE_AT, BASE_WO = LOADS_P1, LOADS_P1 + LOADS_AT
    BASE_MOE = [BASE_WO + LOADS_WO] * 4 + [1, 2]

    @block.sync
    def _(sp):
        sp.dma_start(x_rows[:, 0:2, :], xp_t).then_inc(x_in, 16)
        sp.dma_start(x_rows[0:NS, 2, :], xs_t).then_inc(x_in, 16)
        sp.dma_start(ring[:, 5, 0:384 + 2 * EC], a["c_bias"]).then_inc(landed[5], 16)
        for par in range(2):
            load_columns(sp, w_in_t, par * TILE, par)
        with sp.Fori(1, 4) as i:
            for par in range(2):
                sp.wait_ge(used[2 * par], i)
                sp.wait_ge(proj_done, 2 * i + (par - 1))
                load_columns(sp, w_in_t, (2 * i + par) * TILE, par)
        sp.wait_ge(bias_moved, 4)
        sp.dma_start(ring[:, 5, 0:1792], a["c_pool"]).then_inc(landed[5], 16)
        sp.dma_start(ring[:, 5, 1792:3840].rearrange("p (g c e) -> p g c e", g=4, c=2),
                     a["w_pool"][0].rearrange("g (c p) e -> p g c e", p=P)).then_inc(state_in, 16)
        sp.wait_ge(h_turned, 12)
        sp.dma_start(state, a["state_pool"][0].rearrange("b r n -> (b r) n")).then_inc(state_in, 16)

        def cached(s, i):
            rows = a["cache_k" if s < 2 else "cache_v"][0, bass.ds(i, 1)]
            if s % 2 == 0:
                sp.dma_start(ring[:, s, :], rows[:, PAST - NEAR:PAST].rearrange("a (p j) h d -> p (a j h d)", j=4)
                             ).then_inc(landed[s], 16)
            else:
                sp.dma_start(ring[0:FAR, s, :].rearrange("p (j n) -> p j n", j=4),
                             rows[:, 0:PAST - NEAR].rearrange("a (p j) h d -> p (a j) (h d)", j=16)[:, 0:4, :]
                             ).then_inc(landed[s], 16)

        for s, freed, n in ((0, used[0], 4), (1, proj_done, 7), (2, used[2], 4), (3, proj_done, 8)):
            sp.wait_ge(freed, n)
            cached(s, 0)
        with sp.Fori(1, DEC_B) as i:
            for s, freed, n in ((0, kt_turned, 16 * i - 1), (1, kt_turned, 16 * i), (2, used[2], i + 4),
                                (3, used[3], i)):
                sp.wait_ge(h_turned, 12)
                sp.wait_ge(freed, n)
                cached(s, i)
        for par, freed in enumerate((((kt_turned, 128),), ((used[2], 12), (used[3], 8)))):
            for which, n in freed:
                sp.wait_ge(which, n)
            load_columns(sp, w_o_t, par * TILE, par)
        sp.wait_ge(sO, DEC_B)
        sp.wait_ge(stage_ready, 3 * PAIRS)
        sp.wait_ge(stored, 16 * 5)
        sp.wait_ge(pstored, 16 * 9)
        sp.dma_start(z[:, 0:2, 0:D], xp_t).then_inc(x_again, 16)
        sp.dma_start(z[0:NS, 2, 0:D], xs_t).then_inc(x_again, 16)
        sp.dma_start(route, a["c_route"]).then_inc(route_in, 16)
        for par in range(2):
            sp.wait_ge(used[2 * par], (5, 13)[par])
            sp.wait_ge(wo_done, par + 1)
            load_columns(sp, w_o_t, (2 + par) * TILE, par)
        sp.wait_ge(pS, 2 * PAIRS)
        sp.wait_ge(y_done, 8)
        sp.wait_ge(wo_done, 4)

        def experts(it, par8):
            for k in range(8):
                e = par8 * 8 + k
                wg, wu, wd = (a[n][0, bass.ds(e, 1)] for n in ("w_gate", "w_up", "w_down"))
                for s, w, half, freed, n in ((4, wg, 0, used[4], 1), (5, wg, 1, gate_done, 1),
                                             (0, wu, 0, used[0], 6), (1, wu, 1, up_done, 1)):
                    sp.wait_ge(freed, it * 8 + (n + k))
                    sp.dma_start(ring[:, s, :].rearrange("p (c n) -> p c n", n=TILE),
                                 w.rearrange("a (c p) n -> p (a c) n", p=P)[:, half * 8:half * 8 + 8, :]
                                 ).then_inc(landed[s], 16)
                for s, half, freed, n in ((2, 0, used[2], 14), (3, 1, down_done, 1)):
                    sp.wait_ge(freed, it * 8 + (n + k))
                    sp.dma_start(ring[:, s, :].rearrange("p (f n) -> p f n", n=D),
                                 wd.rearrange("a (f p) n -> p (a f) n", p=P)[:, half * 2:half * 2 + 2, :]
                                 ).then_inc(landed[s], 16)

        with sp.Fori(0, 2) as it:
            experts(it, it)
        sp.wait_ge(idx_ready, 1)
        most = sp.value_load(pidx[0:1, 24:25], min_val=0, max_val=TOK)
        with sp.If(most > P):
            with sp.Fori(1, PASSES) as c:
                with sp.Fori(0, 2) as j:
                    experts(c * 2 + j, j)

    @block.gpsimd
    def _(pool):
        pool.dma_start(o["pool_sample"][0, :, 0:BUF - DEC_T, :], a["state_pool"][0, :, DEC_T:BUF, :]).then_inc(pstored, 16)
        pool.wait_ge(normed, 4)
        for n, name in ((1, "k"), (2, "v")):
            if n == 2:
                pool.wait_ge(z_moved, 6 + 18)
            pool.dma_start(o[f"{name}_prompt"][0, 0].rearrange("(c p) h d -> p c (h d)", p=P),
                           z[:, 0:2, n * AW:(n + 1) * AW]).then_inc(stored, 16)
            pool.dma_start(o[f"{name}_sample"][0].rearrange("b t h d -> (b t) (h d)"),
                           z[0:NS, 2, n * AW:(n + 1) * AW]).then_inc(stored, 16)
        pool.wait_ge(z_moved, 6 + 24)
        pool.dma_start(o["pool_prompt"][0, 0], z[P - BUF:P, 1, 3 * AW:IN_W]).then_inc(stored, 16)
        for b in range(DEC_B):
            pool.dma_start(o["pool_sample"][0, b, BUF - DEC_T:BUF, :],
                           z[b * DEC_T:(b + 1) * DEC_T, 2, 3 * AW:IN_W]).then_inc(pstored, 16)
        with pool.Fori(0, PAIRS) as i:
            pool.wait_ge(pT, i + 1)
            for n, dst in ((0, st_q), (1, st_k), (2, st_v)):
                if n == 2:
                    pool.wait_ge(pO, i + 1)
                pool.tensor_copy(dst, z[:, 0:2, bass.ds(i * P + n * AW, P)]).then_inc(stage_ready, 1)

        def experts(it, col0):
            for n in range(2):
                col = col0 * 2 + n
                for kind in range(2):
                    pool.tensor_copy(pidx[:, 26 + 2 * n + kind:27 + 2 * n + kind],
                                     pidx[:, bass.ds(col + 12 * kind, 1)]).then_inc(idx_copied, 1)
                pool.wait_ge(idx_copied, it * 4 + (2 * n + 2))
                pool.sem_inc(pool_turn, 1)
                pool.indirect_dma_start(
                    out=XG[n], out_offset=None, in_=x1_scr,
                    in_offset=bass.IndirectOffsetOnAxis(ap=pidx[:, 26 + 2 * n:27 + 2 * n], axis=0),
                ).then_inc(gathered[n], 16)
            for n in range(2):
                pool.wait_ge(out_rows, it * 8 + (4 * n + 8))
                if n:
                    pool.wait_ge(scattered[0], it * 16 + 16)
                pool.sem_inc(pool_turn, 1)
                pool.indirect_dma_start(
                    out=o["y"], out_offset=bass.IndirectOffsetOnAxis(ap=pidx[:, 27 + 2 * n:28 + 2 * n], axis=0),
                    in_=XG[n][:, 0:D], in_offset=None).then_inc(scattered[n], 16)
            pool.wait_ge(scattered[1], it * 16 + 16)

        pool.wait_ge(stored, 16 * 5)
        pool.wait_ge(pstored, 16 * (1 + DEC_B))
        pool.wait_ge(idx_ready, 1)
        pool.wait_ge(x1_stored, 32)
        with pool.Fori(0, 2) as it:
            experts(it, it)
        most = pool.value_load(pidx[0:1, 24:25], min_val=0, max_val=TOK)
        with pool.If(most > P):
            with pool.Fori(1, PASSES) as c:
                with pool.Fori(0, 2) as j:
                    experts(c * 2 + j, c * 2 + j)

    @block.scalar
    def _(act):
        act.dma_start(eye2[:, :], a["c_eye"]).then_inc(const_in, 16)
        act.dma_start(small[:, 0:569], a["small"]).then_inc(const_in, 16)
        act.sem_inc(z_moved, 6)
        act.sem_inc(ppt_moved, 2)
        act.sem_inc(po_moved, 1)
        steps = Steps(act, act_step)

        def rms_roots(src, scratch, n):
            for k, (t0, m) in enumerate(CHUNKS):
                act.activation(scratch[0:m, k], src[0:m, k, 0:D], ACT.Square,
                               accum_out=stat[0:m, k:k + 1]).then_inc(squares, 1)
            act.wait_ge(root_in, n)
            act.activation(stat[:, 4:7], stat[:, 4:7], ACT.Sqrt).then_inc(roots, 1)

        act.wait_ge(root_in, 1)
        act.wait_ge(x_in, 32)
        rms_roots(x_rows, Z[:, 0:3 * D].rearrange("p (c d) -> p c d", d=D), 2)
        act.wait_ge(bias_moved, 1)
        act.wait_ge(g_ready, 1)
        act.dma_start(g_scr, gS[:, :]).then_inc(g_stored, 16)
        act.wait_ge(g_stored, 16)
        act.dma_start(T, bass.AP(g_scr.tensor, 0, [[1, P], [384, H], [1, 256]])).then_inc(landed[4], 16)

        def z_out(i):
            for par in range(2):
                act.wait_ge(proj_done, 2 * i + (par + 1))
                for k, (t0, m) in enumerate(CHUNKS):
                    act.activation(z[0:m, k, bass.ds(i * 2 * TILE + par * TILE, TILE)],
                                   PS[0:m, par * 3 + k, :], ACT.Copy).then_inc(z_moved, 1)

        act.wait_ge(roots, 1)
        with act.Fori(0, 2) as i:
            z_out(i)
        for n in range(4):
            act.wait_ge(root_in, 3 + n)
            act.activation(stat[:, 16:48] if n % 2 == 0 else stat[0:NS, 48:64],
                           stat[:, 16:48] if n % 2 == 0 else stat[0:NS, 48:64], ACT.Sqrt).then_inc(roots, 1)
        with act.Fori(2, 4) as i:
            z_out(i)
        act.wait_ge(sT_done, 1)
        act.activation(qkTs[:, 0], PS[:, 6, 0:256].rearrange("p (a t) -> p a t", t=NS), ACT.Copy,
                       scale=SCALE).then_inc(sT_moved, 1)
        act.activation(qkTs[:, 1], PS[:, 6, 256:512].rearrange("p (a t) -> p a t", t=NS),
                       ACT.Copy).then_inc(sT_moved, 1)
        for g in range(4):
            for eh in range(2):
                act.wait_ge(y_done, 2 * g + eh + 1)
                act.activation(hT[:, 8 + 2 * g + eh, :], PS[:, 4 + eh, 0:TOK], ACT.Identity,
                               scale=pscale[:, 2 * g + eh:2 * g + eh + 1]).then_inc(y_moved, 1)
        act.wait_ge(diag, 4)
        with act.Fori(0, PAIRS) as i:
            act.wait_ge(pT, i + 2)
            for par in range(2):
                r = slice(64 * par, 64 * par + 64)
                act.activation(qTz[par][r], PS[r, 6, 0:256], ACT.Copy, scale=SCALE).then_inc(qk_moved, 1)
            act.activation(kTp, PS[:, 6, 256:512], ACT.Copy).then_inc(qk_moved, 1)

            def keys_out(pair):
                act.wait_ge(kt_turned, i * 16 + (2 * pair + 1))
                act.wait_ge(s_pair, i * 8 + (pair + 1))
                act.activation(KT[:, pair % 2, 0:NEAR], PS[:, 2 * (pair % 2), :], ACT.Copy).then_inc(ktn, 1)

            def prompt_exp(par):
                act.wait_ge(p_negmax, i * 2 + (par + 1))
                for q, (c0, c1) in enumerate(((0, 128), (128, 384))):
                    act.activation(PP[:, par, c0:c1], PS[:, 7 - par, c0:c1], ACT.Exp,
                                   bias=stat[:, 68 + 4 * par + q:69 + 4 * par + q],
                                   accum_out=stat[:, 76 + 4 * par + q:77 + 4 * par + q]).then_inc(p_exp, 1)

            def prompt_turned(par):
                act.wait_ge(pPT, i * 2 + (par + 1))
                act.activation(PPT[:, par, :], PS[:, par, 0:384], ACT.Copy).then_inc(ppt_moved, 1)

            for pair in range(6):
                keys_out(pair)
            prompt_exp(0)
            keys_out(6)
            prompt_exp(1)
            keys_out(7)
            prompt_turned(0)
            prompt_turned(1)
            act.wait_ge(s_negmax, i + 1)
            act.activation(SB, SB, ACT.Exp, bias=stat[0:64, 65:66],
                           accum_out=stat[0:64, 66:67]).then_inc(s_exp, 1)
            act.wait_ge(pO, i + 2)
            act.activation(hT[:, bass.ds(i, 1), 0:SEQ].rearrange("p a t -> p (a t)"), PS[:, 2, 0:SEQ],
                           ACT.Copy).then_inc(po_moved, 1)
            act.wait_ge(sPT, i + 1)
            act.activation(PTs[:, 0:4, :], PS[:, 4, 0:256].rearrange("p (c n) -> p c n", n=64),
                           ACT.Copy).then_inc(pts_n, 1)
            act.activation(PTs[0:FAR, 4:8, :], PS[0:FAR, 4, 256:512].rearrange("p (c n) -> p c n", n=64),
                           ACT.Copy).then_inc(pts_n, 1)
            act.wait_ge(sO, i + 1)
            act.wait_ge(s_inv, i + 1)
            act.activation(OS[:, 0:TILE], PS[0:64, 6, :], ACT.Identity,
                           scale=stat[0:64, 67:68]).then_inc(os_a, 1)
        act.wait_ge(wo_moved, 6 + 12)
        act.wait_ge(root_in, 7)
        rms_roots(z, x_rows, 8)
        act.wait_ge(rl_done, 1)
        act.activation(LG, PS[0:20, 5, 0:TOK], ACT.Identity, bias=rb).then_inc(rl_moved, 1)
        for n in range(2):
            act.wait_ge(exp_in, n + 1)
            v = R[:, 60:72] if n == 0 else R[:, 132:135]
            act.activation(v, v, ACT.Exp).then_inc(expd, 1)
        act.wait_ge(gates_ready, 1)
        act.dma_start(x1_scr[0:SEQ].rearrange("(c p) d -> p c d", p=P), z[:, 0:2, 0:ROWG]).then_inc(x1_stored, 16)
        act.dma_start(x1_scr[SEQ:TOK], z[0:NS, 2, 0:ROWG]).then_inc(x1_stored, 16)

        act.wait_ge(x1_stored, 32)

        def experts(it):
            def sil(k):
                act.wait_ge(gate_done, it * 8 + (k + 2))
                act.activation(SIL, PS[:, 0, :], ACT.Silu).then_inc(sil_ready, 1)

            def turned(k):
                act.wait_ge(hidT_done, it * 8 + (k + 1))
                act.activation(HIDT, PS[:, 2, :].rearrange("p (f t) -> p f t", t=P), ACT.Copy).then_inc(hidT_moved, 1)

            for k in range(8):
                if k:
                    act.wait_ge(hid_ready, it * 8 + k)
                sil(k)
                if k:
                    turned(k - 1)
            turned(7)

        with act.Fori(0, 2) as it:
            experts(it)
        act.wait_ge(idx_ready, 1)
        most = act.value_load(pidx[0:1, 24:25], min_val=0, max_val=TOK)
        with act.If(most > P):
            with act.Fori(1, PASSES) as c:
                with act.Fori(0, 2) as j:
                    experts(c * 2 + j)

    @block.tensor
    def _(pe):
        def mm(out, lhsT, rhs, start, stop):
            return pe.matmul(out, lhsT, rhs, start=start, stop=stop, skip_group_check=True)

        def turn_rows(rows, moved0):
            for n in range(12):
                k, g = n // 4, n % 4
                m = CHUNKS[k][1]
                if n >= 2:
                    pe.wait_ge(h_moved, moved0 + n - 1)
                for q in range(4):
                    c = 4 * g + q
                    ins = pe.transpose(PS[:, 6 + n % 2, q * m:(q + 1) * m], rows[0:m, k, c * P:(c + 1) * P],
                                       eye[0:m, 0:m])
                ins.then_inc(h_turned, 1)

        pe.sem_inc(pT, 1)
        pe.sem_inc(pO, 1)
        pe.sem_inc(s_pair, 2)
        for s in (used[4], gate_done, up_done, down_done):
            pe.sem_inc(s, 1)
        pe.wait_ge(const_in, 32)
        pe.wait_ge(landed[5], 16)
        mm(PS[0:H, 0, 0:384], relP, c_one, True, True).then_inc(bias_mm, 1)
        for n, (c0, c1) in enumerate(((0, 512), (512, 896), (896, EC))):
            mm(PS[0:64, 1 + n, 0:c1 - c0], relS, c_hot[:, c0:c1], True, True).then_inc(bias_mm, 1)
        pe.wait_ge(h_rows, 3)
        turn_rows(x_rows, 0)
        pe.wait_ge(h_moved, 12)
        pe.wait_ge(bias_moved, 4)

        def columns(i, done, moved, base):
            for par in range(2):
                pe.wait_ge(moved, 6 * i + (3 * par + 3))
                for half in range(2):
                    s = 2 * par + half
                    pe.wait_ge(landed[s], 16 * i + 16 * (base + 1))
                    w = ring[:, s, :].rearrange("p (c n) -> p c n", n=TILE)
                    for c in range(8):
                        cc = half * 8 + c
                        for k, (t0, m) in enumerate(CHUNKS):
                            ins = mm(PS[0:m, par * 3 + k, :], hT[:, cc, t0:t0 + m], w[:, c, :],
                                     cc == 0, cc == DC - 1)
                            if k == 2 and c == 7 and half == 0:
                                ins.then_inc(used[s], 1)
                ins.then_inc(done, 1)

        with pe.Fori(0, 4) as i:
            columns(i, proj_done, z_moved, 0)
        pe.wait_ge(normed, 4)
        for w in range(2):
            for pair in range(PAIRS):
                ins = pe.transpose(PS[:, 6, w * 256 + pair * NS:w * 256 + (pair + 1) * NS],
                                   z[0:NS, 2, w * AW + pair * P:w * AW + (pair + 1) * P], eye[0:NS, 0:NS])
        ins.then_inc(sT_done, 1)
        pe.wait_ge(z_moved, 6 + 24)
        pe.wait_ge(landed[5], 32)
        pe.wait_ge(state_in, 32)

        def windows(g):
            for ch in range(2):
                if g >= 2:
                    pe.wait_ge(d_moved, 2 * (g - 2) + ch + 1)
                u0 = 3 * AW + g * GW + ch * P
                bank = PS[:, 2 * (g % 2) + ch, :]
                mm(bank[:, 0:256], z[:, 0, u0:u0 + P], c_pool[:, g * 256:(g + 1) * 256], True, False)
                mm(bank[:, 128:256], z[:, 1, u0:u0 + P], c_pool[:, 1024 + g * 128:1152 + g * 128], False, True)
                mm(bank[:, 256:288], state[:, g * GW + ch * P:g * GW + (ch + 1) * P],
                   c_pool[0:DEC_B * BUF, 1536 + g * 32:1568 + g * 32], False, False)
                mm(bank[:, 256:288], z[0:NS, 2, u0:u0 + P],
                   c_pool[0:NS, 1664 + g * 32:1696 + g * 32], False, True).then_inc(d_done, 1)

        def group_map(g):
            pe.wait_ge(d_moved, 2 * g + 2)
            for eh in range(2):
                if g:
                    pe.wait_ge(y_moved, 2 * (g - 1) + eh + 1)
                for ch in range(2):
                    ins = mm(PS[:, 4 + eh, 0:TOK], wpool[:, g, ch, eh * P:(eh + 1) * P], dT[:, g % 2, ch, :],
                             ch == 0, ch == 1)
                ins.then_inc(y_done, 1)

        windows(0)
        for g in range(4):
            if g < 3:
                windows(g + 1)
            group_map(g)
        pe.wait_ge(landed[4], 16)
        pe.wait_ge(y_moved, 8)
        pe.wait_ge(sT_moved, 2)
        pe.wait_ge(d_moved, 8)
        with pe.Fori(0, PAIRS) as i:
            pe.wait_ge(stage_ready, i * 3 + 2)
            for w, src in enumerate((st_q, st_k)):
                for c in range(2):
                    ins = pe.transpose(PS[:, 6, (2 * w + c) * P:(2 * w + c + 1) * P], src[:, c, :], eye)
            ins.then_inc(pT, 1)

            def turn_keys(pair):
                b = 2 * (pair % 2)
                if pair == 0:
                    pe.wait_ge(landed[0], i * 16 + 16 * (BASE_AT + 1))
                    pe.wait_ge(ppt_moved, i * 2 + 2)
                elif pair == 1:
                    pe.wait_ge(po_moved, i + 1)
                    pe.wait_ge(diag, i * 2 + 4)
                else:
                    pe.wait_ge(ktn, i * 8 + (pair - 1))
                    pe.wait_ge(ktf, i * 8 + (pair - 1))
                kn = ring[:, 0, :].rearrange("p (j n) -> p j n", j=4)
                kf = ring[:, 1, :].rearrange("p (j n) -> p j n", j=4)
                for j in range(4):
                    ins = pe.transpose(PS[:, b, j * P:(j + 1) * P], kn[:, j, pair * P:(pair + 1) * P], eye)
                ins.then_inc(kt_turned, 1)
                if pair == 0:
                    pe.wait_ge(landed[1], i * 16 + 16 * (BASE_AT + 1))
                for j in range(4):
                    ins = pe.transpose(PS[:, b + 1, j * FAR:(j + 1) * FAR], kf[0:FAR, j, pair * P:(pair + 1) * P],
                                       eye[0:FAR, 0:FAR])
                ins.then_inc(kt_turned, 1)

            def sample_scores(pair):
                q = Qbd[:, pair * 64:pair * 64 + 64]
                first, last = pair == 0, pair == PAIRS - 1
                if first:
                    pe.wait_ge(qbd_ready, i * 2 + 2)
                pe.wait_ge(ktn, i * 8 + (pair + 1))
                mm(PS[0:64, 4, :], q, KT[:, pair % 2, 0:NEAR], first, last)
                pe.wait_ge(ktf, i * 8 + (pair + 1))
                mm(PS[0:64, 5, 0:4 * FAR], q, KT[:, pair % 2, NEAR:NEAR + 4 * FAR], first, last)
                mm(PS[0:64, 5, 4 * FAR:4 * FAR + NS], q, qkTs[:, 1, pair, :], False, last).then_inc(s_pair, 1)

            def prompt_scores(par):
                if par == 0:
                    pe.wait_ge(qk_moved, i * 3 + 3)
                bank = PS[:, 7 - par, :]
                bias = T[:, bass.ds(2 * i + par, 1), :].rearrange("p a n -> p (a n)")
                bias_late = T[:, bass.ds(2 * i + par, 1), 128:256].rearrange("p a n -> p (a n)")
                mm(bank[:, 0:128], qTz[par][:, 0:128], kTp[:, 0:128], True, False)
                mm(bank[:, 0:128], flip, bias_late, False, True)
                mm(bank[:, 128:384], qTz[par][:, 128:256], kTp, True, False)
                mm(bank[:, 128:384], flip, bias, False, True).then_inc(pS, 1)

            for pair in range(PAIRS + 1):
                if pair < PAIRS:
                    turn_keys(pair)
                if pair:
                    sample_scores(pair - 1)
                if pair in (4, 5):
                    prompt_scores(pair - 4)
            for par in range(2):
                pe.wait_ge(p_norm, i * 4 + (2 * par + 2))
                for n in range(3):
                    ins = pe.transpose(PS[:, par, n * P:(n + 1) * P], PP[:, par, n * P:(n + 1) * P], eye)
                ins.then_inc(pPT, 1)
            pe.wait_ge(stage_ready, i * 3 + 3)
            for par in range(2):
                pe.wait_ge(ppt_moved, i * 2 + (par + 3))
                out = PS[64 * par:64 * par + 64, 2, :]
                mm(out[:, 0:256], st_v[:, 0, 64 * par:64 * par + 64], PPT[:, par, 0:256], True, False)
                ins = mm(out[:, 128:256], st_v[:, 1, 64 * par:64 * par + 64], PPT[:, par, 256:384], False, True)
            ins.then_inc(pO, 1)
            pe.wait_ge(const_in, 32)
            pe.wait_ge(s_exp, i + 1)
            for j in range(4):
                pe.transpose(PS[:, 4, j * 64:(j + 1) * 64], SB[:, j * P:(j + 1) * P], eye[0:64, 0:64])
            for j in range(4):
                c0 = NEAR + j * FAR
                pe.transpose(PS[0:FAR, 4, 256 + j * 64:320 + j * 64], SB[:, c0:c0 + FAR], eye[0:64, 0:64])
            pe.transpose(PS[0:NS, 5, 0:64], SB[:, KEYS - NS:KEYS], eye[0:64, 0:64]).then_inc(sPT, 1)
            pe.wait_ge(p_exp, i * 4 + 4)
            pe.wait_ge(pts_n, i * 2 + 2)
            pe.wait_ge(landed[2], i * 16 + 16 * (BASE_AT + 1))
            vn = ring[:, 2, :].rearrange("p (j n) -> p j n", j=4)
            vf = ring[:, 3, :].rearrange("p (j n) -> p j n", j=4)
            for vh in range(2):
                for j in range(4):
                    ins = mm(PS[0:64, 6 + vh, :], PTs[:, j, :], vn[:, j, vh * TILE:(vh + 1) * TILE], j == 0, False)
            ins.then_inc(used[2], 1)
            pe.wait_ge(pts_f, i + 1)
            pe.wait_ge(landed[3], i * 16 + 16 * (BASE_AT + 1))
            for vh in range(2):
                for j in range(4):
                    ins = mm(PS[0:64, 6 + vh, :], PTs[0:FAR, 4 + j, :], vf[0:FAR, j, vh * TILE:(vh + 1) * TILE],
                             False, False)
            ins.then_inc(used[3], 1)
            for vh in range(2):
                ins = mm(PS[0:64, 6 + vh, :], PTs[0:NS, 8, :], z[0:NS, 2, 2 * AW + vh * TILE:2 * AW + (vh + 1) * TILE],
                         False, True)
            ins.then_inc(sO, 1)
            pe.wait_ge(const_in, 32)
            pe.wait_ge(os_a, i + 1)
            pe.wait_ge(os_b, i + 1)
            for pair in range(PAIRS):
                ins = pe.transpose(PS[:, 3, pair * 64:(pair + 1) * 64], OS[:, pair * P:(pair + 1) * P], eye[0:64, 0:64])
            ins.then_inc(sOT, 1)
        pe.wait_ge(po_moved, PAIRS + 1)
        pe.wait_ge(diag, 2 + 2 + 2 * DEC_B)
        with pe.Fori(0, 2) as i:
            columns(i, wo_done, wo_moved, BASE_WO)
        pe.wait_ge(h_rows, 6)
        turn_rows(x_rows, 12)
        pe.wait_ge(h_moved, 24)
        for c in range(DC):
            ins = mm(PS[0:20, 5, 0:TOK], wr[:, c, :], hT[:, c, :], c == 0, c == DC - 1)
        ins.then_inc(rl_done, 1)
        pe.wait_ge(rl_moved, 1)
        for k, (t0, m) in enumerate(CHUNKS):
            ins = pe.transpose(PS[0:m, 6, k * 20:(k + 1) * 20], LG[:, t0:t0 + m], eye[0:20, 0:20])
        ins.then_inc(lgT_done, 1)
        tri, ones = route[:, 0:P], route[:, P:2 * P]
        oh = [R[:, 72 + 4 * k:76 + 4 * k] for k in range(3)]
        pe.wait_ge(oh_ready, 1)
        for n, parts in enumerate((((tri, 0),), ((ones, 0), (tri, 1)), ((ones, 0), (ones, 1), (tri, 2)),
                                   ((ones, 0), (ones, 1), (ones, 2)))):
            for q, (m, k) in enumerate(parts):
                ins = mm(PS[:, 7, 4 * n:4 * n + 4], m, oh[k], q == 0, q == len(parts) - 1)
        ins.then_inc(rank_done, 1)
        pe.wait_ge(pm_ready, 9)
        for c in range(PASSES):
            for k in range(3):
                ins = mm(PS[:, 6, 64 + 8 * c:72 + 8 * c], Pm[:, c, k, :], R[:, 160 + 8 * k:168 + 8 * k], k == 0, k == 2)
        ins.then_inc(idx_done, 1)

        def experts(it):
            def turn_part(n, r):
                if r == 0:
                    pe.wait_ge(hn_ready, it * 2 + (n + 1))
                pe.wait_ge(htg_moved, it * 8 + (4 * n + r + 1))
                for q in range(4):
                    c = 4 * r + q
                    ins = pe.transpose(PS[:, 7, q * P:(q + 1) * P], HN[:, c * P:(c + 1) * P], eye)
                ins.then_inc(htg_turned, 1)

            def up(k, bank, slot0, done):
                for half in range(2):
                    s = slot0 + half
                    pe.wait_ge(landed[s], it * 128 + 16 * (BASE_MOE[s] + k + 1))
                    w = ring[:, s, :].rearrange("p (c n) -> p c n", n=TILE)
                    for c in range(8):
                        cc = half * 8 + c
                        ins = mm(PS[:, bank, :], HTG[k // 4][:, cc, :], w[:, c, :], cc == 0, cc == DC - 1)
                    if half == 0:
                        ins.then_inc(used[s], 1)
                ins.then_inc(done, 1)

            def gate(k):
                if k:
                    pe.wait_ge(sil_ready, it * 8 + k)
                up(k, 0, 4, gate_done)

            def raise_(k):
                if k:
                    pe.wait_ge(hid_ready, it * 8 + k)
                up(k, 1, 0, up_done)

            def turn_hidden(k):
                pe.wait_ge(hid_ready, it * 8 + (k + 1))
                for f in range(4):
                    ins = pe.transpose(PS[:, 2, f * P:(f + 1) * P], HID[:, f * P:(f + 1) * P], eye)
                ins.then_inc(hidT_done, 1)

            def down(k):
                pe.wait_ge(hidT_moved, it * 8 + (k + 1))
                if k % 4 == 0:
                    pe.wait_ge(out_rows, it * 8 + (k + 4))
                for half in range(2):
                    s = 2 + half
                    pe.wait_ge(landed[s], it * 128 + 16 * (BASE_MOE[s] + k + 1))
                    w = ring[:, s, :].rearrange("p (f n) -> p f n", n=D)
                    for f in range(2):
                        ff = half * 2 + f
                        for q in range(4):
                            ins = mm(PS[:, 3 + q, :], HIDT[:, ff, :], w[:, f, q * TILE:(q + 1) * TILE],
                                     k % 4 == 0 and ff == 0, k % 4 == 3 and ff == 3)
                    if half == 0:
                        ins.then_inc(used[s], 1)
                ins.then_inc(down_done, 1)

            for r in range(4):
                turn_part(0, r)
            pe.wait_ge(htg_moved, it * 8 + 5)
            for k in range(8):
                if k == 4:
                    pe.wait_ge(htg_moved, it * 8 + 9)
                gate(k)
                if k:
                    turn_hidden(k - 1)
                if k == 3:
                    turn_part(1, 2)
                raise_(k)
                if k:
                    down(k - 1)
                if 1 <= k <= 3:
                    turn_part(1, (0, 1, 3)[k - 1])
            turn_hidden(7)
            down(7)

        pe.wait_ge(idx_ready, 1)
        with pe.Fori(0, 2) as it:
            experts(it)
        most = pe.value_load(pidx[0:1, 24:25], min_val=0, max_val=TOK)
        with pe.If(most > P):
            with pe.Fori(1, PASSES) as c:
                with pe.Fori(0, 2) as j:
                    experts(c * 2 + j)

    @block.vector
    def _(dve):
        steps = Steps(dve, dve_step)
        did, settle = steps.did, steps.settle
        dve.sem_inc(diag, 2)
        dve.sem_inc(wo_moved, 6)
        dve.memset(stat[:, 0:3], 1.0).then_inc(root_in, 1)

        def rms_rows(src, dst, n):
            dve.wait_ge(squares, 3 * n)
            dve.tensor_scalar(stat[:, 4:7], stat[:, 0:3], 1.0 / D, EPS, ALU.mult, ALU.add).then_inc(root_in, 1)
            dve.wait_ge(roots, 1 if n == 1 else 6)
            did(dve.reciprocal(stat[:, 8:11], stat[:, 4:7]))
            settle()
            for k, (t0, m) in enumerate(CHUNKS):
                dve.tensor_scalar(dst[0:m, k, 0:D], src[0:m, k, 0:D], stat[0:m, 8 + k:9 + k], None,
                                  ALU.mult).then_inc(h_rows, 1)

        def columns_out(gain, turned0):
            for n in range(12):
                k, g = n // 4, n % 4
                t0, m = CHUNKS[k]
                dve.wait_ge(h_turned, turned0 + n + 1)
                dve.tensor_tensor(hT[:, 4 * g:4 * g + 4, t0:t0 + m],
                                  PS[:, 6 + n % 2, 0:4 * m].rearrange("p (c t) -> p c t", c=4),
                                  gain[:, 4 * g:4 * g + 4].unsqueeze(2).to_broadcast([P, 4, m]),
                                  ALU.mult).then_inc(h_moved, 1)

        rms_rows(x_rows, x_rows, 1)
        dve.wait_ge(bias_mm, 4)
        dve.tensor_copy(gS[:, :], PS[0:H, 0, 0:384]).then_inc(g_ready, 1)
        dve.wait_ge(g_ready, 1)
        for n, (c0, c1) in enumerate(((0, 512), (512, 896), (896, EC))):
            dve.tensor_tensor(E[:, c0:c1], PS[0:64, 1 + n, 0:c1 - c0], c_mask[:, c0:c1], ALU.add).then_inc(bias_moved, 1)
        dve.memset(Qbd[:, :], 0.0).then_inc(bias_moved, 1)
        columns_out(ln1T, 0)
        for w in range(2):
            dve.wait_ge(z_moved, 12 + 6 * w)
            for part, (m, k0, k1, s0) in enumerate(((P, 0, 2, 16), (NS, 2, 3, 48))):
                nk = k1 - k0
                v = z[0:m, k0:k1, w * AW:(w + 1) * AW]
                tmp = sq_tmp[0:m, 0:nk * AW]
                v4 = v.rearrange("p c (h d) -> p c h d", d=HD)
                sums = stat[0:m, s0:s0 + nk * H]
                did(dve.tensor_tensor(tmp.rearrange("p (c n) -> p c n", n=AW), v, v, ALU.mult))
                settle()
                did(dve.tensor_reduce(sums, tmp.rearrange("p (s d) -> p s d", d=HD), AX.X, ALU.add))
                settle()
                dve.tensor_scalar(sums, sums, 1.0 / HD, EPS, ALU.mult, ALU.add).then_inc(root_in, 1)
                dve.wait_ge(roots, 2 + 2 * w + part)
                did(dve.reciprocal(sums, sums))
                settle()
                did(dve.tensor_tensor(v4, v4, sums.rearrange("p (c h) -> p c h", h=H).unsqueeze(3).to_broadcast(
                    [m, nk, H, HD]), ALU.mult))
                settle()
                dve.tensor_tensor(v4, v4, qkw[0:m, w, :].unsqueeze(1).unsqueeze(1).to_broadcast([m, nk, H, HD]),
                                  ALU.mult).then_inc(normed, 1)
        for g in range(4):
            for ch in range(2):
                dve.wait_ge(d_done, 2 * g + ch + 1)
                if g >= 2:
                    dve.wait_ge(y_done, 2 * (g - 1))
                dve.tensor_copy(dT[:, g % 2, ch, :], PS[:, 2 * (g % 2) + ch, 0:TOK]).then_inc(d_moved, 1)
        for par in range(2):
            other = slice(64 - 64 * par, 128 - 64 * par)
            dve.memset(qTz[par][other], 0.0).then_inc(diag, 1)
        dve.wait_ge(y_done, 8)
        dve.wait_ge(sT_moved, 2)
        with dve.Fori(0, PAIRS) as i:
            steps.begin(i, 7)
            dve.wait_ge(s_pair, i * 8 + 2)
            for par in range(2):
                r = slice(64 * par, 64 * par + 64)
                dve.tensor_copy(Qbd[r, :].rearrange("p (a n) -> p a n", n=65)[:, :, 8 * par:8 * par + 49:16],
                                qkTs[r, 0, :, bass.ds(i * 4, 4)]).then_inc(qbd_ready, 1)

            def keys_out(pair):
                dve.wait_ge(kt_turned, i * 16 + (2 * pair + 2))
                dve.wait_ge(s_pair, i * 8 + (pair + 1))
                dve.tensor_copy(KT[:, pair % 2, NEAR:NEAR + 4 * FAR],
                                PS[:, 2 * (pair % 2) + 1, 0:4 * FAR]).then_inc(ktf, 1)

            def prompt_max(par):
                dve.wait_ge(pS, i * 2 + (par + 1))
                for q, (c0, c1) in enumerate(((0, 128), (128, 384))):
                    did(dve.tensor_reduce(stat[:, 84 + 2 * par + q:85 + 2 * par + q], PS[:, 7 - par, c0:c1],
                                          AX.X, ALU.max))
                settle()
                dve.tensor_scalar(stat[:, 68 + 4 * par:70 + 4 * par], stat[:, 84 + 2 * par:86 + 2 * par], -1.0, None,
                                  ALU.mult).then_inc(p_negmax, 1)

            def prompt_norm(par):
                dve.wait_ge(p_exp, i * 4 + (2 * par + 2))
                did(dve.reciprocal(stat[:, 88 + 2 * par:90 + 2 * par], stat[:, 76 + 4 * par:78 + 4 * par]))
                settle()
                for q, (c0, c1) in enumerate(((0, 128), (128, 384))):
                    dve.tensor_scalar(PP[:, par, c0:c1], PP[:, par, c0:c1], stat[:, 88 + 2 * par + q:89 + 2 * par + q],
                                      None, ALU.mult).then_inc(p_norm, 1)

            for pair in range(5):
                keys_out(pair)
            prompt_max(0)
            keys_out(5)
            prompt_max(1)
            keys_out(6)
            prompt_norm(0)
            keys_out(7)
            prompt_norm(1)
            dve.wait_ge(s_pair, i * 8 + 10)
            dve.tensor_tensor(SB[:, 0:NEAR], PS[0:64, 4, :], E[:, 0:NEAR], ALU.add).then_inc(s_sum, 1)
            dve.tensor_tensor(SB[:, NEAR:KEYS - NS], PS[0:64, 5, 0:4 * FAR], E[:, NEAR:KEYS - NS],
                              ALU.add).then_inc(s_sum, 1)
            dve.tensor_tensor(SB[:, KEYS - NS:KEYS], PS[0:64, 5, 4 * FAR:4 * FAR + NS],
                              E[:, bass.ds(i * NS + (KEYS - NS), NS)], ALU.add).then_inc(s_sum, 1)
            dve.wait_ge(s_sum, i * 3 + 3)
            did(dve.tensor_reduce(stat[0:64, 64:65], SB, AX.X, ALU.max))
            settle()
            dve.tensor_scalar(stat[0:64, 65:66], stat[0:64, 64:65], -1.0, None, ALU.mult).then_inc(s_negmax, 1)
            dve.wait_ge(s_exp, i + 1)
            dve.reciprocal(stat[0:64, 67:68], stat[0:64, 66:67]).then_inc(s_inv, 1)
            dve.wait_ge(sPT, i + 1)
            dve.tensor_copy(PTs[0:NS, 8, :], PS[0:NS, 5, 0:64]).then_inc(pts_f, 1)
            dve.wait_ge(sO, i + 1)
            dve.wait_ge(s_inv, i + 1)
            dve.tensor_scalar(OS[:, TILE:2 * TILE], PS[0:64, 7, :], stat[0:64, 67:68], None, ALU.mult).then_inc(os_b, 1)
            dve.wait_ge(sOT, i + 1)
            for par in range(2):
                r = slice(64 * par, 64 * par + 64)
                blocks = PS[r, 3:5, :].rearrange("p a n -> p (a n)")[:, 0:520].rearrange(
                    "p (a n) -> p a n", n=65)[:, :, 8 * par:8 * par + 49:16]
                dve.tensor_copy(hT[r, 0:PAIRS, bass.ds(i * 4 + SEQ, 4)], blocks).then_inc(diag, 1)
        steps.end(PAIRS)
        dve.wait_ge(x_again, 32)

        with dve.Fori(0, 2) as i:
            for par in range(2):
                dve.wait_ge(wo_done, 2 * i + (par + 1))
                for k, (t0, m) in enumerate(CHUNKS):
                    xt = z[0:m, k, bass.ds(i * 2 * TILE + par * TILE, TILE)]
                    dve.tensor_tensor(xt, PS[0:m, par * 3 + k, :], xt, ALU.add).then_inc(wo_moved, 1)
        dve.memset(stat[:, 0:3], 1.0).then_inc(root_in, 1)
        rms_rows(z, x_rows, 2)
        columns_out(ln2T, 12)
        dve.wait_ge(h_turned, 24)
        did(dve.memset(R, 0.0))
        settle()
        dve.wait_ge(lgT_done, 1)
        dve.wait_ge(route_in, 16)

        def step(ins):
            did(ins)
            settle()

        def col(c, n=1):
            return R[:, c:c + 3 * n].rearrange("p (k n) -> p k n", n=n)

        L = col(0, 20)
        for k, (t0, m) in enumerate(CHUNKS):
            step(dve.tensor_copy(L[0:m, k, :], PS[0:m, 6, 20 * k:20 * k + 20]))
        lg, le = L[:, :, 0:4], L[:, :, 4:20]
        expg, oh, leg, top, work, m1, m2 = col(60, 4), col(72, 4), col(84, 4), col(96, 4), col(108, 4), col(120), col(123)
        free, tmp3, ge, gate4 = col(126), col(129), col(132), col(136, 4)
        valid = route[:, 5 * P + 3:5 * P + 6].unsqueeze(2)
        tokens = route[:, 5 * P:5 * P + 3].unsqueeze(2)

        def first_of(dst, src, best):
            step(dve.tensor_tensor(dst, src, best.to_broadcast([P, 3, 4]), ALU.is_equal))
            step(dve.memset(free, 1.0))
            for g in range(4):
                d = dst[:, :, g:g + 1]
                step(dve.tensor_tensor(d, d, free, ALU.mult))
                step(dve.tensor_tensor(free, free, d, ALU.subtract))

        step(dve.tensor_reduce(m1, lg, AX.X, ALU.max))
        dve.tensor_tensor(expg, lg, m1.to_broadcast([P, 3, 4]), ALU.subtract).then_inc(exp_in, 1)
        first_of(oh, lg, m1)
        dve.tensor_tensor(oh, oh, valid.to_broadcast([P, 3, 4]), ALU.mult).then_inc(oh_ready, 1)
        dve.wait_ge(oh_ready, 1)
        step(dve.tensor_tensor(leg, le[:, :, 0:4], oh[:, :, 0:1].to_broadcast([P, 3, 4]), ALU.mult))
        for g in range(1, 4):
            step(dve.tensor_tensor(work, le[:, :, 4 * g:4 * g + 4], oh[:, :, g:g + 1].to_broadcast([P, 3, 4]), ALU.mult))
            step(dve.tensor_tensor(leg, leg, work, ALU.add))
        step(dve.tensor_reduce(m1, leg, AX.X, ALU.max))
        first_of(top, leg, m1)
        step(dve.tensor_scalar(work, top, NEG, None, ALU.mult))
        step(dve.tensor_tensor(leg, leg, work, ALU.add))
        step(dve.tensor_reduce(m2, leg, AX.X, ALU.max))
        first_of(work, leg, m2)
        dve.tensor_tensor(ge, m2, m1, ALU.subtract).then_inc(exp_in, 1)
        dve.wait_ge(expd, 2)
        step(dve.tensor_reduce(m1, expg, AX.X, ALU.add))
        step(dve.tensor_scalar(tmp3, ge, 1.0, None, ALU.add))
        step(dve.tensor_tensor(m1, m1, tmp3, ALU.mult))
        step(dve.reciprocal(m1, m1))
        step(dve.tensor_tensor(m2, m1, ge, ALU.mult))
        step(dve.tensor_tensor(gate4, top, m1.to_broadcast([P, 3, 4]), ALU.mult))
        step(dve.tensor_tensor(work, work, m2.to_broadcast([P, 3, 4]), ALU.mult))
        step(dve.tensor_tensor(z[:, :, D:D + 4], gate4, work, ALU.add))
        step(dve.memset(z[:, :, D + 5:D + 8], 0.0))
        dve.tensor_copy(z[:, :, D + 4:D + 5], stat[:, 8:11].unsqueeze(2)).then_inc(gates_ready, 1)
        dve.wait_ge(rank_done, 1)
        rank, pos = col(108, 4), col(120)
        step(dve.tensor_tensor(rank, PS[:, 7, 0:12].rearrange("p (k n) -> p k n", n=4), oh, ALU.mult))
        step(dve.tensor_reduce(pos, rank, AX.X, ALU.add))
        rh = R[:, 160:184].rearrange("p (k n) -> p k n", n=8)
        step(dve.tensor_tensor(rh[:, :, 0:4], oh, tokens.to_broadcast([P, 3, 4]), ALU.mult))
        step(dve.tensor_copy(rh[:, :, 4:8], oh))
        for c in range(PASSES):
            for k in range(3):
                dve.tensor_scalar(Pm[:, c, k, :], route[:, (2 + c) * P:(3 + c) * P], R[:, 120 + k:121 + k], None,
                                  ALU.is_equal).then_inc(pm_ready, 1)
        dve.wait_ge(idx_done, 1)
        got = R[:, 184:208].rearrange("p (c n) -> p c n", n=8)
        step(dve.tensor_copy(got, PS[:, 6, 64:88].rearrange("p (c n) -> p c n", n=8)))
        miss = R[:, 208:220].rearrange("p (c n) -> p c n", n=4)
        spare = route[:, 5 * P + 6:5 * P + 9].unsqueeze(2)
        step(dve.tensor_scalar(miss, got[:, :, 4:8], -1.0, 1.0, ALU.mult, ALU.add))
        step(dve.tensor_tensor(miss, miss, spare.to_broadcast([P, 3, 4]), ALU.mult))
        step(dve.tensor_tensor(miss, miss, got[:, :, 0:4], ALU.add))
        step(dve.tensor_copy(pidx[:, 0:12].rearrange("p (c n) -> p c n", n=4), got[:, :, 0:4]))
        step(dve.tensor_copy(pidx[:, 12:24].rearrange("p (c n) -> p c n", n=4), miss))
        step(dve.tensor_reduce(R[:, 224:225], PS[:, 7, 12:16], AX.X, ALU.max))
        dve.sem_inc(out_rows, 4)
        dve.tensor_copy(pidx[:, 24:25], R[:, 224:225]).then_inc(idx_ready, 1)
        dve.wait_ge(x1_stored, 32)
        dve.wait_ge(idx_ready, 1)
        dve.sem_inc(htg_moved, 1)

        def experts(it):
            def rows_in(n):
                dve.wait_ge(gathered[n], it * 16 + 16)
                if n:
                    dve.wait_ge(htg_turned, it * 8 + 4)
                dve.tensor_scalar(HN, XG[n][:, 0:D], XG[n][:, D + 4:D + 5], None, ALU.mult).then_inc(hn_ready, 1)

            def turned_out(n, r):
                dve.wait_ge(htg_turned, it * 8 + (4 * n + r + 1))
                dve.tensor_tensor(HTG[n][:, 4 * r:4 * r + 4, :], PS[:, 7, :].rearrange("p (c t) -> p c t", c=4),
                                  ln2T[:, 4 * r:4 * r + 4].unsqueeze(2).to_broadcast([P, 4, P]),
                                  ALU.mult).then_inc(htg_moved, 1)

            def hidden(k):
                dve.wait_ge(sil_ready, it * 8 + (k + 1))
                dve.wait_ge(up_done, it * 8 + (k + 2))
                if k:
                    dve.wait_ge(hidT_done, it * 8 + k)
                dve.scalar_tensor_tensor(HID, SIL, XG[k // 4][:, D + k % 4:D + k % 4 + 1], PS[:, 1, :],
                                         ALU.mult, ALU.mult).then_inc(hid_ready, 1)

            def rows_out(n):
                dve.wait_ge(down_done, it * 8 + (4 * n + 5))
                for q in range(4):
                    v = XG[n][:, q * TILE:(q + 1) * TILE]
                    dve.tensor_tensor(v, PS[:, 3 + q, :], v, ALU.add).then_inc(out_rows, 1)

            rows_in(0)
            for r in range(4):
                turned_out(0, r)
            rows_in(1)
            for k in range(8):
                if k == 3:
                    turned_out(1, 2)
                hidden(k)
                if 1 <= k <= 3:
                    turned_out(1, (0, 1, 3)[k - 1])
                if k == 4:
                    rows_out(0)
            rows_out(1)

        with dve.Fori(0, 2) as it:
            experts(it)
        most = dve.value_load(pidx[0:1, 24:25], min_val=0, max_val=TOK)
        with dve.If(most > P):
            with dve.Fori(1, PASSES) as c:
                with dve.Fori(0, 2) as j:
                    experts(c * 2 + j)


_OUTS = [("y", (TOK + P, D)), ("k_prompt", (1, 1, SEQ, H, HD)), ("v_prompt", (1, 1, SEQ, H, HD)),
         ("pool_prompt", (1, 1, BUF, PW)), ("k_sample", (1, DEC_B, DEC_T, H, HD)),
         ("v_sample", (1, DEC_B, DEC_T, H, HD)), ("pool_sample", (1, DEC_B, BUF, PW))]


def small_inputs(i):
    s = np.zeros((P, 569), np.float32)
    s[:, 0:16] = i["ln1_w"][0].reshape(DC, P).T
    s[:, 16:32] = i["ln2_w"][0].reshape(DC, P).T
    s[:, 32:96] = i["q_norm_w"][0][None]
    s[:, 96:160] = i["k_norm_w"][0][None]
    s[:, 160:168] = i["pool_scale"][0].reshape(8, P).T
    s[:, 168:488].reshape(P, DC, 20)[:, :, 0:4] = i["w_router_group"][0].reshape(DC, P, 4).transpose(1, 0, 2)
    s[:, 168:488].reshape(P, DC, 20)[:, :, 4:20] = i["w_router_expert"][0].reshape(DC, P, 16).transpose(1, 0, 2)
    s[0:4, 488] = i["b_router_group"][0]
    s[4:20, 488] = i["b_router_expert"][0]
    rel = i["rel_bias"]
    for t in range(4):
        s[32 * t:32 * t + 32, 489 + 16 * t:505 + 16 * t] = rel.reshape(NB, 8, 2).transpose(0, 2, 1).reshape(NB, 16)
    s[0:32, 553:569] = rel
    s[32, 553:569] = 1.0
    return s


def kernel(**inputs):
    import concourse.bacc as _bacc
    from concourse.bass_utils import run_bass_kernel_spmd as _run

    inputs = {k: np.asarray(v) for k, v in inputs.items()}
    nc = _bacc.Bacc("TRN2", target_bir_lowering=False, num_devices=1)
    arrays, a, o = {}, {}, {}
    given = {n: inputs[n] for n in ("x_prompt", "x_sample", "cache_k", "cache_v", "state_pool", "w_in", "w_pool",
                                    "w_o", "w_gate", "w_up", "w_down")}
    given["small"] = small_inputs(inputs)
    given.update(shape_constants())
    for name, v in given.items():
        v = np.ascontiguousarray(v)
        arrays[f"in_{name}"] = v
        a[name] = nc.dram_tensor(f"in_{name}", v.shape, mybir.dt.from_np(v.dtype), kind="ExternalInput").ap()
    for name, shape in _OUTS:
        o[name] = nc.dram_tensor(f"out_{name}", shape, F32, kind="ExternalOutput").ap()
    hybrid_layer(nc, a, o)
    r = _run(nc, [arrays], core_ids=[0]).results[0]
    y = r["out_y"]
    return (y[0:SEQ].reshape(1, SEQ, D), y[SEQ:TOK].reshape(DEC_B, DEC_T, D),
            r["out_k_prompt"], r["out_v_prompt"], r["out_pool_prompt"],
            r["out_k_sample"], r["out_v_sample"], r["out_pool_sample"])
```

```python
from contextlib import ExitStack
import math

import numpy as np

import concourse.bass as bass
from concourse import mybir
from concourse.alu_op_type import AluOpType as ALU

F32 = mybir.dt.float32
I32 = mybir.dt.int32
ACT = mybir.ActivationFunctionType
AX = mybir.AxisListType

P = 128
D = 2048
DC = D // P
SEQ, DEC_B, DEC_T, PAST = 256, 8, 4, 2048
NS = DEC_B * DEC_T
TOK = SEQ + NS
CHUNKS = [(0, 128), (128, 128), (256, 32)]
H, HD = 16, 64
PAIRS = H // 2
AW = H * HD
PW = D - AW
IN_W = 3 * AW + PW
TILE = 512
POOL_W = (2, 4, 8, 16)
BUF = 15
GW = PW // 4
NB = 32
EPS = 1e-6
SCALE = HD ** -0.5
NEG = -1e30
FE = 512
NG, EPG = 4, 4
NE = NG * EPG
SLOTS = 6
SLOT = 4096
NEAR = 512
FAR = 96
GV = 5
KEYS = NEAR + 4 * FAR + NS
PASSES = 3


def counted(dist):
    d = np.asarray(dist)
    n = ((d <= 128).astype(int) + ((d <= 512) & (d % 4 == 0)) + ((d <= 2048) & (d % 16 == 0)))
    return np.where(d >= 0, n, 0)


def bucket(dist):
    d = np.maximum(np.asarray(dist), 1)
    df = d.astype(np.float32)
    large = 16 + (np.log(df / np.float32(16)) / np.float32(math.log(2048 / 16)) * np.float32(16)).astype(np.int32)
    return np.where(np.asarray(dist) < 16, np.maximum(dist, 0), np.minimum(large, NB - 1))


def log_count(dist):
    n = counted(dist)
    return np.where(n > 0, np.log(np.maximum(n, 1)), NEG).astype(np.float32)


def shape_constants():
    out = {}
    y = np.arange(384)
    dist = 255 - y
    one = np.zeros((33, 384), np.float32)
    one[np.clip(bucket(dist), 0, NB - 1), y] = 1.0
    one[32] = log_count(dist)
    cols = KEYS - NS + DEC_B * NS
    hot = np.zeros((4, NB, cols), np.float32)
    mask = np.full((4, 16, cols), NEG, np.float32)
    for t in range(4):
        near = np.array([[NEAR + t - 4 * p - j for p in range(128)] for j in range(4)]).ravel()
        far = np.array([[PAST + t - 16 * p - j for p in range(FAR)] for j in range(4)]).ravel()
        new = np.array([[t - k % 4 if k // 4 == b else -1 for k in range(NS)] for b in range(DEC_B)]).ravel()
        d = np.concatenate([near, far, new])
        hot[t, np.clip(bucket(d), 0, NB - 1), np.arange(cols)] = 1.0
        mask[t] = log_count(d)[None]
    bias = np.zeros((P, 384 + 2 * cols), np.float32)
    bias[:33, :384] = one
    bias[:, 384:384 + cols] = hot.reshape(P, cols)
    bias[:64, 384 + cols:] = mask.reshape(64, cols)
    out["c_bias"] = bias
    rows, l = np.arange(SEQ)[:, None], np.arange(SEQ)[None]
    pool = np.zeros((P, 4 * 256 + 4 * 128 + 2 * 4 * 32), np.float32)
    for g, w in enumerate(POOL_W):
        full = ((rows <= l) & (rows > l - w)) / np.minimum(l + 1, w) - (rows == l)
        pool[:, g * 256:(g + 1) * 256] = full[:128]
        pool[:, 1024 + g * 128:1024 + (g + 1) * 128] = full[128:, 128:]
        for b in range(DEC_B):
            for t in range(DEC_T):
                at = BUF + t
                for r in range(at - w + 1, at + 1):
                    if r < BUF:
                        pool[b * BUF + r, 1536 + g * 32 + b * 4 + t] = 1.0 / w
                    else:
                        pool[b * 4 + r - BUF, 1664 + g * 32 + b * 4 + t] = 1.0 / w
                pool[b * 4 + t, 1664 + g * 32 + b * 4 + t] -= 1.0
    out["c_pool"] = pool
    eye = np.eye(P, dtype=np.float32)
    out["c_eye"] = np.concatenate([eye, eye[::-1]], axis=1).copy()
    r = np.zeros((P, 2 * P + 3 * P + 3 + 3 + 3 + 4), np.float32)
    r[:, 5 * P + 9:] = [4, 3, 2, 1]
    r[:, :P] = np.triu(np.ones((P, P), np.float32), 1)
    r[:, P:2 * P] = 1.0
    r[:, 2 * P:5 * P] = np.arange(3 * P)[None]
    for k, (t0, n) in enumerate(CHUNKS):
        r[:, 5 * P + k] = t0 + np.arange(P)
        r[:n, 5 * P + 3 + k] = 1.0
        r[:, 5 * P + 6 + k] = TOK + np.arange(P)
    out["c_route"] = r
    return out


class Steps:

    def __init__(self, eng, sem):
        self.eng, self.sem, self.n = eng, sem, 0
        self.turn = None

    def did(self, ins):
        ins.then_inc(self.sem, 1)
        self.n += 1

    def settle(self):
        self.eng.wait_ge(self.sem, self.n if self.turn is None else self.turn + self.n)

    def begin(self, turn, per):
        self.outer, self.per = self.n, per
        self.turn, self.n = turn * per, self.n

    def end(self, turns):
        assert self.n - self.outer == self.per, (self.n - self.outer, self.per)
        self.turn, self.n = None, self.outer + self.per * turns


def hybrid_layer(nc, a, o):
    ctx = ExitStack()
    with ctx:
        build(nc, a, o, ctx)


def build(nc, a, o, ctx):
    def sb(name, shape, dt=F32):
        return ctx.enter_context(nc.sbuf_tensor(name, shape, dt))

    def sem(name):
        return ctx.enter_context(nc.semaphore(name))

    ring = sb("ring", [P, SLOTS, SLOT])
    HT = sb("HT", [P, DC * TOK])
    X = sb("X", [P, 3 * D])
    Z = sb("Z", [P, 3 * IN_W])
    eye2 = sb("eye2", [P, 2 * P])
    small = sb("small", [P, 16 + 16 + 128 + 8 + 16 * 20 + 20 + 64 + 16])
    E = sb("E", [64, KEYS - NS + DEC_B * NS])
    Qbd = sb("Qbd", [P, 520])
    qkTs = sb("qkTs", [P, 2, PAIRS, NS])
    stage = sb("stage", [P, 6, 256])
    stat = sb("stat", [P, 160])
    pidx = sb("pidx", [P, 40], I32)
    gS = sb("gS", [H, 384])
    gates = sb("gates", [P, 80])
    PS = ctx.enter_context(nc.psum_tensor("PS", [P, 8, TILE], F32))

    hT = HT[:, :].rearrange("p (c t) -> p c t", t=TOK)
    x_rows = X[:, :].rearrange("p (c d) -> p c d", d=D)
    z = Z[:, :].rearrange("p (c n) -> p c n", n=IN_W)
    eye, flip = eye2[:, 0:P], eye2[:, P:2 * P]
    ln1T, ln2T = small[:, 0:16], small[:, 16:32]
    qkw = small[:, 32:160].rearrange("p (w d) -> p w d", d=HD)
    pscale = small[:, 160:168]
    wr = small[:, 168:488].rearrange("p (c n) -> p c n", n=20)
    rb = small[:, 488:508]
    relS = small[:, 508:572]
    relP = small[0:33, 572:588]

    sq_tmp = X[:, 0:2048]
    state = X[0:DEC_B * BUF, 2048:3072]
    dT = X[:, 3072:3072 + 4 * TOK].rearrange("p (b c t) -> p b c t", b=2, t=TOK)
    KT = X[:, 0:1792].rearrange("p (b n) -> p b n", b=2)
    PTs = X[:, 1792:2368].rearrange("p (c n) -> p c n", n=64)
    SB = X[0:64, 2368:2368 + KEYS]
    OS = X[0:64, 3296:4320]
    PP = X[:, 4320:5088].rearrange("p (b n) -> p b n", b=2)
    PPT = X[:, 5088:5856].rearrange("p (b n) -> p b n", b=2)
    st_q, st_k, st_v = (stage[:, n, :].rearrange("p (c n) -> p c n", c=2) for n in range(3))
    qTz = [stage[:, 3, :], stage[:, 4, :]]
    kTp = stage[:, 5, :]
    zTs = stage[:, :, :].rearrange("p a b -> p (a b)")[:, 0:2 * TOK].rearrange("p (b t) -> p b t", b=2)
    T = ring[:, 4, :].rearrange("p (h n) -> p h n", h=H)
    EC = KEYS - NS + DEC_B * NS
    c_one = ring[0:33, 5, 0:384]
    c_hot = ring[:, 5, 384:384 + EC]
    c_mask = ring[0:64, 5, 384 + EC:384 + 2 * EC]
    c_pool = ring[:, 5, 0:1792]
    wpool = ring[:, 5, 1792:3840].rearrange("p (g c e) -> p g c e", g=4, c=2)
    x1T = X[:, 0:DC * TOK].rearrange("p (c t) -> p c t", t=TOK)
    route = X[:, 4608:4608 + 653]
    R = X[:, 5264:5264 + 460]
    LG = X[0:20, 5728:5728 + TOK]
    Pm = Z[:, 2048:3200].rearrange("p (c k n) -> p c k n", c=3, k=3)
    GT = gates[:, 0:70].rearrange("p (n v) -> p n v", v=GV)
    GS = [gates[:, 70 + GV * n:70 + GV * (n + 1)] for n in range(2)]
    HTG = [HT[:, n * 2048:(n + 1) * 2048].rearrange("p (c t) -> p c t", t=P) for n in range(2)]
    XG = [X[:, n * D:(n + 1) * D] for n in range(2)]
    HN = Z[:, 0:2048]
    SIL, HID = Z[:, 3200:3712], Z[:, 3712:4224]
    HIDT = Z[:, 4224:4736].rearrange("p (f t) -> p f t", t=P)

    g_scr = nc.dram_tensor("g_scr", (H, 384), F32).ap()
    x1_scr = nc.dram_tensor("x1_scr", (TOK, D), F32).ap()

    landed = [sem(f"landed{s}") for s in range(SLOTS)]
    used = [sem(f"used{s}") for s in range(SLOTS)]
    x_in, const_in, state_in = sem("x_in"), sem("const_in"), sem("state_in")
    g_stored, x_again, route_in, x1_stored = sem("g_stored"), sem("x_again"), sem("route_in"), sem("x1_stored")
    stored, pstored = sem("stored"), sem("pstored")
    dve_step, act_step = sem("dve_step"), sem("act_step")
    squares, root_in, roots = sem("squares"), sem("root_in"), sem("roots")
    h_rows, h_turned, h_moved = sem("h_rows"), sem("h_turned"), sem("h_moved")
    bias_mm, bias_moved, g_ready = sem("bias_mm"), sem("bias_moved"), sem("g_ready")
    proj_done, z_moved, zT_moved, zT_turned = (sem(n) for n in ("proj_done", "z_moved", "zT_moved", "zT_turned"))
    normed = sem("normed")
    sT_done, sT_moved = sem("sT_done"), sem("sT_moved")
    d_done, d_moved, y_done, y_moved = sem("d_done"), sem("d_moved"), sem("y_done"), sem("y_moved")
    stage_ready = sem("stage_ready")
    pT, kt_turned, s_pair = sem("pT"), sem("kt_turned"), sem("s_pair")
    pS, pPT, pO, sPT, sO, sOT = (sem(n) for n in ("pS", "pPT", "pO", "sPT", "sO", "sOT"))
    qk_moved, ktn, ktf, p_exp, ppt_moved = (sem(n) for n in ("qk_moved", "ktn", "ktf", "p_exp", "ppt_moved"))
    s_exp, pts_n, pts_f, os_a, os_b, po_moved = (sem(n) for n in ("s_exp", "pts_n", "pts_f", "os_a", "os_b", "po_moved"))
    qbd_ready, p_negmax, p_norm, s_negmax, s_inv, diag = (
        sem(n) for n in ("qbd_ready", "p_negmax", "p_norm", "s_negmax", "s_inv", "diag"))
    wo_done, wo_moved, s_sum = sem("wo_done"), sem("wo_moved"), sem("s_sum")
    rl_done, rl_moved, lgT_done, expd = sem("rl_done"), sem("rl_moved"), sem("lgT_done"), sem("expd")
    exp_in, oh_ready, rank_done, pm_ready, idx_done, idx_ready, gates_ready = (
        sem(n) for n in ("exp_in", "oh_ready", "rank_done", "pm_ready", "idx_done", "idx_ready", "gates_ready"))
    idx_copied, pool_turn, rows_ready = sem("idx_copied"), sem("pool_turn"), sem("rows_ready")
    x1_turned, x1_moved = sem("x1_turned"), sem("x1_moved")
    gathered = [sem(f"gathered{n}") for n in range(2)]
    scattered = [sem(f"scattered{n}") for n in range(2)]
    hn_ready, htg_turned, htg_moved, gs_ready, rms_in = (
        sem(n) for n in ("hn_ready", "htg_turned", "htg_moved", "gs_ready", "rms_in"))
    gate_done, up_done, sil_ready, hid_ready = sem("gate_done"), sem("up_done"), sem("sil_ready"), sem("hid_ready")
    hidT_done, hidT_moved, down_done, out_rows = sem("hidT_done"), sem("hidT_moved"), sem("down_done"), sem("out_rows")

    w_in_t = a["w_in"][0].rearrange("(c p) n -> p c n", p=P)
    w_o_t = a["w_o"][0].rearrange("(c p) n -> p c n", p=P)
    xp_t = a["x_prompt"][0].rearrange("(c p) d -> p c d", p=P)
    xs_t = a["x_sample"].rearrange("b t d -> (b t) d")

    def near_rows(cache, b):
        return cache[0, b, PAST - NEAR:PAST].rearrange("(p j) h d -> p (j h d)", j=4)

    def far_rows(cache, b):
        return cache[0, b, 0:PAST - NEAR].rearrange("(p j) h d -> p j (h d)", j=16)[:, 0:4, :]

    def load_columns(sp, w_t, col, par):
        for half in range(2):
            s = 2 * par + half
            sp.dma_start(ring[:, s, :].rearrange("p (c n) -> p c n", n=TILE),
                         w_t[:, half * 8:half * 8 + 8, bass.ds(col, TILE)]).then_inc(landed[s], 16)

    FIRST_BANKS = (7, 0, 1, 2)
    block = ctx.enter_context(nc.Block())

    LOADS_P1, LOADS_AT, LOADS_WO = 4, 8, 2
    BASE_AT, BASE_WO = LOADS_P1, LOADS_P1 + LOADS_AT
    BASE_MOE = [BASE_WO + LOADS_WO] * 4 + [1, 2]

    @block.sync
    def _(sp):
        sp.dma_start(x_rows[:, 0:2, :], xp_t).then_inc(x_in, 16)
        sp.dma_start(x_rows[0:NS, 2, :], xs_t).then_inc(x_in, 16)
        sp.dma_start(ring[:, 5, 0:384 + 2 * EC], a["c_bias"]).then_inc(landed[5], 16)
        for par in range(2):
            load_columns(sp, w_in_t, par * TILE, par)
        with sp.Fori(1, 4) as i:
            for par in range(2):
                sp.wait_ge(proj_done, 8 * i + (4 * par - 4))
                load_columns(sp, w_in_t, (2 * i + par) * TILE, par)
        sp.wait_ge(bias_moved, 4)
        sp.dma_start(ring[:, 5, 0:1792], a["c_pool"]).then_inc(landed[5], 16)
        sp.dma_start(ring[:, 5, 1792:3840].rearrange("p (g c e) -> p g c e", g=4, c=2),
                     a["w_pool"][0].rearrange("g (c p) e -> p g c e", p=P)).then_inc(state_in, 16)
        sp.wait_ge(h_turned, 12)
        sp.dma_start(state, a["state_pool"][0].rearrange("b r n -> (b r) n")).then_inc(state_in, 16)

        def cached(s, i):
            rows = a["cache_k" if s < 2 else "cache_v"][0, bass.ds(i, 1)]
            if s % 2 == 0:
                sp.dma_start(ring[:, s, :], rows[:, PAST - NEAR:PAST].rearrange("a (p j) h d -> p (a j h d)", j=4)
                             ).then_inc(landed[s], 16)
            else:
                sp.dma_start(ring[0:FAR, s, :].rearrange("p (j n) -> p j n", j=4),
                             rows[:, 0:PAST - NEAR].rearrange("a (p j) h d -> p (a j) (h d)", j=16)[:, 0:4, :]
                             ).then_inc(landed[s], 16)

        for s, freed, n in ((0, proj_done, 28), (1, proj_done, 28), (2, proj_done, 32), (3, proj_done, 32)):
            sp.wait_ge(freed, n)
            cached(s, 0)
        with sp.Fori(1, DEC_B) as i:
            for s, freed, n in ((0, kt_turned, 16 * i - 1), (1, kt_turned, 16 * i), (2, used[2], i),
                                (3, used[3], i)):
                sp.wait_ge(h_turned, 12)
                sp.wait_ge(freed, n)
                cached(s, i)
        for par, freed in enumerate((((kt_turned, 128),), ((used[2], 8), (used[3], 8)))):
            for which, n in freed:
                sp.wait_ge(which, n)
            load_columns(sp, w_o_t, par * TILE, par)
        sp.wait_ge(sO, DEC_B)
        sp.wait_ge(stage_ready, 3 * PAIRS)
        sp.wait_ge(stored, 16 * 5)
        sp.wait_ge(pstored, 16 * 9)
        sp.dma_start(z[:, 0:2, 0:D], xp_t).then_inc(x_again, 16)
        sp.dma_start(z[0:NS, 2, 0:D], xs_t).then_inc(x_again, 16)
        sp.dma_start(route, a["c_route"]).then_inc(route_in, 16)
        for par in range(2):
            sp.wait_ge(wo_done, 4 * par + 4)
            load_columns(sp, w_o_t, (2 + par) * TILE, par)
        sp.wait_ge(pS, 2 * PAIRS)
        sp.wait_ge(y_done, 8)

        def experts(it, par8):
            def up(k):
                wg, wu = (a[n][0, bass.ds(par8 * 8 + k, 1)].rearrange("a (c p) n -> p (a c) n", p=P)
                          for n in ("w_gate", "w_up"))
                for s, w, half, freed, n in ((4, wg, 0, used[4], 1), (5, wg, 1, gate_done, 1),
                                             (0, wu, 0, used[0], 1), (1, wu, 1, up_done, 1)):
                    if s == 0:
                        sp.wait_ge(wo_done, 12)
                    sp.wait_ge(freed, it * 8 + (n + k))
                    sp.dma_start(ring[:, s, :].rearrange("p (c n) -> p c n", n=TILE),
                                 w[:, half * 8:half * 8 + 8, :]).then_inc(landed[s], 16)

            def down(k):
                wd = a["w_down"][0, bass.ds(par8 * 8 + k, 1)].rearrange("a (f p) n -> p (a f) n", p=P)
                sp.wait_ge(wo_done, 16)
                for s, half, freed, n in ((2, 0, used[2], 8), (3, 1, down_done, 1)):
                    sp.wait_ge(freed, it * 8 + (n + k))
                    sp.dma_start(ring[:, s, :].rearrange("p (f n) -> p f n", n=D),
                                 wd[:, half * 2:half * 2 + 2, :]).then_inc(landed[s], 16)

            up(0)
            for k in range(8):
                if k < 7:
                    up(k + 1)
                down(k)

        with sp.Fori(0, 2) as it:
            experts(it, it)
        sp.wait_ge(idx_ready, 1)
        most = sp.value_load(pidx[0:1, 28:29], min_val=0, max_val=TOK)
        with sp.If(most > P):
            with sp.Fori(1, PASSES) as c:
                with sp.Fori(0, 2) as j:
                    experts(c * 2 + j, j)

    @block.gpsimd
    def _(pool):
        pool.dma_start(o["pool_sample"][0, :, 0:BUF - DEC_T, :], a["state_pool"][0, :, DEC_T:BUF, :]).then_inc(pstored, 16)
        pool.wait_ge(normed, 4)
        for n, name in ((1, "k"), (2, "v")):
            if n == 2:
                pool.wait_ge(z_moved, 3 + 18)
            pool.dma_start(o[f"{name}_prompt"][0, 0].rearrange("(c p) h d -> p c (h d)", p=P),
                           z[:, 0:2, n * AW:(n + 1) * AW]).then_inc(stored, 16)
            pool.dma_start(o[f"{name}_sample"][0].rearrange("b t h d -> (b t) (h d)"),
                           z[0:NS, 2, n * AW:(n + 1) * AW]).then_inc(stored, 16)
        pool.wait_ge(z_moved, 3 + 24)
        pool.dma_start(o["pool_prompt"][0, 0], z[P - BUF:P, 1, 3 * AW:IN_W]).then_inc(stored, 16)
        for b in range(DEC_B):
            pool.dma_start(o["pool_sample"][0, b, BUF - DEC_T:BUF, :],
                           z[b * DEC_T:(b + 1) * DEC_T, 2, 3 * AW:IN_W]).then_inc(pstored, 16)
        with pool.Fori(0, PAIRS) as i:
            pool.wait_ge(pT, i + 1)
            for n, dst in ((0, st_q), (1, st_k), (2, st_v)):
                if n == 2:
                    pool.wait_ge(pO, i + 1)
                pool.tensor_copy(dst, z[:, 0:2, bass.ds(i * P + n * AW, P)]).then_inc(stage_ready, 1)

        def stage_rows(col, target, n, nth):
            at = 29 + 2 * n + target
            pool.tensor_copy(pidx[:, at:at + 1], pidx[:, bass.ds(col + 14 * target, 1)]).then_inc(idx_copied, 1)
            pool.wait_ge(idx_copied, nth)

        def gather(n):
            pool.indirect_dma_start(
                out=XG[n], out_offset=None, in_=x1_scr,
                in_offset=bass.IndirectOffsetOnAxis(ap=pidx[:, 29 + 2 * n:30 + 2 * n], axis=0),
            ).then_inc(gathered[n], 16)

        def experts(it):
            for n in range(2):
                stage_rows(it * 2 + n, 1, n, it * 4 + (2 * n + 3))
                pool.wait_ge(out_rows, it * 8 + (4 * n + 8))
                if n:
                    pool.wait_ge(scattered[0], it * 16 + 16)
                pool.sem_inc(pool_turn, 1)
                pool.indirect_dma_start(
                    out=o["y"], out_offset=bass.IndirectOffsetOnAxis(ap=pidx[:, 30 + 2 * n:31 + 2 * n], axis=0),
                    in_=XG[n], in_offset=None).then_inc(scattered[n], 16)
                stage_rows(it * 2 + (n + 2), 0, n, it * 4 + (2 * n + 4))
                pool.wait_ge(scattered[n], it * 16 + 16)
                pool.sem_inc(pool_turn, 1)
                gather(n)

        pool.wait_ge(stored, 16 * 5)
        pool.wait_ge(pstored, 16 * (1 + DEC_B))
        pool.wait_ge(rows_ready, 1)
        pool.wait_ge(x1_stored, 16 * 8)
        for n in range(2):
            stage_rows(n, 0, n, n + 1)
            gather(n)
        pool.wait_ge(idx_ready, 1)
        with pool.Fori(0, 2) as it:
            experts(it)
        most = pool.value_load(pidx[0:1, 28:29], min_val=0, max_val=TOK)
        with pool.If(most > P):
            with pool.Fori(1, PASSES) as c:
                with pool.Fori(0, 2) as j:
                    experts(c * 2 + j)
        for n in range(2):
            pool.wait_ge(gathered[n], 16 * 3)

    @block.scalar
    def _(act):
        act.dma_start(eye2[:, :], a["c_eye"]).then_inc(const_in, 16)
        act.dma_start(small[:, 0:588], a["small"]).then_inc(const_in, 16)
        act.sem_inc(z_moved, 3)
        act.sem_inc(zT_moved, 2)
        act.sem_inc(zT_turned, 2)
        act.sem_inc(ppt_moved, 2)
        act.sem_inc(po_moved, 1)

        act.wait_ge(root_in, 1)
        act.wait_ge(x_in, 32)
        for k, (t0, m) in enumerate(CHUNKS):
            act.activation(Z[0:m, k * D:(k + 1) * D], x_rows[0:m, k, 0:D], ACT.Square,
                           accum_out=stat[0:m, k:k + 1]).then_inc(squares, 1)
        act.wait_ge(root_in, 2)
        act.activation(stat[:, 4:7], stat[:, 4:7], ACT.Sqrt).then_inc(roots, 1)
        act.wait_ge(bias_moved, 1)
        act.wait_ge(g_ready, 1)
        act.dma_start(g_scr, gS[:, :]).then_inc(g_stored, 16)
        act.wait_ge(g_stored, 16)
        act.dma_start(T, bass.AP(g_scr.tensor, 0, [[1, P], [384, H], [1, 256]])).then_inc(landed[4], 16)

        def block_out(i, q, done, turn0):
            act.wait_ge(done, 8 * i + (q + 1))
            act.wait_ge(zT_turned, 8 * i + (8 * turn0 + q + 1))
            act.activation(zTs[:, q % 2, :], PS[:, q % 2, 0:TOK], ACT.Copy).then_inc(zT_moved, 1)

        def z_out(i):
            for q in range(8):
                block_out(i, q, proj_done, 0)
                if q in (4, 7):
                    par = q // 7
                    act.wait_ge(zT_turned, 8 * i + (4 * par + 6))
                    for k, (t0, m) in enumerate(CHUNKS):
                        act.activation(z[0:m, k, bass.ds(i * 2 * TILE + par * TILE, TILE)],
                                       PS[0:m, 2 + k, :], ACT.Copy).then_inc(z_moved, 1)

        def head_roots(w):
            for part in range(2):
                act.wait_ge(root_in, 3 + 2 * w + part)
                v = stat[:, 16:48] if part == 0 else stat[0:NS, 48:64]
                act.activation(v, v, ACT.Sqrt).then_inc(roots, 1)

        act.wait_ge(roots, 1)
        with act.Fori(0, 2) as i:
            z_out(i)
        head_roots(0)
        with act.Fori(2, 3) as i:
            z_out(i)
        head_roots(1)
        with act.Fori(3, 4) as i:
            z_out(i)
        act.wait_ge(sT_done, 1)
        act.activation(qkTs[:, 0], PS[:, 6, 0:256].rearrange("p (a t) -> p a t", t=NS), ACT.Copy,
                       scale=SCALE).then_inc(sT_moved, 1)
        act.activation(qkTs[:, 1], PS[:, 6, 256:512].rearrange("p (a t) -> p a t", t=NS),
                       ACT.Copy).then_inc(sT_moved, 1)
        for g in range(4):
            for eh in range(2):
                act.wait_ge(y_done, 2 * g + eh + 1)
                act.activation(hT[:, 8 + 2 * g + eh, :], PS[:, 4 + eh, 0:TOK], ACT.Identity,
                               scale=pscale[:, 2 * g + eh:2 * g + eh + 1]).then_inc(y_moved, 1)
        act.wait_ge(diag, 4)
        with act.Fori(0, PAIRS) as i:
            act.wait_ge(pT, i + 2)
            for par in range(2):
                r = slice(64 * par, 64 * par + 64)
                act.activation(qTz[par][r], PS[r, 6, 0:256], ACT.Copy, scale=SCALE).then_inc(qk_moved, 1)
            act.activation(kTp, PS[:, 6, 256:512], ACT.Copy).then_inc(qk_moved, 1)

            def keys_out(pair):
                act.wait_ge(kt_turned, i * 16 + (2 * pair + 1))
                act.wait_ge(s_pair, i * 8 + (pair + 1))
                act.activation(KT[:, pair % 2, 0:NEAR], PS[:, 2 * (pair % 2), :], ACT.Copy).then_inc(ktn, 1)

            def prompt_exp(par):
                act.wait_ge(p_negmax, i * 2 + (par + 1))
                for q, (c0, c1) in enumerate(((0, 128), (128, 384))):
                    act.activation(PP[:, par, c0:c1], PS[:, 7 - par, c0:c1], ACT.Exp,
                                   bias=stat[:, 68 + 4 * par + q:69 + 4 * par + q],
                                   accum_out=stat[:, 76 + 4 * par + q:77 + 4 * par + q]).then_inc(p_exp, 1)

            def prompt_turned(par):
                act.wait_ge(pPT, i * 2 + (par + 1))
                act.activation(PPT[:, par, :], PS[:, par, 0:384], ACT.Copy).then_inc(ppt_moved, 1)

            for pair in range(6):
                keys_out(pair)
            prompt_exp(0)
            keys_out(6)
            prompt_exp(1)
            keys_out(7)
            prompt_turned(0)
            prompt_turned(1)
            act.wait_ge(s_negmax, i + 1)
            act.activation(SB, SB, ACT.Exp, bias=stat[0:64, 65:66],
                           accum_out=stat[0:64, 66:67]).then_inc(s_exp, 1)
            act.wait_ge(pO, i + 2)
            act.activation(hT[:, bass.ds(i, 1), 0:SEQ].rearrange("p a t -> p (a t)"), PS[:, 2, 0:SEQ],
                           ACT.Copy).then_inc(po_moved, 1)
            act.wait_ge(sPT, i + 1)
            act.activation(PTs[:, 0:4, :], PS[:, 4, 0:256].rearrange("p (c n) -> p c n", n=64),
                           ACT.Copy).then_inc(pts_n, 1)
            act.activation(PTs[0:FAR, 4:8, :], PS[0:FAR, 4, 256:512].rearrange("p (c n) -> p c n", n=64),
                           ACT.Copy).then_inc(pts_n, 1)
            act.wait_ge(sO, i + 1)
            act.wait_ge(s_inv, i + 1)
            act.activation(OS[:, 0:TILE], PS[0:64, 6, :], ACT.Identity,
                           scale=stat[0:64, 67:68]).then_inc(os_a, 1)
        act.wait_ge(root_in, 7)
        for n in range(4 * 4 + 3):
            if n < 16:
                block_out(n // 8, n % 8, wo_done, 4)
            if n % 4 == 2 and n > 4:
                t = n // 4 - 1
                act.wait_ge(wo_moved, 3 * t + 6)
                for k, (t0, m) in enumerate(CHUNKS):
                    act.activation(z[0:m, k, D + t * TILE:D + (t + 1) * TILE], z[0:m, k, t * TILE:(t + 1) * TILE],
                                   ACT.Square, accum_out=stat[0:m, 96 + 4 * k + t:97 + 4 * k + t]).then_inc(squares, 1)
                act.dma_start(x1_scr[0:SEQ, t * TILE:(t + 1) * TILE].rearrange("(c p) d -> p c d", p=P),
                              z[:, 0:2, t * TILE:(t + 1) * TILE]).then_inc(x1_stored, 16)
                act.dma_start(x1_scr[SEQ:TOK, t * TILE:(t + 1) * TILE],
                              z[0:NS, 2, t * TILE:(t + 1) * TILE]).then_inc(x1_stored, 16)
        act.wait_ge(rl_done, 1)
        act.activation(LG, PS[0:20, 5, 0:TOK], ACT.Copy).then_inc(rl_moved, 1)
        act.wait_ge(root_in, 8)
        act.activation(stat[:, 4:7], stat[:, 4:7], ACT.Sqrt).then_inc(roots, 1)
        for n in range(2):
            act.wait_ge(exp_in, n + 1)
            v = R[:, 60:72] if n == 0 else R[:, 132:135]
            act.activation(v, v, ACT.Exp).then_inc(expd, 1)

        def experts(it):
            def sil(k):
                act.wait_ge(gate_done, it * 8 + (k + 2))
                act.activation(SIL, PS[:, 0, :], ACT.Silu).then_inc(sil_ready, 1)

            def turned(k):
                act.wait_ge(hidT_done, it * 8 + (k + 1))
                act.activation(HIDT, PS[:, 2, :].rearrange("p (f t) -> p f t", t=P), ACT.Copy).then_inc(hidT_moved, 1)

            for k in range(8):
                if k:
                    act.wait_ge(hid_ready, it * 8 + k)
                sil(k)
                if k:
                    turned(k - 1)
            turned(7)

        with act.Fori(0, 2) as it:
            experts(it)
        act.wait_ge(idx_ready, 1)
        most = act.value_load(pidx[0:1, 28:29], min_val=0, max_val=TOK)
        with act.If(most > P):
            with act.Fori(1, PASSES) as c:
                with act.Fori(0, 2) as j:
                    experts(c * 2 + j)

    @block.tensor
    def _(pe):
        def mm(out, lhsT, rhs, start, stop):
            return pe.matmul(out, lhsT, rhs, start=start, stop=stop, skip_group_check=True)

        def turn_rows(rows, moved0):
            for n in range(12):
                k, g = n // 4, n % 4
                m = CHUNKS[k][1]
                if n >= 2:
                    pe.wait_ge(h_moved, moved0 + n - 1)
                for q in range(4):
                    c = 4 * g + q
                    ins = pe.transpose(PS[:, 6 + n % 2, q * m:(q + 1) * m], rows[0:m, k, c * P:(c + 1) * P],
                                       eye[0:m, 0:m])
                ins.then_inc(h_turned, 1)

        pe.sem_inc(pT, 1)
        pe.sem_inc(pO, 1)
        pe.sem_inc(s_pair, 2)
        for s in (used[4], used[0], gate_done, up_done, down_done):
            pe.sem_inc(s, 1)
        pe.wait_ge(const_in, 32)
        pe.wait_ge(landed[5], 16)
        mm(PS[0:H, 0, 0:384], relP, c_one, True, True).then_inc(bias_mm, 1)
        for n, (c0, c1) in enumerate(((0, 512), (512, 896), (896, EC))):
            mm(PS[0:64, 1 + n, 0:c1 - c0], relS, c_hot[:, c0:c1], True, True).then_inc(bias_mm, 1)
        pe.wait_ge(h_rows, 3)
        turn_rows(x_rows, 0)
        pe.wait_ge(h_moved, 12)
        pe.wait_ge(bias_moved, 4)

        def column_block(i, q, done, moved, base, turn0):
            def turn_block(q):
                pe.wait_ge(zT_moved, 8 * i + (8 * turn0 + q + 3))
                if q % 4 == 0:
                    pe.wait_ge(moved, 6 * i + (3 * (q // 4) + 3))
                for k, (t0, m) in enumerate(CHUNKS):
                    ins = pe.transpose(PS[0:m, 2 + k, (q % 4) * P:(q % 4 + 1) * P], zTs[:, q % 2, t0:t0 + m], eye)
                ins.then_inc(zT_turned, 1)

            pe.wait_ge(zT_moved, 8 * i + (8 * turn0 + q + 1))
            for half in range(2):
                s = 2 * (q // 4) + half
                if q % 4 == 0:
                    pe.wait_ge(landed[s], 16 * i + 16 * (base + 1))
                w = ring[:, s, :].rearrange("p (c n) -> p c n", n=TILE)
                for c in range(8):
                    cc = half * 8 + c
                    ins = mm(PS[:, q % 2, 0:TOK], w[:, c, (q % 4) * P:(q % 4 + 1) * P], hT[:, cc, :],
                             cc == 0, cc == DC - 1)
            ins.then_inc(done, 1)
            if q:
                turn_block(q - 1)
            if q == 7:
                turn_block(7)

        with pe.Fori(0, 4) as i:
            for q in range(8):
                column_block(i, q, proj_done, z_moved, 0, 0)
        pe.wait_ge(normed, 4)
        for w in range(2):
            for pair in range(PAIRS):
                ins = pe.transpose(PS[:, 6, w * 256 + pair * NS:w * 256 + (pair + 1) * NS],
                                   z[0:NS, 2, w * AW + pair * P:w * AW + (pair + 1) * P], eye[0:NS, 0:NS])
        ins.then_inc(sT_done, 1)
        pe.wait_ge(z_moved, 3 + 24)
        pe.wait_ge(landed[5], 32)
        pe.wait_ge(state_in, 32)

        def windows(g):
            for ch in range(2):
                if g >= 2:
                    pe.wait_ge(d_moved, 2 * (g - 2) + ch + 1)
                u0 = 3 * AW + g * GW + ch * P
                bank = PS[:, 2 * (g % 2) + ch, :]
                mm(bank[:, 0:256], z[:, 0, u0:u0 + P], c_pool[:, g * 256:(g + 1) * 256], True, False)
                mm(bank[:, 128:256], z[:, 1, u0:u0 + P], c_pool[:, 1024 + g * 128:1152 + g * 128], False, True)
                mm(bank[:, 256:288], state[:, g * GW + ch * P:g * GW + (ch + 1) * P],
                   c_pool[0:DEC_B * BUF, 1536 + g * 32:1568 + g * 32], False, False)
                mm(bank[:, 256:288], z[0:NS, 2, u0:u0 + P],
                   c_pool[0:NS, 1664 + g * 32:1696 + g * 32], False, True).then_inc(d_done, 1)

        def group_map(g):
            pe.wait_ge(d_moved, 2 * g + 2)
            for eh in range(2):
                if g:
                    pe.wait_ge(y_moved, 2 * (g - 1) + eh + 1)
                for ch in range(2):
                    ins = mm(PS[:, 4 + eh, 0:TOK], wpool[:, g, ch, eh * P:(eh + 1) * P], dT[:, g % 2, ch, :],
                             ch == 0, ch == 1)
                ins.then_inc(y_done, 1)

        windows(0)
        for g in range(4):
            if g < 3:
                windows(g + 1)
            group_map(g)
        pe.wait_ge(landed[4], 16)
        pe.wait_ge(y_moved, 8)
        pe.wait_ge(sT_moved, 2)
        pe.wait_ge(d_moved, 8)
        with pe.Fori(0, PAIRS) as i:
            pe.wait_ge(stage_ready, i * 3 + 2)
            for w, src in enumerate((st_q, st_k)):
                for c in range(2):
                    ins = pe.transpose(PS[:, 6, (2 * w + c) * P:(2 * w + c + 1) * P], src[:, c, :], eye)
            ins.then_inc(pT, 1)

            def turn_keys(pair):
                b = 2 * (pair % 2)
                if pair == 0:
                    pe.wait_ge(landed[0], i * 16 + 16 * (BASE_AT + 1))
                    pe.wait_ge(ppt_moved, i * 2 + 2)
                elif pair == 1:
                    pe.wait_ge(po_moved, i + 1)
                    pe.wait_ge(diag, i * 2 + 4)
                else:
                    pe.wait_ge(ktn, i * 8 + (pair - 1))
                    pe.wait_ge(ktf, i * 8 + (pair - 1))
                kn = ring[:, 0, :].rearrange("p (j n) -> p j n", j=4)
                kf = ring[:, 1, :].rearrange("p (j n) -> p j n", j=4)
                for j in range(4):
                    ins = pe.transpose(PS[:, b, j * P:(j + 1) * P], kn[:, j, pair * P:(pair + 1) * P], eye)
                ins.then_inc(kt_turned, 1)
                if pair == 0:
                    pe.wait_ge(landed[1], i * 16 + 16 * (BASE_AT + 1))
                for j in range(4):
                    ins = pe.transpose(PS[:, b + 1, j * FAR:(j + 1) * FAR], kf[0:FAR, j, pair * P:(pair + 1) * P],
                                       eye[0:FAR, 0:FAR])
                ins.then_inc(kt_turned, 1)

            def sample_scores(pair):
                q = Qbd[:, pair * 64:pair * 64 + 64]
                first, last = pair == 0, pair == PAIRS - 1
                if first:
                    pe.wait_ge(qbd_ready, i * 2 + 2)
                pe.wait_ge(ktn, i * 8 + (pair + 1))
                mm(PS[0:64, 4, :], q, KT[:, pair % 2, 0:NEAR], first, last)
                pe.wait_ge(ktf, i * 8 + (pair + 1))
                mm(PS[0:64, 5, 0:4 * FAR], q, KT[:, pair % 2, NEAR:NEAR + 4 * FAR], first, last)
                mm(PS[0:64, 5, 4 * FAR:4 * FAR + NS], q, qkTs[:, 1, pair, :], False, last).then_inc(s_pair, 1)

            def prompt_scores(par):
                if par == 0:
                    pe.wait_ge(qk_moved, i * 3 + 3)
                bank = PS[:, 7 - par, :]
                bias = T[:, bass.ds(2 * i + par, 1), :].rearrange("p a n -> p (a n)")
                bias_late = T[:, bass.ds(2 * i + par, 1), 128:256].rearrange("p a n -> p (a n)")
                mm(bank[:, 0:128], qTz[par][:, 0:128], kTp[:, 0:128], True, False)
                mm(bank[:, 0:128], flip, bias_late, False, True)
                mm(bank[:, 128:384], qTz[par][:, 128:256], kTp, True, False)
                mm(bank[:, 128:384], flip, bias, False, True).then_inc(pS, 1)

            for pair in range(PAIRS + 1):
                if pair < PAIRS:
                    turn_keys(pair)
                if pair:
                    sample_scores(pair - 1)
                if pair in (4, 5):
                    prompt_scores(pair - 4)
            for par in range(2):
                pe.wait_ge(p_norm, i * 4 + (2 * par + 2))
                for n in range(3):
                    ins = pe.transpose(PS[:, par, n * P:(n + 1) * P], PP[:, par, n * P:(n + 1) * P], eye)
                ins.then_inc(pPT, 1)
            pe.wait_ge(stage_ready, i * 3 + 3)
            for par in range(2):
                pe.wait_ge(ppt_moved, i * 2 + (par + 3))
                out = PS[64 * par:64 * par + 64, 2, :]
                mm(out[:, 0:256], st_v[:, 0, 64 * par:64 * par + 64], PPT[:, par, 0:256], True, False)
                ins = mm(out[:, 128:256], st_v[:, 1, 64 * par:64 * par + 64], PPT[:, par, 256:384], False, True)
            ins.then_inc(pO, 1)
            pe.wait_ge(const_in, 32)
            pe.wait_ge(s_exp, i + 1)
            for j in range(4):
                pe.transpose(PS[:, 4, j * 64:(j + 1) * 64], SB[:, j * P:(j + 1) * P], eye[0:64, 0:64])
            for j in range(4):
                c0 = NEAR + j * FAR
                pe.transpose(PS[0:FAR, 4, 256 + j * 64:320 + j * 64], SB[:, c0:c0 + FAR], eye[0:64, 0:64])
            pe.transpose(PS[0:NS, 5, 0:64], SB[:, KEYS - NS:KEYS], eye[0:64, 0:64]).then_inc(sPT, 1)
            pe.wait_ge(p_exp, i * 4 + 4)
            pe.wait_ge(pts_n, i * 2 + 2)
            pe.wait_ge(landed[2], i * 16 + 16 * (BASE_AT + 1))
            vn = ring[:, 2, :].rearrange("p (j n) -> p j n", j=4)
            vf = ring[:, 3, :].rearrange("p (j n) -> p j n", j=4)
            for vh in range(2):
                for j in range(4):
                    ins = mm(PS[0:64, 6 + vh, :], PTs[:, j, :], vn[:, j, vh * TILE:(vh + 1) * TILE], j == 0, False)
            ins.then_inc(used[2], 1)
            pe.wait_ge(pts_f, i + 1)
            pe.wait_ge(landed[3], i * 16 + 16 * (BASE_AT + 1))
            for vh in range(2):
                for j in range(4):
                    ins = mm(PS[0:64, 6 + vh, :], PTs[0:FAR, 4 + j, :], vf[0:FAR, j, vh * TILE:(vh + 1) * TILE],
                             False, False)
            ins.then_inc(used[3], 1)
            for vh in range(2):
                ins = mm(PS[0:64, 6 + vh, :], PTs[0:NS, 8, :], z[0:NS, 2, 2 * AW + vh * TILE:2 * AW + (vh + 1) * TILE],
                         False, True)
            ins.then_inc(sO, 1)
            pe.wait_ge(const_in, 32)
            pe.wait_ge(os_a, i + 1)
            pe.wait_ge(os_b, i + 1)
            for pair in range(PAIRS):
                ins = pe.transpose(PS[:, 3, pair * 64:(pair + 1) * 64], OS[:, pair * P:(pair + 1) * P], eye[0:64, 0:64])
            ins.then_inc(sOT, 1)
        pe.wait_ge(po_moved, PAIRS + 1)
        pe.wait_ge(diag, 2 + 2 + 2 * DEC_B)
        def x1_block(c):
            pe.wait_ge(wo_moved, 3 * (c // 4) + 6)
            if c >= 2:
                pe.wait_ge(x1_moved, c - 1)
            for k, (t0, m) in enumerate(CHUNKS):
                ins = pe.transpose(PS[:, 6 + c % 2, t0:t0 + m], z[0:m, k, c * P:(c + 1) * P], eye[0:m, 0:m])
            ins.then_inc(x1_turned, 1)

        def router_block(c):
            pe.wait_ge(x1_moved, c + 1)
            ins = mm(PS[0:20, 5, 0:TOK], wr[:, c, :], x1T[:, c, :], c == 0, c == DC - 1)
            if c == DC - 1:
                ins.then_inc(rl_done, 1)

        for n in range(DC + 6):
            if n < DC:
                column_block(n // 8, n % 8, wo_done, wo_moved, BASE_WO, 4)
            if 5 <= n < DC + 5:
                x1_block(n - 5)
            if n >= 6:
                router_block(n - 6)
        pe.wait_ge(rl_moved, 1)
        for k, (t0, m) in enumerate(CHUNKS):
            ins = pe.transpose(PS[0:m, 6, k * 20:(k + 1) * 20], LG[:, t0:t0 + m], eye[0:20, 0:20])
        ins.then_inc(lgT_done, 1)
        tri, ones = route[:, 0:P], route[:, P:2 * P]
        oh = [R[:, 72 + 4 * k:76 + 4 * k] for k in range(3)]
        pe.wait_ge(oh_ready, 1)
        for n, parts in enumerate((((tri, 0),), ((ones, 0), (tri, 1)), ((ones, 0), (ones, 1), (tri, 2)),
                                   ((ones, 0), (ones, 1), (ones, 2)))):
            for q, (m, k) in enumerate(parts):
                ins = mm(PS[:, 7, 4 * n:4 * n + 4], m, oh[k], q == 0, q == len(parts) - 1)
        ins.then_inc(rank_done, 1)
        def pass_tables(c):
            for what, (sem_in, n_in, col0, n_col) in enumerate(((pm_ready, 3 * c + 3, 160, 8),
                                                                (gates_ready, 1, 232, 20))):
                pe.wait_ge(sem_in, n_in)
                bank = 6 if what == 0 else 5
                for k in range(3):
                    ins = mm(PS[:, bank, 64 + n_col * c:64 + n_col * (c + 1)], Pm[:, c, k, :],
                             R[:, col0 + n_col * k:col0 + n_col * (k + 1)], k == 0, k == 2)
                ins.then_inc(idx_done, 1)

        pass_tables(0)

        def experts(it):
            def up(k, bank, slot0, done):
                for half in range(2):
                    s = slot0 + half
                    pe.wait_ge(landed[s], it * 128 + 16 * (BASE_MOE[s] + k + 1))
                    w = ring[:, s, :].rearrange("p (c n) -> p c n", n=TILE)
                    for c in range(8):
                        cc = half * 8 + c
                        ins = mm(PS[:, bank, :], HTG[k // 4][:, cc, :], w[:, c, :], cc == 0, cc == DC - 1)
                    if half == 0:
                        ins.then_inc(used[s], 1)
                ins.then_inc(done, 1)

            def gate(k):
                if k:
                    pe.wait_ge(sil_ready, it * 8 + k)
                up(k, 0, 4, gate_done)

            def raise_(k):
                if k:
                    pe.wait_ge(hid_ready, it * 8 + k)
                up(k, 1, 0, up_done)

            def turn_hidden(k):
                pe.wait_ge(hid_ready, it * 8 + (k + 1))
                for f in range(4):
                    ins = pe.transpose(PS[:, 2, f * P:(f + 1) * P], HID[:, f * P:(f + 1) * P], eye)
                ins.then_inc(hidT_done, 1)

            def down(k):
                pe.wait_ge(hidT_moved, it * 8 + (k + 1))
                if k % 4 == 0:
                    pe.wait_ge(out_rows, it * 8 + (k + 4))
                for half in range(2):
                    s = 2 + half
                    pe.wait_ge(landed[s], it * 128 + 16 * (BASE_MOE[s] + k + 1))
                    w = ring[:, s, :].rearrange("p (f n) -> p f n", n=D)
                    for f in range(2):
                        ff = half * 2 + f
                        for q in range(4):
                            ins = mm(PS[:, 3 + q, :], HIDT[:, ff, :], w[:, f, q * TILE:(q + 1) * TILE],
                                     k % 4 == 0 and ff == 0, k % 4 == 3 and ff == 3)
                    if half == 0:
                        ins.then_inc(used[s], 1)
                ins.then_inc(down_done, 1)

            def turn_part(j):
                if j % 4 == 0:
                    pe.wait_ge(hn_ready, it * 2 + (j // 4 + 2))
                pe.wait_ge(htg_moved, it * 8 + (j + 4))
                rows_part(7, j % 4)

            for k in range(8):
                if k % 4 == 0:
                    pe.wait_ge(htg_moved, it * 8 + (k + 4))
                gate(k)
                if k:
                    turn_hidden(k - 1)
                if k % 4 == 3:
                    turn_part(k - 1)
                raise_(k)
                if k:
                    down(k - 1)
                if k % 4:
                    turn_part((k - 1, k - 1, k)[k % 4 - 1])
            turn_hidden(7)
            down(7)

        def rows_part(bank, r):
            for q in range(4):
                c = 4 * r + q
                ins = pe.transpose(PS[:, bank, q * P:(q + 1) * P], HN[:, c * P:(c + 1) * P], eye)
            ins.then_inc(htg_turned, 1)

        pe.wait_ge(hn_ready, 1)
        for r, bank in enumerate(FIRST_BANKS):
            rows_part(bank, r)
        for c in range(1, PASSES):
            pass_tables(c)
        pe.wait_ge(idx_ready, 1)
        with pe.Fori(0, 2) as it:
            experts(it)
        most = pe.value_load(pidx[0:1, 28:29], min_val=0, max_val=TOK)
        with pe.If(most > P):
            with pe.Fori(1, PASSES) as c:
                with pe.Fori(0, 2) as j:
                    experts(c * 2 + j)

    @block.vector
    def _(dve):
        steps = Steps(dve, dve_step)
        did, settle = steps.did, steps.settle
        dve.sem_inc(diag, 2)
        dve.sem_inc(wo_moved, 3)
        dve.memset(stat[:, 0:3], 1.0).then_inc(root_in, 1)

        def rms_rows(src, dst, n):
            dve.wait_ge(squares, 3 * n)
            dve.tensor_scalar(stat[:, 4:7], stat[:, 0:3], 1.0 / D, EPS, ALU.mult, ALU.add).then_inc(root_in, 1)
            dve.wait_ge(roots, 1 if n == 1 else 6)
            did(dve.reciprocal(stat[:, 8:11], stat[:, 4:7]))
            settle()
            for k, (t0, m) in enumerate(CHUNKS):
                dve.tensor_scalar(dst[0:m, k, 0:D], src[0:m, k, 0:D], stat[0:m, 8 + k:9 + k], None,
                                  ALU.mult).then_inc(h_rows, 1)

        def columns_out(gain, turned0):
            for n in range(12):
                k, g = n // 4, n % 4
                t0, m = CHUNKS[k]
                dve.wait_ge(h_turned, turned0 + n + 1)
                dve.tensor_tensor(hT[:, 4 * g:4 * g + 4, t0:t0 + m],
                                  PS[:, 6 + n % 2, 0:4 * m].rearrange("p (c t) -> p c t", c=4),
                                  gain[:, 4 * g:4 * g + 4].unsqueeze(2).to_broadcast([P, 4, m]),
                                  ALU.mult).then_inc(h_moved, 1)

        rms_rows(x_rows, x_rows, 1)
        dve.wait_ge(bias_mm, 4)
        dve.tensor_copy(gS[:, :], PS[0:H, 0, 0:384]).then_inc(g_ready, 1)
        dve.wait_ge(g_ready, 1)
        for n, (c0, c1) in enumerate(((0, 512), (512, 896), (896, EC))):
            dve.tensor_tensor(E[:, c0:c1], PS[0:64, 1 + n, 0:c1 - c0], c_mask[:, c0:c1], ALU.add).then_inc(bias_moved, 1)
        dve.memset(Qbd[:, :], 0.0).then_inc(bias_moved, 1)
        columns_out(ln1T, 0)
        for w in range(2):
            dve.wait_ge(z_moved, 9 + 6 * w)
            for part, (m, k0, k1, s0) in enumerate(((P, 0, 2, 16), (NS, 2, 3, 48))):
                nk = k1 - k0
                v = z[0:m, k0:k1, w * AW:(w + 1) * AW]
                tmp = sq_tmp[0:m, 0:nk * AW]
                v4 = v.rearrange("p c (h d) -> p c h d", d=HD)
                sums = stat[0:m, s0:s0 + nk * H]
                did(dve.tensor_tensor(tmp.rearrange("p (c n) -> p c n", n=AW), v, v, ALU.mult))
                settle()
                did(dve.tensor_reduce(sums, tmp.rearrange("p (s d) -> p s d", d=HD), AX.X, ALU.add))
                settle()
                dve.tensor_scalar(sums, sums, 1.0 / HD, EPS, ALU.mult, ALU.add).then_inc(root_in, 1)
                dve.wait_ge(roots, 2 + 2 * w + part)
                did(dve.reciprocal(sums, sums))
                settle()
                did(dve.tensor_tensor(v4, v4, sums.rearrange("p (c h) -> p c h", h=H).unsqueeze(3).to_broadcast(
                    [m, nk, H, HD]), ALU.mult))
                settle()
                dve.tensor_tensor(v4, v4, qkw[0:m, w, :].unsqueeze(1).unsqueeze(1).to_broadcast([m, nk, H, HD]),
                                  ALU.mult).then_inc(normed, 1)
        for g in range(4):
            for ch in range(2):
                dve.wait_ge(d_done, 2 * g + ch + 1)
                if g >= 2:
                    dve.wait_ge(y_done, 2 * (g - 1))
                dve.tensor_copy(dT[:, g % 2, ch, :], PS[:, 2 * (g % 2) + ch, 0:TOK]).then_inc(d_moved, 1)
        for par in range(2):
            other = slice(64 - 64 * par, 128 - 64 * par)
            dve.memset(qTz[par][other], 0.0).then_inc(diag, 1)
        dve.wait_ge(y_done, 8)
        dve.wait_ge(sT_moved, 2)
        with dve.Fori(0, PAIRS) as i:
            steps.begin(i, 7)
            dve.wait_ge(s_pair, i * 8 + 2)
            for par in range(2):
                r = slice(64 * par, 64 * par + 64)
                dve.tensor_copy(Qbd[r, :].rearrange("p (a n) -> p a n", n=65)[:, :, 8 * par:8 * par + 49:16],
                                qkTs[r, 0, :, bass.ds(i * 4, 4)]).then_inc(qbd_ready, 1)

            def keys_out(pair):
                dve.wait_ge(kt_turned, i * 16 + (2 * pair + 2))
                dve.wait_ge(s_pair, i * 8 + (pair + 1))
                dve.tensor_copy(KT[:, pair % 2, NEAR:NEAR + 4 * FAR],
                                PS[:, 2 * (pair % 2) + 1, 0:4 * FAR]).then_inc(ktf, 1)

            def prompt_max(par):
                dve.wait_ge(pS, i * 2 + (par + 1))
                for q, (c0, c1) in enumerate(((0, 128), (128, 384))):
                    did(dve.tensor_reduce(stat[:, 84 + 2 * par + q:85 + 2 * par + q], PS[:, 7 - par, c0:c1],
                                          AX.X, ALU.max))
                settle()
                dve.tensor_scalar(stat[:, 68 + 4 * par:70 + 4 * par], stat[:, 84 + 2 * par:86 + 2 * par], -1.0, None,
                                  ALU.mult).then_inc(p_negmax, 1)

            def prompt_norm(par):
                dve.wait_ge(p_exp, i * 4 + (2 * par + 2))
                did(dve.reciprocal(stat[:, 88 + 2 * par:90 + 2 * par], stat[:, 76 + 4 * par:78 + 4 * par]))
                settle()
                for q, (c0, c1) in enumerate(((0, 128), (128, 384))):
                    dve.tensor_scalar(PP[:, par, c0:c1], PP[:, par, c0:c1], stat[:, 88 + 2 * par + q:89 + 2 * par + q],
                                      None, ALU.mult).then_inc(p_norm, 1)

            for pair in range(5):
                keys_out(pair)
            prompt_max(0)
            keys_out(5)
            prompt_max(1)
            keys_out(6)
            prompt_norm(0)
            keys_out(7)
            prompt_norm(1)
            dve.wait_ge(s_pair, i * 8 + 10)
            dve.tensor_tensor(SB[:, 0:NEAR], PS[0:64, 4, :], E[:, 0:NEAR], ALU.add).then_inc(s_sum, 1)
            dve.tensor_tensor(SB[:, NEAR:KEYS - NS], PS[0:64, 5, 0:4 * FAR], E[:, NEAR:KEYS - NS],
                              ALU.add).then_inc(s_sum, 1)
            dve.tensor_tensor(SB[:, KEYS - NS:KEYS], PS[0:64, 5, 4 * FAR:4 * FAR + NS],
                              E[:, bass.ds(i * NS + (KEYS - NS), NS)], ALU.add).then_inc(s_sum, 1)
            dve.wait_ge(s_sum, i * 3 + 3)
            did(dve.tensor_reduce(stat[0:64, 64:65], SB, AX.X, ALU.max))
            settle()
            dve.tensor_scalar(stat[0:64, 65:66], stat[0:64, 64:65], -1.0, None, ALU.mult).then_inc(s_negmax, 1)
            dve.wait_ge(s_exp, i + 1)
            dve.reciprocal(stat[0:64, 67:68], stat[0:64, 66:67]).then_inc(s_inv, 1)
            dve.wait_ge(sPT, i + 1)
            dve.tensor_copy(PTs[0:NS, 8, :], PS[0:NS, 5, 0:64]).then_inc(pts_f, 1)
            dve.wait_ge(sO, i + 1)
            dve.wait_ge(s_inv, i + 1)
            dve.tensor_scalar(OS[:, TILE:2 * TILE], PS[0:64, 7, :], stat[0:64, 67:68], None, ALU.mult).then_inc(os_b, 1)
            dve.wait_ge(sOT, i + 1)
            for par in range(2):
                r = slice(64 * par, 64 * par + 64)
                blocks = PS[r, 3:5, :].rearrange("p a n -> p (a n)")[:, 0:520].rearrange(
                    "p (a n) -> p a n", n=65)[:, :, 8 * par:8 * par + 49:16]
                dve.tensor_copy(hT[r, 0:PAIRS, bass.ds(i * 4 + SEQ, 4)], blocks).then_inc(diag, 1)
        steps.end(PAIRS)
        dve.wait_ge(x_again, 32)

        dve.memset(stat[:, 96:108], 1.0).then_inc(root_in, 1)
        for n in range(DC + 5):
            if n in (4, 8, 12, 16):
                t = n // 4 - 1
                dve.wait_ge(zT_turned, 32 + 4 * t + 6)
                for k, (t0, m) in enumerate(CHUNKS):
                    xt = z[0:m, k, t * TILE:(t + 1) * TILE]
                    dve.tensor_tensor(xt, PS[0:m, 2 + k, :], xt, ALU.add).then_inc(wo_moved, 1)
            if n >= 5:
                c = n - 5
                dve.wait_ge(x1_turned, c + 1)
                dve.tensor_scalar(x1T[:, c, :], PS[:, 6 + c % 2, 0:TOK], ln2T[:, c:c + 1], None,
                                  ALU.mult).then_inc(x1_moved, 1)
        dve.wait_ge(squares, 3 + 12)
        did(dve.tensor_reduce(stat[:, 0:3], stat[:, 96:108].rearrange("p (k t) -> p k t", t=4), AX.X, ALU.add))
        settle()
        dve.tensor_scalar(stat[:, 4:7], stat[:, 0:3], 1.0 / D, EPS, ALU.mult, ALU.add).then_inc(root_in, 1)
        dve.wait_ge(route_in, 16)

        def step(ins):
            did(ins)
            settle()

        step(dve.memset(R, 0.0))
        dve.wait_ge(roots, 6)
        step(dve.reciprocal(stat[:, 8:11], stat[:, 4:7]))

        def col(c, n=1):
            return R[:, c:c + 3 * n].rearrange("p (k n) -> p k n", n=n)

        dve.wait_ge(lgT_done, 1)
        L = col(0, 20)
        for k, (t0, m) in enumerate(CHUNKS):
            did(dve.scalar_tensor_tensor(L[0:m, k, :], PS[0:m, 6, 20 * k:20 * k + 20], stat[0:m, 8 + k:9 + k],
                                         rb[0:m], ALU.mult, ALU.add))
        settle()
        lg, le = L[:, :, 0:4], L[:, :, 4:20]
        expg, oh, leg, top, work, m1, m2 = col(60, 4), col(72, 4), col(84, 4), col(96, 4), col(108, 4), col(120), col(123)
        best, tmp3, ge, gate4 = col(126), col(129), col(132), col(136, 4)
        valid = route[:, 5 * P + 3:5 * P + 6].unsqueeze(2)
        tokens = route[:, 5 * P:5 * P + 3].unsqueeze(2)
        order = route[:, 5 * P + 9:5 * P + 13].unsqueeze(1).to_broadcast([P, 3, 4])
        spare = route[:, 5 * P + 6:5 * P + 9]

        def wide(v):
            return v.to_broadcast([P, 3, 4])

        def first_of(dst, src, most):
            step(dve.tensor_tensor(dst, src, wide(most), ALU.is_equal))
            step(dve.tensor_tensor(dst, dst, order, ALU.mult))
            step(dve.tensor_reduce(best, dst, AX.X, ALU.max))
            step(dve.tensor_tensor(dst, dst, wide(best), ALU.is_equal))

        step(dve.tensor_reduce(m1, lg, AX.X, ALU.max))
        first_of(oh, lg, m1)
        dve.tensor_tensor(oh, oh, valid.to_broadcast([P, 3, 4]), ALU.mult).then_inc(oh_ready, 1)
        dve.tensor_tensor(expg, lg, wide(m1), ALU.subtract).then_inc(exp_in, 1)
        rank, pos = col(148, 4), col(220)
        rh = R[:, 160:184].rearrange("p (k n) -> p k n", n=8)
        dve.wait_ge(oh_ready, 1)
        did(dve.tensor_tensor(rh[:, :, 0:4], oh, tokens.to_broadcast([P, 3, 4]), ALU.mult))
        did(dve.tensor_copy(rh[:, :, 4:8], oh))
        dve.wait_ge(rank_done, 1)
        step(dve.tensor_tensor(rank, PS[:, 7, 0:12].rearrange("p (k n) -> p k n", n=4), oh, ALU.mult))
        did(dve.tensor_reduce(R[:, 224:225], PS[:, 7, 12:16], AX.X, ALU.max))
        step(dve.tensor_reduce(pos, rank, AX.X, ALU.add))

        def slots(c):
            for k in range(3):
                dve.tensor_scalar(Pm[:, c, k, :], route[:, (2 + c) * P:(3 + c) * P], R[:, 220 + k:221 + k], None,
                                  ALU.is_equal).then_inc(pm_ready, 1)

        def rows_of(c):
            got, miss = R[:, 184 + 8 * c:192 + 8 * c], R[:, 208 + 4 * c:212 + 4 * c]
            step(dve.tensor_copy(got, PS[:, 6, 64 + 8 * c:72 + 8 * c]))
            step(dve.tensor_scalar(miss, got[:, 4:8], -1.0, 1.0, ALU.mult, ALU.add))
            step(dve.tensor_scalar(miss, miss, spare[:, 0:1], None, ALU.mult))
            step(dve.tensor_tensor(miss, miss, got[:, 0:4], ALU.add))
            step(dve.tensor_copy(pidx[:, 14 + 4 * c:18 + 4 * c], miss))
            dve.tensor_copy(pidx[:, 4 * c:4 * c + 4], got[:, 0:4]).then_inc(rows_ready, 1)

        slots(0)
        step(dve.memset(pidx[:, 12:14], 0))
        step(dve.memset(GT, 0.0))
        dve.wait_ge(idx_done, 1)
        rows_of(0)
        step(dve.tensor_tensor(leg, le[:, :, 0:4], wide(oh[:, :, 0:1]), ALU.mult))
        for g in range(1, 4):
            step(dve.tensor_tensor(work, le[:, :, 4 * g:4 * g + 4], wide(oh[:, :, g:g + 1]), ALU.mult))
            step(dve.tensor_tensor(leg, leg, work, ALU.add))
        step(dve.tensor_reduce(m1, leg, AX.X, ALU.max))
        first_of(top, leg, m1)
        step(dve.tensor_scalar(work, top, NEG, None, ALU.mult))
        step(dve.tensor_tensor(leg, leg, work, ALU.add))
        step(dve.tensor_reduce(m2, leg, AX.X, ALU.max))
        first_of(work, leg, m2)
        dve.tensor_tensor(ge, m2, m1, ALU.subtract).then_inc(exp_in, 1)
        dve.wait_ge(expd, 2)
        step(dve.tensor_reduce(m1, expg, AX.X, ALU.add))
        step(dve.tensor_scalar(tmp3, ge, 1.0, None, ALU.add))
        step(dve.tensor_tensor(m1, m1, tmp3, ALU.mult))
        step(dve.reciprocal(m1, m1))
        step(dve.tensor_tensor(m2, m1, ge, ALU.mult))
        step(dve.tensor_tensor(gate4, top, wide(m1), ALU.mult))
        step(dve.tensor_tensor(work, work, wide(m2), ALU.mult))
        step(dve.tensor_tensor(gate4, gate4, work, ALU.add))
        rg = R[:, 232:292].rearrange("p (k g v) -> p k g v", g=NG, v=GV)
        for g in range(NG):
            did(dve.tensor_tensor(rg[:, :, g, 0:4], gate4, wide(oh[:, :, g:g + 1]), ALU.mult))
        dve.tensor_tensor(rg[:, :, :, 4], oh, wide(stat[:, 8:11].unsqueeze(2)), ALU.mult).then_inc(rms_in, 1)
        dve.wait_ge(rms_in, 1)
        settle()
        dve.memset(stat[:, 110:111], 0.0).then_inc(gates_ready, 1)

        def gates_of(c):
            dve.wait_ge(idx_done, 2 * c + 2)
            step(dve.tensor_copy(gates[:, 20 * c:20 * c + 20], PS[:, 5, 64 + 20 * c:84 + 20 * c]))

        gates_of(0)
        dve.sem_inc(out_rows, 4)

        def rows_in(it, n, ahead):
            dve.wait_ge(gathered[n], it * 16 + 16 * (ahead + 1))
            dve.wait_ge(htg_turned, it * 8 + 4 * (n + 2 * ahead))
            scaled_rows(n, it * 2 + (n + 2 * ahead), it * 2 + (n + 2 * ahead + 1))

        def scaled_rows(n, group, nth):
            dve.tensor_copy(GS[n].unsqueeze(1), GT[:, bass.ds(group, 1), :]).then_inc(gs_ready, 1)
            dve.wait_ge(gs_ready, nth)
            dve.tensor_scalar(HN, XG[n], GS[n][:, 4:5], None, ALU.mult).then_inc(hn_ready, 1)

        def quarter_out(n, r, bank):
            dve.tensor_tensor(HTG[n][:, 4 * r:4 * r + 4, :], PS[:, bank, :].rearrange("p (c t) -> p c t", c=4),
                              ln2T[:, 4 * r:4 * r + 4].unsqueeze(2).to_broadcast([P, 4, P]),
                              ALU.mult).then_inc(htg_moved, 1)

        dve.wait_ge(gathered[0], 16)
        scaled_rows(0, 0, 1)
        for r, bank in enumerate(FIRST_BANKS):
            dve.wait_ge(htg_turned, r + 1)
            quarter_out(0, r, bank)
        for c in range(1, PASSES):
            slots(c)
            dve.wait_ge(idx_done, 2 * c + 1)
            rows_of(c)
            gates_of(c)
        dve.tensor_copy(pidx[:, 28:29], R[:, 224:225]).then_inc(idx_ready, 1)
        dve.wait_ge(idx_ready, 1)

        def experts(it):
            def turned_out(j):
                dve.wait_ge(htg_turned, it * 8 + (j + 5))
                quarter_out(1 - j // 4, j % 4, 7)

            def hidden(k):
                dve.wait_ge(sil_ready, it * 8 + (k + 1))
                dve.wait_ge(up_done, it * 8 + (k + 2))
                if k:
                    dve.wait_ge(hidT_done, it * 8 + k)
                dve.scalar_tensor_tensor(HID, SIL, GS[k // 4][:, k % 4:k % 4 + 1], PS[:, 1, :],
                                         ALU.mult, ALU.mult).then_inc(hid_ready, 1)

            def rows_out(n):
                dve.wait_ge(down_done, it * 8 + (4 * n + 5))
                for q in range(4):
                    v = XG[n][:, q * TILE:(q + 1) * TILE]
                    dve.tensor_tensor(v, PS[:, 3 + q, :], v, ALU.add).then_inc(out_rows, 1)

            rows_in(it, 1, 0)
            for k in range(8):
                if k % 4 == 3:
                    turned_out(k - 1)
                hidden(k)
                if k == 4:
                    rows_out(0)
                if k % 4:
                    if k == 5:
                        rows_in(it, 0, 1)
                    turned_out((k - 1, k - 1, k)[k % 4 - 1])
            rows_out(1)

        with dve.Fori(0, 2) as it:
            experts(it)
        most = dve.value_load(pidx[0:1, 28:29], min_val=0, max_val=TOK)
        with dve.If(most > P):
            with dve.Fori(1, PASSES) as c:
                with dve.Fori(0, 2) as j:
                    experts(c * 2 + j)


_OUTS = [("y", (TOK + P, D)), ("k_prompt", (1, 1, SEQ, H, HD)), ("v_prompt", (1, 1, SEQ, H, HD)),
         ("pool_prompt", (1, 1, BUF, PW)), ("k_sample", (1, DEC_B, DEC_T, H, HD)),
         ("v_sample", (1, DEC_B, DEC_T, H, HD)), ("pool_sample", (1, DEC_B, BUF, PW))]


def small_inputs(i):
    s = np.zeros((P, 588), np.float32)
    s[:, 0:16] = i["ln1_w"][0].reshape(DC, P).T
    s[:, 16:32] = i["ln2_w"][0].reshape(DC, P).T
    s[:, 32:96] = i["q_norm_w"][0][None]
    s[:, 96:160] = i["k_norm_w"][0][None]
    s[:, 160:168] = i["pool_scale"][0].reshape(8, P).T
    s[:, 168:488].reshape(P, DC, 20)[:, :, 0:4] = i["w_router_group"][0].reshape(DC, P, 4).transpose(1, 0, 2)
    s[:, 168:488].reshape(P, DC, 20)[:, :, 4:20] = i["w_router_expert"][0].reshape(DC, P, 16).transpose(1, 0, 2)
    s[:, 488:492] = i["b_router_group"][0][None]
    s[:, 492:508] = i["b_router_expert"][0][None]
    rel = i["rel_bias"]
    for t in range(4):
        s[32 * t:32 * t + 32, 508 + 16 * t:524 + 16 * t] = rel.reshape(NB, 8, 2).transpose(0, 2, 1).reshape(NB, 16)
    s[0:32, 572:588] = rel
    s[32, 572:588] = 1.0
    return s


def kernel(**inputs):
    import concourse.bacc as _bacc
    from concourse.bass_utils import run_bass_kernel_spmd as _run

    inputs = {k: np.asarray(v) for k, v in inputs.items()}
    nc = _bacc.Bacc("TRN2", target_bir_lowering=False, num_devices=1)
    arrays, a, o = {}, {}, {}
    given = {n: inputs[n] for n in ("x_prompt", "x_sample", "cache_k", "cache_v", "state_pool", "w_in", "w_pool",
                                    "w_o", "w_gate", "w_up", "w_down")}
    given["small"] = small_inputs(inputs)
    given.update(shape_constants())
    for name, v in given.items():
        v = np.ascontiguousarray(v)
        arrays[f"in_{name}"] = v
        a[name] = nc.dram_tensor(f"in_{name}", v.shape, mybir.dt.from_np(v.dtype), kind="ExternalInput").ap()
    for name, shape in _OUTS:
        o[name] = nc.dram_tensor(f"out_{name}", shape, F32, kind="ExternalOutput").ap()
    hybrid_layer(nc, a, o)
    r = _run(nc, [arrays], core_ids=[0]).results[0]
    y = r["out_y"]
    return (y[0:SEQ].reshape(1, SEQ, D), y[SEQ:TOK].reshape(DEC_B, DEC_T, D),
            r["out_k_prompt"], r["out_v_prompt"], r["out_pool_prompt"],
            r["out_k_sample"], r["out_v_sample"], r["out_pool_sample"])
```

```python
from contextlib import ExitStack
import math

import numpy as np

import concourse.bass as bass
from concourse import mybir
from concourse.alu_op_type import AluOpType as ALU

F32 = mybir.dt.float32
I32 = mybir.dt.int32
BF16 = mybir.dt.bfloat16
ACT = mybir.ActivationFunctionType
AX = mybir.AxisListType

P = 128
D = 2048
DC = D // P
SEQ, DEC_B, DEC_T, PAST = 256, 8, 4, 2048
NS = DEC_B * DEC_T
TOK = SEQ + NS
CHUNKS = [(0, 128), (128, 128), (256, 32)]
H, HD = 16, 64
PAIRS = H // 2
AW = H * HD
PW = D - AW
IN_W = 3 * AW + PW
TILE = 512
POOL_W = (2, 4, 8, 16)
BUF = 15
GW = PW // 4
NB = 32
EPS = 1e-6
SCALE = HD ** -0.5
NEG = -1e30
FE = 512
NG, EPG = 4, 4
NE = NG * EPG
SLOTS = 6
SLOT = 4096
NEAR = 128
MID = 96
FAR = 96
GV = 5
KEYS = NEAR + MID + FAR + NS
PASSES = 3


def counted(dist):
    d = np.asarray(dist)
    n = ((d <= 128).astype(int) + ((d <= 512) & (d % 4 == 0)) + ((d <= 2048) & (d % 16 == 0)))
    return np.where(d >= 0, n, 0)


def bucket(dist):
    d = np.maximum(np.asarray(dist), 1)
    df = d.astype(np.float32)
    large = 16 + (np.log(df / np.float32(16)) / np.float32(math.log(2048 / 16)) * np.float32(16)).astype(np.int32)
    return np.where(np.asarray(dist) < 16, np.maximum(dist, 0), np.minimum(large, NB - 1))


def log_count(dist):
    n = counted(dist)
    return np.where(n > 0, np.log(np.maximum(n, 1)), NEG).astype(np.float32)


def shape_constants():
    out = {}
    y = np.arange(384)
    dist = 255 - y
    one = np.zeros((33, 384), np.float32)
    one[np.clip(bucket(dist), 0, NB - 1), y] = 1.0
    one[32] = log_count(dist)
    cols = KEYS - NS + DEC_B * NS
    hot = np.zeros((4, NB, cols), np.float32)
    mask = np.full((4, 16, cols), NEG, np.float32)
    for t in range(4):
        near = NEAR + t - np.arange(NEAR)
        mid = 512 - 4 * np.arange(MID)
        far = PAST - 16 * np.arange(FAR)
        new = np.array([[t - k % 4 if k // 4 == b else -1 for k in range(NS)] for b in range(DEC_B)]).ravel()
        d = np.concatenate([near, mid, far, new])
        hot[t, np.clip(bucket(d), 0, NB - 1), np.arange(cols)] = 1.0
        mask[t] = log_count(d)[None]
    bias = np.zeros((P, 384 + 2 * cols), np.float32)
    bias[:33, :384] = one
    bias[:, 384:384 + cols] = hot.reshape(P, cols)
    bias[:64, 384 + cols:] = mask.reshape(64, cols)
    out["c_bias"] = bias
    rows, l = np.arange(SEQ)[:, None], np.arange(SEQ)[None]
    pool = np.zeros((P, 4 * 256 + 4 * 128 + 2 * 4 * 32), np.float32)
    for g, w in enumerate(POOL_W):
        full = ((rows <= l) & (rows > l - w)) / np.minimum(l + 1, w) - (rows == l)
        pool[:, g * 256:(g + 1) * 256] = full[:128]
        pool[:, 1024 + g * 128:1024 + (g + 1) * 128] = full[128:, 128:]
        for b in range(DEC_B):
            for t in range(DEC_T):
                at = BUF + t
                for r in range(at - w + 1, at + 1):
                    if r < BUF:
                        pool[b * BUF + r, 1536 + g * 32 + b * 4 + t] = 1.0 / w
                    else:
                        pool[b * 4 + r - BUF, 1664 + g * 32 + b * 4 + t] = 1.0 / w
                pool[b * 4 + t, 1664 + g * 32 + b * 4 + t] -= 1.0
    out["c_pool"] = pool
    eye = np.eye(P, dtype=np.float32)
    out["c_eye"] = np.concatenate([eye, eye[::-1]], axis=1).copy()
    r = np.zeros((P, 2 * P + 3 * P + 3 + 3 + 3 + 4), np.float32)
    r[:, 5 * P + 9:] = [4, 3, 2, 1]
    r[:, :P] = np.triu(np.ones((P, P), np.float32), 1)
    r[:, P:2 * P] = 1.0
    r[:, 2 * P:5 * P] = np.arange(3 * P)[None]
    for k, (t0, n) in enumerate(CHUNKS):
        r[:, 5 * P + k] = t0 + np.arange(P)
        r[:n, 5 * P + 3 + k] = 1.0
        r[:, 5 * P + 6 + k] = TOK + np.arange(P)
    out["c_route"] = r
    return out


class Steps:

    def __init__(self, eng, sem):
        self.eng, self.sem, self.n = eng, sem, 0
        self.turn = None

    def did(self, ins):
        ins.then_inc(self.sem, 1)
        self.n += 1

    def settle(self):
        self.eng.wait_ge(self.sem, self.n if self.turn is None else self.turn + self.n)

    def begin(self, turn, per):
        self.outer, self.per = self.n, per
        self.turn, self.n = turn * per, self.n

    def end(self, turns):
        assert self.n - self.outer == self.per, (self.n - self.outer, self.per)
        self.turn, self.n = None, self.outer + self.per * turns


def hybrid_layer(nc, a, o):
    ctx = ExitStack()
    with ctx:
        build(nc, a, o, ctx)


def build(nc, a, o, ctx):
    def sb(name, shape, dt=F32):
        return ctx.enter_context(nc.sbuf_tensor(name, shape, dt))

    def sem(name):
        return ctx.enter_context(nc.semaphore(name))

    ring = sb("ring", [P, SLOTS, SLOT])
    HT = sb("HT", [P, DC * TOK])
    X = sb("X", [P, 3 * D])
    Z = sb("Z", [P, 3 * IN_W])
    eye2 = sb("eye2", [P, 2 * P])
    small = sb("small", [P, 16 + 16 + 128 + 8 + 16 * 20 + 20 + 64 + 16])
    E = sb("E", [64, KEYS - NS + DEC_B * NS])
    Qbd = sb("Qbd", [P, 520])
    qTs = sb("qTs", [P, PAIRS, NS])
    stage = sb("stage", [P, 6, 256])
    ranks = sb("ranks", [P, 2 * P + 12], BF16)
    sf = sb("sf", [MID, 128])
    stat = sb("stat", [P, 160])
    pidx = sb("pidx", [P, 40], I32)
    gS = sb("gS", [H, 384])
    gates = sb("gates", [P, 80])
    PS = ctx.enter_context(nc.psum_tensor("PS", [P, 8, TILE], F32))

    hT = HT[:, :].rearrange("p (c t) -> p c t", t=TOK)
    x_rows = X[:, :].rearrange("p (c d) -> p c d", d=D)
    z = Z[:, :].rearrange("p (c n) -> p c n", n=IN_W)
    eye, flip = eye2[:, 0:P], eye2[:, P:2 * P]
    ln1T, ln2T = small[:, 0:16], small[:, 16:32]
    qkw = small[:, 32:160].rearrange("p (w d) -> p w d", d=HD)
    pscale = small[:, 160:168]
    wr = small[:, 168:488].rearrange("p (c n) -> p c n", n=20)
    rb = small[:, 488:508]
    relS = small[:, 508:572]
    relP = small[0:33, 572:588]

    sq_tmp = X[:, 0:2048]
    state = X[0:DEC_B * BUF, 2048:3072]
    dT = X[:, 3072:3072 + 4 * TOK].rearrange("p (b c t) -> p b c t", b=2, t=TOK)
    KT = X[:, 0:1280].rearrange("p (a n) -> p a n", n=NEAR + NS)
    SB = X[0:64, 1280:1280 + KEYS]
    SB_strided = X[0:64, 1280 + NEAR:1280 + NEAR + 2 * P].rearrange("p (a n) -> p a n", n=P)[:, :, 0:MID]
    SB_new = SB[:, NEAR + MID:NEAR + MID + NS]
    PTn = X[:, 1664:1728]
    PTb = [X[:, 1760 + 320 * n:2080 + 320 * n] for n in range(2)]
    SF = [sf[0:MID, 64 * n:64 * n + 64] for n in range(2)]
    OS = X[0:64, 3296:4320]
    PP = X[:, 4320:5088].rearrange("p (b n) -> p b n", b=2)
    PPT = X[:, 5088:5856].rearrange("p (b n) -> p b n", b=2)
    st_q, st_k, st_v = (stage[:, n, :].rearrange("p (c n) -> p c n", c=2) for n in range(3))
    qTz = [stage[:, 3, :], stage[:, 4, :]]
    kTp = stage[:, 5, :]
    zTs = stage[:, :, :].rearrange("p a b -> p (a b)")[:, 0:2 * TOK].rearrange("p (b t) -> p b t", b=2)
    near_k, near_v = z[:, 0, 3 * AW:IN_W], z[:, 1, 3 * AW:IN_W]
    T = ring[:, 4, :].rearrange("p (h n) -> p h n", h=H)
    EC = KEYS - NS + DEC_B * NS
    c_one = ring[0:33, 5, 0:384]
    c_hot = ring[:, 5, 384:384 + EC]
    c_mask = ring[0:64, 5, 384 + EC:384 + 2 * EC]
    c_pool = ring[:, 5, 0:1792]
    wpool = ring[:, 5, 1792:3840].rearrange("p (g c e) -> p g c e", g=4, c=2)
    x1T = X[:, 0:DC * TOK].rearrange("p (c t) -> p c t", t=TOK)
    route = X[:, 4608:4608 + 653]
    R = X[:, 5264:5264 + 460]
    LG = X[0:20, 5728:5728 + TOK]
    Pm = Z[:, 2048:3200].rearrange("p (c k n) -> p c k n", c=3, k=3)
    GT = gates[:, 0:70].rearrange("p (n v) -> p n v", v=GV)
    GS = [gates[:, 70 + GV * n:70 + GV * (n + 1)] for n in range(2)]
    HTG = [HT[:, n * 2048:(n + 1) * 2048].rearrange("p (c t) -> p c t", t=P) for n in range(2)]
    XG = [X[:, n * D:(n + 1) * D] for n in range(2)]
    HN = Z[:, 0:2048]
    SIL, HID = Z[:, 3200:3712], Z[:, 3712:4224]
    HIDT = Z[:, 4224:4736].rearrange("p (f t) -> p f t", t=P)

    g_scr = nc.dram_tensor("g_scr", (H, 384), F32).ap()
    q_scr = nc.dram_tensor("q_scr", (NS, AW), F32).ap()
    x1_scr = nc.dram_tensor("x1_scr", (TOK, D), F32).ap()

    landed = [sem(f"landed{s}") for s in range(SLOTS)]
    used = [sem(f"used{s}") for s in range(SLOTS)]
    x_in = [sem(f"x_in{k}") for k in range(3)]
    const_in, state_in = sem("const_in"), sem("state_in")
    g_stored, x_again, route_in, x1_stored = sem("g_stored"), sem("x_again"), sem("route_in"), sem("x1_stored")
    stored, pstored = sem("stored"), sem("pstored")
    dve_step = sem("dve_step")
    squares, root_in, roots = sem("squares"), sem("root_in"), sem("roots")
    h_turned, h_moved = sem("h_turned"), sem("h_moved")
    rms_ready, h_rows = sem("rms_ready"), [sem(f"h_rows{k}") for k in range(3)]
    bias_mm, bias_moved, g_ready = sem("bias_mm"), sem("bias_moved"), sem("g_ready")
    proj_done, z_moved, zT_moved, zT_turned = (sem(n) for n in ("proj_done", "z_moved", "zT_moved", "zT_turned"))
    normed = sem("normed")
    sT_done, sT_moved = sem("sT_done"), sem("sT_moved")
    d_done, d_moved, d_late_moved, y_done, y_moved = (
        sem(n) for n in ("d_done", "d_moved", "d_late_moved", "y_done", "y_moved"))
    stage_ready = sem("stage_ready")
    pT, kt_turned, s_done = sem("pT"), sem("kt_turned"), sem("s_done")
    q_stored, near_in, near_v_in, near_v_used = sem("q_stored"), sem("near_in"), sem("near_v_in"), sem("near_v_used")
    mid_done, far_done, sf_turned, pads_ready = sem("mid_done"), sem("far_done"), sem("sf_turned"), sem("pads_ready")
    p_inv, new_v_in, down_part, tables_in = sem("p_inv"), sem("new_v_in"), sem("down_part"), sem("tables_in")
    pS, pPT, pO, sPT, sOT = (sem(n) for n in ("pS", "pPT", "pO", "sPT", "sOT"))
    qk_moved, ktn, p_exp, ppt_moved = (sem(n) for n in ("qk_moved", "ktn", "p_exp", "ppt_moved"))
    s_exp, pts_moved, os_moved, po_moved = (sem(n) for n in ("s_exp", "pts_moved", "os_moved", "po_moved"))
    qbd_ready, p_negmax, p_norm, s_negmax, s_inv, diag = (
        sem(n) for n in ("qbd_ready", "p_negmax", "p_norm", "s_negmax", "s_inv", "diag"))
    wo_done, wo_moved, s_sum = sem("wo_done"), sem("wo_moved"), sem("s_sum")
    rl_done, rl_moved, lgT_done, expd = sem("rl_done"), sem("rl_moved"), sem("lgT_done"), sem("expd")
    exp_in, oh_ready, rank_done, pm_ready, idx_done, idx_ready, gates_ready = (
        sem(n) for n in ("exp_in", "oh_ready", "rank_done", "pm_ready", "idx_done", "idx_ready", "gates_ready"))
    idx_copied, pool_turn, rows_ready = sem("idx_copied"), sem("pool_turn"), sem("rows_ready")
    x1_turned, x1_moved = sem("x1_turned"), sem("x1_moved")
    gathered = [sem(f"gathered{n}") for n in range(2)]
    scattered = [sem(f"scattered{n}") for n in range(2)]
    hn_ready, htg_turned, htg_moved, gs_ready = (
        sem(n) for n in ("hn_ready", "htg_turned", "htg_moved", "gs_ready"))
    gate_done, up_done, sil_ready, hid_ready = sem("gate_done"), sem("up_done"), sem("sil_ready"), sem("hid_ready")
    hidT_done, hidT_moved, down_done, out_rows = sem("hidT_done"), sem("hidT_moved"), sem("down_done"), sem("out_rows")

    w_in_t = a["w_in"][0].rearrange("(c p) n -> p c n", p=P)
    w_o_t = a["w_o"][0].rearrange("(c p) n -> p c n", p=P)
    xp_t = a["x_prompt"][0].rearrange("(c p) d -> p c d", p=P)
    xs_t = a["x_sample"].rearrange("b t d -> (b t) d")

    def load_columns(sp, w_t, col, par):
        for half in range(2):
            s = 2 * par + half
            sp.dma_start(ring[:, s, :].rearrange("p (c n) -> p c n", n=TILE),
                         w_t[:, half * 8:half * 8 + 8, bass.ds(col, TILE)]).then_inc(landed[s], 16)

    TURN_BANKS = (6, 7, 0, 1)
    FIRST_BANKS = (7, 0, 1, 2)
    block = ctx.enter_context(nc.Block())

    BASE_AT = [4, 4, 5, 4]
    BASE_WO = [n + DEC_B for n in BASE_AT]
    BASE_MOE = [n + 2 for n in BASE_WO] + [1, 2 + DEC_B - 1]

    @block.sync
    def _(sp):
        sp.dma_start(x_rows[:, 0, :], xp_t[:, 0, :]).then_inc(x_in[0], 16)
        sp.dma_start(x_rows[0:NS, 2, :], xs_t).then_inc(x_in[2], 16)
        sp.dma_start(x_rows[:, 1, :], xp_t[:, 1, :]).then_inc(x_in[1], 16)
        sp.dma_start(ring[:, 5, 0:384 + 2 * EC], a["c_bias"]).then_inc(landed[5], 16)
        for par in range(2):
            load_columns(sp, w_in_t, par * TILE, par)
        with sp.Fori(1, 4) as i:
            for par in range(2):
                sp.wait_ge(proj_done, 8 * i + (4 * par - 4))
                load_columns(sp, w_in_t, (2 * i + par) * TILE, par)
        sp.wait_ge(bias_moved, 3)
        sp.dma_start(ring[:, 5, 0:1792], a["c_pool"]).then_inc(landed[5], 16)
        sp.dma_start(ring[:, 5, 1792:3840].rearrange("p (g c e) -> p g c e", g=4, c=2),
                     a["w_pool"][0].rearrange("g (c p) e -> p g c e", p=P)).then_inc(state_in, 16)
        sp.wait_ge(h_turned, 12)
        sp.dma_start(state, a["state_pool"][0].rearrange("b r n -> (b r) n")).then_inc(state_in, 16)

        def keys_in(s, i, slot=None):
            slot = s if slot is None else slot
            rows = a["cache_k" if s < 2 else "cache_v"][0, bass.ds(i, 1)]
            if s % 2 == 0:
                sp.dma_start(ring[0:MID, slot, :], rows[:, PAST - 512:PAST - NEAR].rearrange(
                    "a (p j) h d -> p (a j h d)", j=4)).then_inc(landed[slot], 16)
            else:
                sp.dma_start(ring[0:FAR, slot, :].rearrange("p (j n) -> p j n", j=4),
                             rows[:, 0:PAST - 512].rearrange("a (p j) h d -> p (a j) (h d)", j=16)[:, 0:4, :]
                             ).then_inc(landed[slot], 16)

        def near_rows(name, i):
            return a[name][0, bass.ds(i, 1), PAST - NEAR:PAST].rearrange("a p h d -> p (a h d)")

        def queries_in(i, slot=5):
            sp.dma_start(ring[0:MID, slot, :].unsqueeze(1), q_scr.rearrange("(b t) n -> b (t n)", t=DEC_T)[
                bass.ds(i, 1), :].unsqueeze(0).to_broadcast([MID, 1, SLOT])).then_inc(landed[slot], 16)

        def turn_loads(i, first=False, last=False):
            def free(which, n):
                sp.wait_ge(h_turned, 12)
                sp.wait_ge(which, n)

            if not first:
                free(kt_turned, 2 * i)
            sp.dma_start(near_k, near_rows("cache_k", i)).then_inc(near_in, 16)
            if not first:
                free(near_v_used, i)
            sp.dma_start(near_v, near_rows("cache_v", i)).then_inc(near_v_in, 16)
            if not (first or last):
                free(mid_done, i + 1)
                keys_in(0, i + 1)
            if not first:
                free(used[2], i)
            else:
                free(far_done, 1)
            keys_in(2, i)
            if first:
                sp.wait_ge(y_done, 8)
            if not last:
                free(far_done, i + 1)
                queries_in(i + 1)
                sp.wait_ge(h_turned, 12)
                keys_in(1, i + 1)
            if not first:
                free(used[3], i)
                keys_in(3, i)

        sp.wait_ge(proj_done, 28)
        keys_in(0, 0)
        sp.wait_ge(q_stored, 16)
        queries_in(0, slot=1)
        sp.wait_ge(proj_done, 32)
        keys_in(1, 0, slot=2)
        keys_in(3, 0)
        sp.wait_ge(mid_done, 1)
        keys_in(0, 1)
        sp.wait_ge(d_done, 8)
        sp.wait_ge(stored, 16 * 5)
        sp.wait_ge(pstored, 16 * 9)
        turn_loads(0, first=True)
        with sp.Fori(1, DEC_B - 1) as i:
            turn_loads(i)
        turn_loads(DEC_B - 1, last=True)
        for par, frees in enumerate(((mid_done, far_done), (used[2], used[3]))):
            for which in frees:
                sp.wait_ge(which, DEC_B)
            load_columns(sp, w_o_t, par * TILE, par)
        sp.wait_ge(used[3], DEC_B)
        sp.wait_ge(pO, PAIRS + 1)
        sp.wait_ge(stage_ready, 3 * PAIRS)
        sp.wait_ge(stored, 16 * 5)
        sp.wait_ge(pstored, 16 * 9)
        sp.dma_start(z[:, 0:2, 0:D], xp_t).then_inc(x_again, 16)
        sp.dma_start(z[0:NS, 2, 0:D], xs_t).then_inc(x_again, 16)
        sp.dma_start(route, a["c_route"]).then_inc(route_in, 16)
        for par in range(2):
            sp.wait_ge(wo_done, 4 * par + 4)
            load_columns(sp, w_o_t, (2 + par) * TILE, par)
        sp.wait_ge(pS, 2 * PAIRS)
        sp.wait_ge(y_done, 8)

        def experts(it, par8):
            def up(k):
                wg, wu = (a[n][0, bass.ds(par8 * 8 + k, 1)].rearrange("a (c p) n -> p (a c) n", p=P)
                          for n in ("w_gate", "w_up"))
                for s, w, half, freed, n in ((4, wg, 0, used[4], 1), (5, wg, 1, gate_done, 1),
                                             (0, wu, 0, used[0], 1), (1, wu, 1, up_done, 1)):
                    if s == 0:
                        sp.wait_ge(wo_done, 12)
                    sp.wait_ge(freed, it * 8 + (n + k))
                    sp.dma_start(ring[:, s, :].rearrange("p (c n) -> p c n", n=TILE),
                                 w[:, half * 8:half * 8 + 8, :]).then_inc(landed[s], 16)

            def down(k):
                wd = a["w_down"][0, bass.ds(par8 * 8 + k, 1)].rearrange("a (f p) n -> p (a f) n", p=P)
                sp.wait_ge(wo_done, 16)
                for s, half, freed, n in ((2, 0, used[2], 8), (3, 1, down_done, 1)):
                    sp.wait_ge(freed, it * 8 + (n + k))
                    sp.dma_start(ring[:, s, :].rearrange("p (f n) -> p f n", n=D),
                                 wd[:, half * 2:half * 2 + 2, :]).then_inc(landed[s], 16)

            up(0)
            for k in range(8):
                if k < 7:
                    up(k + 1)
                down(k)

        with sp.Fori(0, 2) as it:
            experts(it, it)
        sp.wait_ge(idx_ready, 1)
        most = sp.value_load(pidx[0:1, 28:29], min_val=0, max_val=TOK)
        with sp.If(most > P):
            with sp.Fori(1, PASSES) as c:
                with sp.Fori(0, 2) as j:
                    experts(c * 2 + j, j)

    @block.gpsimd
    def _(pool):
        pool.dma_start(o["pool_sample"][0, :, 0:BUF - DEC_T, :], a["state_pool"][0, :, DEC_T:BUF, :]).then_inc(pstored, 16)
        pool.wait_ge(normed, 2)
        pool.dma_start(q_scr, z[0:NS, 2, 0:AW]).then_inc(q_stored, 16)
        pool.wait_ge(normed, 4)
        for n, name in ((1, "k"), (2, "v")):
            if n == 2:
                pool.wait_ge(z_moved, 3 + 18)
            pool.dma_start(o[f"{name}_prompt"][0, 0].rearrange("(c p) h d -> p c (h d)", p=P),
                           z[:, 0:2, n * AW:(n + 1) * AW]).then_inc(stored, 16)
            pool.dma_start(o[f"{name}_sample"][0].rearrange("b t h d -> (b t) (h d)"),
                           z[0:NS, 2, n * AW:(n + 1) * AW]).then_inc(stored, 16)
        pool.wait_ge(z_moved, 3 + 24)
        pool.dma_start(o["pool_prompt"][0, 0], z[P - BUF:P, 1, 3 * AW:IN_W]).then_inc(stored, 16)
        for b in range(DEC_B):
            pool.dma_start(o["pool_sample"][0, b, BUF - DEC_T:BUF, :],
                           z[b * DEC_T:(b + 1) * DEC_T, 2, 3 * AW:IN_W]).then_inc(pstored, 16)
        pool.wait_ge(proj_done, 32)
        pool.dma_start(ring[MID:P, 2, 0:AW], z[0:NS, 2, 2 * AW:3 * AW]).then_inc(new_v_in, 16)
        with pool.Fori(0, PAIRS) as i:
            pool.wait_ge(pT, i + 1)
            for n, dst in ((0, st_q), (1, st_k), (2, st_v)):
                if n == 2:
                    pool.wait_ge(pO, i + 1)
                pool.tensor_copy(dst, z[:, 0:2, bass.ds(i * P + n * AW, P)]).then_inc(stage_ready, 1)

        def stage_rows(col, target, n, nth):
            at = 29 + 2 * n + target
            pool.tensor_copy(pidx[:, at:at + 1], pidx[:, bass.ds(col + 14 * target, 1)]).then_inc(idx_copied, 1)
            pool.wait_ge(idx_copied, nth)

        def gather(n):
            pool.indirect_dma_start(
                out=XG[n], out_offset=None, in_=x1_scr,
                in_offset=bass.IndirectOffsetOnAxis(ap=pidx[:, 29 + 2 * n:30 + 2 * n], axis=0),
            ).then_inc(gathered[n], 16)

        def experts(it, last=False):
            for n in range(2):
                stage_rows(it * 2 + n, 1, n, it * 4 + (2 * n + 3))
                pool.wait_ge(out_rows, it * 8 + (4 * n + 8))
                if n:
                    pool.wait_ge(scattered[0], it * 16 + 16)
                pool.sem_inc(pool_turn, 1)
                pool.indirect_dma_start(
                    out=o["y"], out_offset=bass.IndirectOffsetOnAxis(ap=pidx[:, 30 + 2 * n:31 + 2 * n], axis=0),
                    in_=XG[n], in_offset=None).then_inc(scattered[n], 16)
                stage_rows(it * 2 + (n + 2), 0, n, it * 4 + (2 * n + 4))
                pool.wait_ge(scattered[n], it * 16 + 16)
                pool.sem_inc(pool_turn, 1)
                if not (last and n):
                    gather(n)

        pool.wait_ge(stored, 16 * 5)
        pool.wait_ge(pstored, 16 * (1 + DEC_B))
        pool.wait_ge(rows_ready, 1)
        pool.wait_ge(x1_stored, 16 * 8)
        for n in range(2):
            stage_rows(n, 0, n, n + 1)
            gather(n)
        pool.wait_ge(idx_ready, 1)
        experts(0)
        experts(1, last=True)
        pool.wait_ge(gathered[0], 16 * 3)
        most = pool.value_load(pidx[0:1, 28:29], min_val=0, max_val=TOK)
        with pool.If(most > P):
            gather(1)
            with pool.Fori(1, PASSES) as c:
                with pool.Fori(0, 2) as j:
                    experts(c * 2 + j)
            for n in range(2):
                pool.wait_ge(gathered[n], 16 * (2 * PASSES + 1))

    @block.scalar
    def _(act):
        act.dma_start(eye2[:, :], a["c_eye"]).then_inc(const_in, 16)
        act.dma_start(small[:, 0:588], a["small"]).then_inc(const_in, 16)
        act.sem_inc(zT_moved, 2)
        act.sem_inc(zT_turned, 2)
        act.sem_inc(ppt_moved, 2)
        act.sem_inc(po_moved, 1)

        act.wait_ge(root_in, 1)
        act.activation(stat[:, 114:115], stat[:, 3:4], ACT.Square).then_inc(tables_in, 1)
        for k in (0, 2, 1):
            m = CHUNKS[k][1]
            act.wait_ge(x_in[k], 16)
            act.activation(Z[0:m, k * D:(k + 1) * D], x_rows[0:m, k, 0:D], ACT.Square,
                           accum_out=stat[0:m, k:k + 1]).then_inc(squares, 1)
        act.wait_ge(root_in, 2)
        act.activation(stat[:, 4:7], stat[:, 4:7], ACT.Sqrt).then_inc(roots, 1)
        act.wait_ge(rms_ready, 1)
        act.activation(x_rows[:, 1, :], x_rows[:, 1, :], ACT.Identity, scale=stat[:, 9:10]).then_inc(h_rows[1], 1)
        act.wait_ge(bias_mm, 1)
        act.activation(gS[:, :], PS[0:H, 5, 0:384], ACT.Copy).then_inc(g_ready, 1)
        act.wait_ge(g_ready, 1)
        act.dma_start(g_scr, gS[:, :]).then_inc(g_stored, 16)
        act.wait_ge(g_stored, 16)
        act.dma_start(T, bass.AP(g_scr.tensor, 0, [[1, P], [384, H], [1, 256]])).then_inc(landed[4], 16)

        def block_out(i, q, done, turn0):
            act.wait_ge(done, 8 * i + (q + 1))
            act.wait_ge(zT_turned, 8 * i + (8 * turn0 + q + 1))
            act.activation(zTs[:, q % 2, :], PS[:, q % 2, 0:TOK], ACT.Copy).then_inc(zT_moved, 1)

        def z_out(i):
            for q in range(8):
                block_out(i, q, proj_done, 0)
                if q in (4, 7):
                    par = q // 7
                    act.wait_ge(zT_turned, 8 * i + (4 * par + 6))
                    for k, (t0, m) in enumerate(CHUNKS):
                        act.activation(z[0:m, k, bass.ds(i * 2 * TILE + par * TILE, TILE)],
                                       PS[0:m, 2 + k, :], ACT.Copy).then_inc(z_moved, 1)

        def head_roots(w):
            for part in range(2):
                act.wait_ge(root_in, 3 + 2 * w + part)
                v = stat[:, 16:48] if part == 0 else stat[0:NS, 48:64]
                act.activation(v, v, ACT.Sqrt).then_inc(roots, 1)

        act.wait_ge(bias_moved, 3)
        act.sem_inc(z_moved, 3)
        with act.Fori(0, 2) as i:
            z_out(i)
        head_roots(0)
        with act.Fori(2, 3) as i:
            z_out(i)
        head_roots(1)
        with act.Fori(3, 4) as i:
            z_out(i)
        act.wait_ge(sT_done, 1)
        act.activation(qTs[:, :, :], PS[:, 6, 0:256].rearrange("p (a t) -> p a t", t=NS), ACT.Copy,
                       scale=SCALE).then_inc(sT_moved, 1)
        act.activation(KT[:, :, NEAR:NEAR + NS], PS[:, 6, 256:512].rearrange("p (a t) -> p a t", t=NS),
                       ACT.Copy).then_inc(sT_moved, 1)
        for g in range(4):
            for eh in range(2):
                act.wait_ge(y_done, 2 * g + eh + 1)
                act.activation(hT[:, 8 + 2 * g + eh, :], PS[:, 4 + eh, 0:TOK], ACT.Identity,
                               scale=pscale[:, 2 * g + eh:2 * g + eh + 1]).then_inc(y_moved, 1)
            if g < 2:
                for ch in range(2):
                    act.wait_ge(d_done, 2 * (g + 2) + ch + 1)
                    act.activation(dT[:, g, ch, :], PS[:, 2 * g + ch, 0:TOK], ACT.Copy).then_inc(d_late_moved, 1)
        act.wait_ge(diag, 4)
        act.wait_ge(pads_ready, 2)
        act.wait_ge(const_in, 32)
        with act.Fori(0, PAIRS) as i:
            act.activation(stat[:, 112:113], eye[:, 0:1], ACT.Exp).then_inc(tables_in, 1)
            for g in range(2):
                act.wait_ge(kt_turned, i * 2 + (g + 1))
                act.wait_ge(s_done, i + 1)
                act.activation(KT[:, 4 * g:4 * g + 4, 0:NEAR], PS[:, g, :].rearrange("p (a n) -> p a n", n=NEAR),
                               ACT.Copy).then_inc(ktn, 1)
            act.wait_ge(pT, i + 2)
            for par in range(2):
                r = slice(64 * par, 64 * par + 64)
                act.activation(qTz[par][r], PS[r, 6, 0:256], ACT.Copy, scale=SCALE).then_inc(qk_moved, 1)
            act.activation(kTp, PS[:, 6, 256:512], ACT.Copy).then_inc(qk_moved, 1)

            def prompt_exp(par):
                act.wait_ge(p_negmax, i * 2 + (par + 1))
                for q, (c0, c1) in enumerate(((0, 128), (128, 384))):
                    act.activation(PP[:, par, c0:c1], PS[:, 2 + par, c0:c1], ACT.Exp,
                                   bias=stat[:, 68 + 4 * par + q:69 + 4 * par + q],
                                   accum_out=stat[:, 76 + 4 * par + q:77 + 4 * par + q]).then_inc(p_exp, 1)

            def prompt_turned(par):
                act.wait_ge(pPT, i * 2 + (par + 1))
                act.activation(PPT[:, par, :], PS[:, par, 0:384], ACT.Copy).then_inc(ppt_moved, 1)

            def prompt_scaled(par):
                act.wait_ge(p_inv, i * 2 + (par + 1))
                for q, (c0, c1) in enumerate(((0, 128), (128, 384))):
                    act.activation(PP[:, par, c0:c1], PP[:, par, c0:c1], ACT.Identity,
                                   scale=stat[:, 88 + 2 * par + q:89 + 2 * par + q]).then_inc(p_norm, 1)

            act.wait_ge(tables_in, i + 2)
            act.wait_ge(s_negmax, i + 1)
            act.activation(SB, SB, ACT.Exp, bias=stat[0:64, 65:66],
                           accum_out=stat[0:64, 66:67]).then_inc(s_exp, 1)
            act.wait_ge(sPT, i + 1)
            act.activation(PTn, PS[:, 5, 0:64], ACT.Copy).then_inc(pts_moved, 1)
            act.activation(PTb[0][MID:P, 0:64], PS[MID:P, 5, 64:128], ACT.Copy).then_inc(pts_moved, 1)
            for n in range(2):
                act.activation(PTb[n][0:MID].rearrange("p (a n) -> p a n", n=80)[:, :, 0:16],
                               PS[0:MID, 5, 64 + 64 * n:128 + 64 * n].rearrange("p (a n) -> p a n", n=16),
                               ACT.Copy).then_inc(pts_moved, 1)
            for par in range(2):
                prompt_exp(par)
            for par in range(2):
                prompt_scaled(par)
            for par in range(2):
                prompt_turned(par)
            act.wait_ge(used[3], i + 1)
            act.wait_ge(s_inv, i + 1)
            for vh in range(2):
                act.activation(OS[:, vh * TILE:(vh + 1) * TILE], PS[0:64, 6 + vh, :], ACT.Identity,
                               scale=stat[0:64, 67:68]).then_inc(os_moved, 1)
            act.wait_ge(pO, i + 2)
            act.activation(hT[:, bass.ds(i, 1), 0:SEQ].rearrange("p a t -> p (a t)"), PS[:, 2, 0:SEQ],
                           ACT.Copy).then_inc(po_moved, 1)
        act.wait_ge(root_in, 7)
        for n in range(4 * 4 + 3):
            if n < 16:
                block_out(n // 8, n % 8, wo_done, 4)
            if n % 4 == 2 and n > 4:
                t = n // 4 - 1
                act.wait_ge(wo_moved, 3 * t + 6)
                for k, (t0, m) in enumerate(CHUNKS):
                    act.activation(z[0:m, k, D + t * TILE:D + (t + 1) * TILE], z[0:m, k, t * TILE:(t + 1) * TILE],
                                   ACT.Square, accum_out=stat[0:m, 96 + 4 * k + t:97 + 4 * k + t]).then_inc(squares, 1)
                act.dma_start(x1_scr[0:SEQ, t * TILE:(t + 1) * TILE].rearrange("(c p) d -> p c d", p=P),
                              z[:, 0:2, t * TILE:(t + 1) * TILE]).then_inc(x1_stored, 16)
                act.dma_start(x1_scr[SEQ:TOK, t * TILE:(t + 1) * TILE],
                              z[0:NS, 2, t * TILE:(t + 1) * TILE]).then_inc(x1_stored, 16)
        act.wait_ge(const_in, 32)
        act.activation(stat[:, 113:114], eye[:, 0:1], ACT.Sqrt).then_inc(tables_in, 1)
        act.wait_ge(root_in, 8)
        act.activation(stat[:, 4:7], stat[:, 4:7], ACT.Sqrt).then_inc(roots, 1)
        act.wait_ge(rl_done, 1)
        act.activation(LG, PS[0:20, 5, 0:TOK], ACT.Copy).then_inc(rl_moved, 1)
        for n in range(2):
            act.wait_ge(exp_in, n + 1)
            v = R[:, 60:72] if n == 0 else R[:, 132:135]
            act.activation(v, v, ACT.Exp).then_inc(expd, 1)

        def experts(it):
            def sil(k):
                act.wait_ge(gate_done, it * 8 + (k + 2))
                act.activation(SIL, PS[:, 0, :], ACT.Silu).then_inc(sil_ready, 1)

            def turned(k):
                act.wait_ge(hidT_done, it * 8 + (k + 1))
                act.activation(HIDT, PS[:, 2, :].rearrange("p (f t) -> p f t", t=P), ACT.Copy).then_inc(hidT_moved, 1)

            for k in range(8):
                if k:
                    act.wait_ge(hid_ready, it * 8 + k)
                sil(k)
                if k:
                    turned(k - 1)
            turned(7)

        with act.Fori(0, 2) as it:
            experts(it)
        act.wait_ge(idx_ready, 1)
        most = act.value_load(pidx[0:1, 28:29], min_val=0, max_val=TOK)
        with act.If(most > P):
            with act.Fori(1, PASSES) as c:
                with act.Fori(0, 2) as j:
                    experts(c * 2 + j)

    @block.tensor
    def _(pe):
        def mm(out, lhsT, rhs, start, stop):
            return pe.matmul(out, lhsT, rhs, start=start, stop=stop, skip_group_check=True)

        pe.sem_inc(pT, 1)
        pe.sem_inc(pO, 1)
        pe.sem_inc(s_done, 1)
        for s in (used[4], used[0], gate_done, up_done, down_done):
            pe.sem_inc(s, 1)
        pe.wait_ge(const_in, 32)
        pe.wait_ge(landed[5], 16)
        mm(PS[0:H, 5, 0:384], relP, c_one, True, True).then_inc(bias_mm, 1)
        for n, (c0, c1) in enumerate(((0, 320), (320, EC))):
            mm(PS[0:64, 3 + n, 0:c1 - c0], relS, c_hot[:, c0:c1], True, True).then_inc(bias_mm, 1)
        for n in range(12):
            k, g = n // 4, n % 4
            m = CHUNKS[k][1]
            if g == 0:
                pe.wait_ge(h_rows[k], 1)
            if n >= 4:
                pe.wait_ge(h_moved, n - 3)
            for q in range(4):
                c = 4 * g + q
                ins = pe.transpose(PS[:, TURN_BANKS[n % 4], q * m:(q + 1) * m], x_rows[0:m, k, c * P:(c + 1) * P],
                                   eye[0:m, 0:m])
            ins.then_inc(h_turned, 1)
        pe.wait_ge(h_moved, 12)

        def column_block(i, q, done, moved, base, turn0):
            def turn_block(q):
                pe.wait_ge(zT_moved, 8 * i + (8 * turn0 + q + 3))
                if q % 4 == 0:
                    pe.wait_ge(moved, 6 * i + (3 * (q // 4) + 3))
                for k, (t0, m) in enumerate(CHUNKS):
                    ins = pe.transpose(PS[0:m, 2 + k, (q % 4) * P:(q % 4 + 1) * P], zTs[:, q % 2, t0:t0 + m], eye)
                ins.then_inc(zT_turned, 1)

            pe.wait_ge(zT_moved, 8 * i + (8 * turn0 + q + 1))
            for half in range(2):
                s = 2 * (q // 4) + half
                if q % 4 == 0:
                    pe.wait_ge(landed[s], 16 * i + 16 * (base[s] + 1))
                w = ring[:, s, :].rearrange("p (c n) -> p c n", n=TILE)
                for c in range(8):
                    cc = half * 8 + c
                    ins = mm(PS[:, q % 2, 0:TOK], w[:, c, (q % 4) * P:(q % 4 + 1) * P], hT[:, cc, :],
                             cc == 0, cc == DC - 1)
            ins.then_inc(done, 1)
            if q:
                turn_block(q - 1)
            if q == 7:
                turn_block(7)

        with pe.Fori(0, 4) as i:
            for q in range(8):
                column_block(i, q, proj_done, z_moved, [0] * 4, 0)
        pe.wait_ge(normed, 4)
        for w in range(2):
            for pair in range(PAIRS):
                ins = pe.transpose(PS[:, 6, w * 256 + pair * NS:w * 256 + (pair + 1) * NS],
                                   z[0:NS, 2, w * AW + pair * P:w * AW + (pair + 1) * P], eye[0:NS, 0:NS])
        ins.then_inc(sT_done, 1)
        pe.wait_ge(z_moved, 3 + 24)
        pe.wait_ge(landed[5], 32)
        pe.wait_ge(state_in, 32)

        def windows(g):
            for ch in range(2):
                if g >= 2:
                    pe.wait_ge(d_moved, 2 * (g - 2) + ch + 1)
                u0 = 3 * AW + g * GW + ch * P
                bank = PS[:, 2 * (g % 2) + ch, :]
                mm(bank[:, 0:256], z[:, 0, u0:u0 + P], c_pool[:, g * 256:(g + 1) * 256], True, False)
                mm(bank[:, 128:256], z[:, 1, u0:u0 + P], c_pool[:, 1024 + g * 128:1152 + g * 128], False, True)
                mm(bank[:, 256:288], state[:, g * GW + ch * P:g * GW + (ch + 1) * P],
                   c_pool[0:DEC_B * BUF, 1536 + g * 32:1568 + g * 32], False, False)
                mm(bank[:, 256:288], z[0:NS, 2, u0:u0 + P],
                   c_pool[0:NS, 1664 + g * 32:1696 + g * 32], False, True).then_inc(d_done, 1)

        def group_map(g):
            pe.wait_ge(d_moved if g < 2 else d_late_moved, 2 * (g % 2) + 2)
            for eh in range(2):
                if g:
                    pe.wait_ge(y_moved, 2 * (g - 1) + eh + 1)
                for ch in range(2):
                    ins = mm(PS[:, 4 + eh, 0:TOK], wpool[:, g, ch, eh * P:(eh + 1) * P], dT[:, g % 2, ch, :],
                             ch == 0, ch == 1)
                ins.then_inc(y_done, 1)

        windows(0)
        for g in range(4):
            if g < 3:
                windows(g + 1)
            group_map(g)
        pe.wait_ge(landed[4], 16)
        pe.wait_ge(new_v_in, 16)
        pe.wait_ge(y_moved, 8)
        pe.wait_ge(sT_moved, 2)
        with pe.Fori(0, PAIRS) as i:
            pe.wait_ge(const_in, 32)
            pe.wait_ge(mid_done, i + 1)
            pe.wait_ge(near_in, i * 16 + 16)
            for pair in range(PAIRS):
                ins = pe.transpose(PS[:, pair // 4, (pair % 4) * P:(pair % 4 + 1) * P],
                                   near_k[:, pair * P:(pair + 1) * P], eye)
                if pair % 4 == 3:
                    ins.then_inc(kt_turned, 1)
            pe.wait_ge(stage_ready, i * 3 + 2)
            for w, src in enumerate((st_q, st_k)):
                for c in range(2):
                    ins = pe.transpose(PS[:, 6, (2 * w + c) * P:(2 * w + c + 1) * P], src[:, c, :], eye)
            ins.then_inc(pT, 1)
            pe.wait_ge(qbd_ready, i * 2 + 2)
            for pair in range(PAIRS):
                if pair % 4 == 0:
                    pe.wait_ge(ktn, i * 2 + (pair // 4 + 1))
                ins = mm(PS[0:64, 4, 0:NEAR + NS], Qbd[:, pair * 64:pair * 64 + 64], KT[:, pair, :],
                         pair == 0, pair == PAIRS - 1)
            ins.then_inc(s_done, 1)
            pe.transpose(PS[0:64, 5, 0:MID], SF[0], eye[0:MID, 0:MID])
            pe.wait_ge(const_in, 32)
            pe.wait_ge(far_done, i + 1)
            pe.transpose(PS[0:64, 5, MID:MID + FAR], SF[1], eye[0:FAR, 0:FAR]).then_inc(sf_turned, 1)
            pe.wait_ge(qk_moved, i * 3 + 3)
            pe.wait_ge(po_moved, i + 1)
            for par in range(2):
                if par:
                    pe.wait_ge(diag, i * 2 + 4)
                bank = PS[:, 2 + par, :]
                bias = T[:, bass.ds(2 * i + par, 1), :].rearrange("p a n -> p (a n)")
                bias_late = T[:, bass.ds(2 * i + par, 1), 128:256].rearrange("p a n -> p (a n)")
                mm(bank[:, 0:128], qTz[par][:, 0:128], kTp[:, 0:128], True, False)
                mm(bank[:, 0:128], flip, bias_late, False, True)
                mm(bank[:, 128:384], qTz[par][:, 128:256], kTp, True, False)
                mm(bank[:, 128:384], flip, bias, False, True).then_inc(pS, 1)
            pe.wait_ge(const_in, 32)
            pe.wait_ge(s_exp, i + 1)
            pe.transpose(PS[:, 5, 0:64], SB[:, 0:NEAR], eye[0:64, 0:64])
            pe.transpose(PS[:, 5, 64:128], SB[:, NEAR:NEAR + P], eye[0:64, 0:64])
            pe.transpose(PS[0:FAR, 5, 128:192], SB[:, NEAR + P:KEYS], eye[0:64, 0:64]).then_inc(sPT, 1)

            def outputs(probs, values, start=False, stop=False):
                for vh in range(2):
                    ins = mm(PS[0:64, 6 + vh, :], probs, values[:, vh * TILE:(vh + 1) * TILE], start, stop)
                return ins

            pe.wait_ge(pts_moved, i * 4 + 1)
            pe.wait_ge(near_v_in, i * 16 + 16)
            outputs(PTn, near_v, start=True).then_inc(near_v_used, 1)

            def strided_outputs(n):
                pe.wait_ge(pts_moved, i * 4 + (n + 3))
                pe.wait_ge(landed[2 + n], i * 16 + 16 * (BASE_AT[2 + n] + 1))
                for j in range(4):
                    rows = slice(0, P if (n, j) == (0, 0) else MID)
                    ins = outputs(PTb[n][rows, j * 64:(j + 1) * 64], ring[rows, 2 + n, j * AW:(j + 1) * AW],
                                  stop=n == 1 and j == 3)
                ins.then_inc(used[2 + n], 1)
                return ins

            strided_outputs(0)
            for par in range(2):
                pe.wait_ge(p_norm, i * 4 + (2 * par + 2))
                for n in range(3):
                    ins = pe.transpose(PS[:, par, n * P:(n + 1) * P], PP[:, par, n * P:(n + 1) * P], eye)
                ins.then_inc(pPT, 1)
            strided_outputs(1)
            pe.wait_ge(stage_ready, i * 3 + 3)
            for par in range(2):
                pe.wait_ge(ppt_moved, i * 2 + (par + 3))
                out = PS[64 * par:64 * par + 64, 2, :]
                mm(out[:, 0:256], st_v[:, 0, 64 * par:64 * par + 64], PPT[:, par, 0:256], True, False)
                ins = mm(out[:, 128:256], st_v[:, 1, 64 * par:64 * par + 64], PPT[:, par, 256:384], False, True)
            ins.then_inc(pO, 1)
            pe.wait_ge(const_in, 32)
            pe.wait_ge(os_moved, i * 2 + 2)
            for pair in range(PAIRS):
                ins = pe.transpose(PS[:, 3, pair * 64:(pair + 1) * 64], OS[:, pair * P:(pair + 1) * P], eye[0:64, 0:64])
            ins.then_inc(sOT, 1)
        pe.wait_ge(po_moved, PAIRS + 1)
        pe.wait_ge(diag, 2 + 2 + 2 * DEC_B)
        def x1_block(c):
            pe.wait_ge(wo_moved, 3 * (c // 4) + 6)
            if c >= 2:
                pe.wait_ge(x1_moved, c - 1)
            for k, (t0, m) in enumerate(CHUNKS):
                ins = pe.transpose(PS[:, 6 + c % 2, t0:t0 + m], z[0:m, k, c * P:(c + 1) * P], eye[0:m, 0:m])
            ins.then_inc(x1_turned, 1)

        def router_block(c):
            pe.wait_ge(x1_moved, c + 1)
            ins = mm(PS[0:20, 5, 0:TOK], wr[:, c, :], x1T[:, c, :], c == 0, c == DC - 1)
            if c == DC - 1:
                ins.then_inc(rl_done, 1)

        for n in range(DC + 6):
            if n < DC:
                column_block(n // 8, n % 8, wo_done, wo_moved, BASE_WO, 4)
            if 5 <= n < DC + 5:
                x1_block(n - 5)
            if n >= 6:
                router_block(n - 6)
        pe.wait_ge(rl_moved, 1)
        for k, (t0, m) in enumerate(CHUNKS):
            ins = pe.transpose(PS[0:m, 6, k * 20:(k + 1) * 20], LG[:, t0:t0 + m], eye[0:20, 0:20])
        ins.then_inc(lgT_done, 1)
        tri, ones = ranks[:, 0:P], ranks[:, P:2 * P]
        oh = [ranks[:, 2 * P + 4 * k:2 * P + 4 * k + 4] for k in range(3)]
        pe.wait_ge(oh_ready, 2)
        for n, parts in enumerate((((tri, 0),), ((ones, 0), (tri, 1)), ((ones, 0), (ones, 1), (tri, 2)),
                                   ((ones, 0), (ones, 1), (ones, 2)))):
            for q, (m, k) in enumerate(parts):
                ins = mm(PS[:, 7, 4 * n:4 * n + 4], m, oh[k], q == 0, q == len(parts) - 1)
        ins.then_inc(rank_done, 1)
        def pass_table(c, bank, col0, n_col):
            for k in range(3):
                ins = mm(PS[:, bank, 64 + n_col * c:64 + n_col * (c + 1)], Pm[:, c, k, :],
                         R[:, col0 + n_col * k:col0 + n_col * (k + 1)], k == 0, k == 2)
            ins.then_inc(idx_done, 1)

        for c in range(PASSES):
            pe.wait_ge(pm_ready, 3 * c + 3)
            pass_table(c, 4 if c else 6, 292, 12)

        def experts(it):
            def up(k, bank, slot0, done):
                for half in range(2):
                    s = slot0 + half
                    pe.wait_ge(landed[s], it * 128 + 16 * (BASE_MOE[s] + k + 1))
                    w = ring[:, s, :].rearrange("p (c n) -> p c n", n=TILE)
                    for c in range(8):
                        cc = half * 8 + c
                        ins = mm(PS[:, bank, :], HTG[k // 4][:, cc, :], w[:, c, :], cc == 0, cc == DC - 1)
                    if half == 0:
                        ins.then_inc(used[s], 1)
                ins.then_inc(done, 1)

            def gate(k):
                if k:
                    pe.wait_ge(sil_ready, it * 8 + k)
                up(k, 0, 4, gate_done)

            def raise_(k):
                if k:
                    pe.wait_ge(hid_ready, it * 8 + k)
                up(k, 1, 0, up_done)

            def turn_hidden(k):
                pe.wait_ge(hid_ready, it * 8 + (k + 1))
                for f in range(4):
                    ins = pe.transpose(PS[:, 2, f * P:(f + 1) * P], HID[:, f * P:(f + 1) * P], eye)
                ins.then_inc(hidT_done, 1)

            def down(k):
                pe.wait_ge(hidT_moved, it * 8 + (k + 1))
                if k % 4 == 0:
                    pe.wait_ge(out_rows, it * 8 + (k + 4))
                for half in range(2):
                    s = 2 + half
                    pe.wait_ge(landed[s], it * 128 + 16 * (BASE_MOE[s] + k + 1))
                    w = ring[:, s, :].rearrange("p (f n) -> p f n", n=D)
                    by_column = half == 1 and k % 4 == 3
                    for a in range(8):
                        f, q = (a % 2, a // 2) if by_column else (a // 4, a % 4)
                        ff = half * 2 + f
                        ins = mm(PS[:, 3 + q, :], HIDT[:, ff, :], w[:, f, q * TILE:(q + 1) * TILE],
                                 k % 4 == 0 and ff == 0, k % 4 == 3 and ff == 3)
                        if by_column and f and q < 3:
                            ins.then_inc(down_part, 1)
                    if half == 0:
                        ins.then_inc(used[s], 1)
                ins.then_inc(down_done, 1)

            def turn_part(j):
                if j % 4 == 0:
                    pe.wait_ge(hn_ready, it * 2 + (j // 4 + 2))
                pe.wait_ge(htg_moved, it * 8 + (j + 4))
                rows_part(7, j % 4)

            for k in range(8):
                if k % 4 == 0:
                    pe.wait_ge(htg_moved, it * 8 + (k + 4))
                gate(k)
                if k:
                    turn_hidden(k - 1)
                if k % 4 == 3:
                    turn_part(k - 1)
                raise_(k)
                if k:
                    down(k - 1)
                if k % 4:
                    turn_part((k - 1, k - 1, k)[k % 4 - 1])
            turn_hidden(7)
            down(7)

        def rows_part(bank, r):
            for q in range(4):
                c = 4 * r + q
                ins = pe.transpose(PS[:, bank, q * P:(q + 1) * P], HN[:, c * P:(c + 1) * P], eye)
            ins.then_inc(htg_turned, 1)

        pe.wait_ge(hn_ready, 1)
        for r, bank in enumerate(FIRST_BANKS):
            rows_part(bank, r)
        pe.wait_ge(gates_ready, 1)
        for c in range(PASSES):
            pass_table(c, 3, 232, 16)
        with pe.Fori(0, 2) as it:
            experts(it)
        pe.wait_ge(idx_ready, 1)
        most = pe.value_load(pidx[0:1, 28:29], min_val=0, max_val=TOK)
        with pe.If(most > P):
            with pe.Fori(1, PASSES) as c:
                with pe.Fori(0, 2) as j:
                    experts(c * 2 + j)

    @block.vector
    def _(dve):
        steps = Steps(dve, dve_step)
        did, settle = steps.did, steps.settle
        dve.sem_inc(diag, 2)
        dve.sem_inc(wo_moved, 3)
        dve.memset(stat[:, 0:4], 1.0).then_inc(root_in, 1)

        dve.wait_ge(squares, 3)
        dve.tensor_scalar(stat[:, 4:7], stat[:, 0:3], 1.0 / D, EPS, ALU.mult, ALU.add).then_inc(root_in, 1)
        dve.wait_ge(roots, 1)
        dve.reciprocal(stat[:, 8:11], stat[:, 4:7]).then_inc(rms_ready, 1)
        dve.wait_ge(rms_ready, 1)
        for k in (0, 2):
            m = CHUNKS[k][1]
            dve.tensor_scalar(x_rows[0:m, k, :], x_rows[0:m, k, :], stat[0:m, 8 + k:9 + k], None,
                              ALU.mult).then_inc(h_rows[k], 1)
        for n in range(12):
            k, g = n // 4, n % 4
            t0, m = CHUNKS[k]
            dve.wait_ge(h_turned, n + 1)
            dve.tensor_tensor(hT[:, 4 * g:4 * g + 4, t0:t0 + m],
                              PS[:, TURN_BANKS[n % 4], 0:4 * m].rearrange("p (c t) -> p c t", c=4),
                              ln1T[:, 4 * g:4 * g + 4].unsqueeze(2).to_broadcast([P, 4, m]),
                              ALU.mult).then_inc(h_moved, 1)
        dve.wait_ge(bias_mm, 3)
        for n, (c0, c1) in enumerate(((0, 320), (320, EC))):
            dve.tensor_tensor(E[:, c0:c1], PS[0:64, 3 + n, 0:c1 - c0], c_mask[:, c0:c1], ALU.add).then_inc(bias_moved, 1)
        dve.memset(Qbd[:, :], 0.0).then_inc(bias_moved, 1)
        for w in range(2):
            dve.wait_ge(z_moved, 9 + 6 * w)
            for part, (m, k0, k1, s0) in enumerate(((P, 0, 2, 16), (NS, 2, 3, 48))):
                nk = k1 - k0
                v = z[0:m, k0:k1, w * AW:(w + 1) * AW]
                tmp = sq_tmp[0:m, 0:nk * AW]
                v4 = v.rearrange("p c (h d) -> p c h d", d=HD)
                sums = stat[0:m, s0:s0 + nk * H]
                did(dve.tensor_tensor(tmp.rearrange("p (c n) -> p c n", n=AW), v, v, ALU.mult))
                settle()
                did(dve.tensor_reduce(sums, tmp.rearrange("p (s d) -> p s d", d=HD), AX.X, ALU.add))
                settle()
                dve.tensor_scalar(sums, sums, 1.0 / HD, EPS, ALU.mult, ALU.add).then_inc(root_in, 1)
                dve.wait_ge(roots, 2 + 2 * w + part)
                did(dve.reciprocal(sums, sums))
                settle()
                did(dve.tensor_tensor(v4, v4, sums.rearrange("p (c h) -> p c h", h=H).unsqueeze(3).to_broadcast(
                    [m, nk, H, HD]), ALU.mult))
                settle()
                dve.tensor_tensor(v4, v4, qkw[0:m, w, :].unsqueeze(1).unsqueeze(1).to_broadcast([m, nk, H, HD]),
                                  ALU.mult).then_inc(normed, 1)
        def queries_out(i):
            for par in range(2):
                r = slice(64 * par, 64 * par + 64)
                dve.tensor_copy(Qbd[r, :].rearrange("p (a n) -> p a n", n=65)[:, :, 8 * par:8 * par + 49:16],
                                qTs[r, :, bass.ds(i * 4, 4)]).then_inc(qbd_ready, 1)

        def products(slot, half, q_slot=5):
            v = ring[0:MID, slot, half * 2048:(half + 1) * 2048]
            step(dve.tensor_tensor(v, v, ring[0:MID, q_slot, half * 2048:(half + 1) * 2048], ALU.mult))

        def sums(n, j, slot=None):
            slot = n if slot is None else slot
            return dve.tensor_reduce(SF[n][:, 16 * j:16 * j + 16].rearrange("p (a b) -> p b a", a=2),
                                     ring[0:MID, slot, j * AW:(j + 1) * AW].rearrange("p (b a d) -> p b a d", a=2, d=HD),
                                     AX.X, ALU.add)

        def step(ins):
            did(ins)
            settle()

        def first_scores(n, slot):
            dve.wait_ge(landed[slot], 16 * (BASE_AT[0] + 1))
            for half in range(2):
                products(slot, half, q_slot=1)
                for j in (2 * half, 2 * half + 1):
                    ins = sums(n, j, slot)
            ins.then_inc((mid_done, far_done)[n], 1)

        dve.wait_ge(landed[1], 16 * (BASE_AT[1] + 1))
        first_scores(0, 0)
        for g in range(2):
            for ch in range(2):
                dve.wait_ge(d_done, 2 * g + ch + 1)
                dve.tensor_copy(dT[:, g % 2, ch, :], PS[:, 2 * (g % 2) + ch, 0:TOK]).then_inc(d_moved, 1)
        for par in range(2):
            other = slice(64 - 64 * par, 128 - 64 * par)
            dve.memset(qTz[par][other], 0.0).then_inc(diag, 1)
        first_scores(1, 2)
        dve.wait_ge(y_done, 8)
        dve.wait_ge(sT_moved, 2)
        for n in range(2):
            dve.memset(PTb[n], 0.0).then_inc(pads_ready, 1)

        queries_out(0)

        def turn(i, last=False):
            dve.wait_ge(s_done, i + 2)
            dve.tensor_tensor(SB[:, 0:NEAR], PS[0:64, 4, 0:NEAR], E[:, 0:NEAR], ALU.add).then_inc(s_sum, 1)
            dve.tensor_tensor(SB_new, PS[0:64, 4, NEAR:NEAR + NS],
                              E[:, bass.ds(i * NS + (KEYS - NS), NS)], ALU.add).then_inc(s_sum, 1)
            dve.wait_ge(sf_turned, i + 1)
            dve.scalar_tensor_tensor(SB_strided, PS[0:64, 5, 0:MID + FAR].rearrange("p (a n) -> p a n", n=MID), SCALE,
                                     E[:, NEAR:KEYS - NS].rearrange("p (a n) -> p a n", n=MID),
                                     ALU.mult, ALU.add).then_inc(s_sum, 1)
            dve.wait_ge(s_sum, i * 3 + 3)
            step(dve.tensor_reduce(stat[0:64, 64:65], SB, AX.X, ALU.max))
            dve.tensor_scalar(stat[0:64, 65:66], stat[0:64, 64:65], -1.0, None, ALU.mult).then_inc(s_negmax, 1)
            if not last:
                queries_out(i + 1)

            def prompt_max(par):
                dve.wait_ge(pS, i * 2 + (par + 1))
                for q, (c0, c1) in enumerate(((0, 128), (128, 384))):
                    did(dve.tensor_reduce(stat[:, 84 + 2 * par + q:85 + 2 * par + q], PS[:, 2 + par, c0:c1],
                                          AX.X, ALU.max))
                settle()
                dve.tensor_scalar(stat[:, 68 + 4 * par:70 + 4 * par], stat[:, 84 + 2 * par:86 + 2 * par], -1.0, None,
                                  ALU.mult).then_inc(p_negmax, 1)

            prompt_max(0)
            prompt_max(1)
            if not last:
                dve.wait_ge(landed[5], i * 16 + 16 * 3)
                dve.wait_ge(landed[0], i * 16 + 16 * (BASE_AT[0] + 2))
                products(0, 0)
                for j in (0, 1):
                    sums(0, j)
            dve.wait_ge(s_exp, i + 1)
            dve.reciprocal(stat[0:64, 67:68], stat[0:64, 66:67]).then_inc(s_inv, 1)
            for par in range(2):
                dve.wait_ge(p_exp, i * 4 + (2 * par + 2))
                dve.reciprocal(stat[:, 88 + 2 * par:90 + 2 * par], stat[:, 76 + 4 * par:78 + 4 * par]).then_inc(p_inv, 1)
            if not last:
                products(0, 1)
                sums(0, 2)
                sums(0, 3).then_inc(mid_done, 1)
                dve.wait_ge(landed[1], i * 16 + 16 * (BASE_AT[1] + 2))
                for half in range(2):
                    products(1, half)
                    for j in (2 * half, 2 * half + 1):
                        ins = sums(1, j)
                ins.then_inc(far_done, 1)
            dve.wait_ge(sOT, i + 1)
            for par in range(2):
                r = slice(64 * par, 64 * par + 64)
                blocks = PS[r, 3:5, :].rearrange("p a n -> p (a n)")[:, 0:520].rearrange(
                    "p (a n) -> p a n", n=65)[:, :, 8 * par:8 * par + 49:16]
                dve.tensor_copy(hT[r, 0:PAIRS, bass.ds(i * 4 + SEQ, 4)], blocks).then_inc(diag, 1)

        with dve.Fori(0, DEC_B - 1) as i:
            steps.begin(i, 9)
            turn(i)
        steps.end(DEC_B - 1)
        turn(DEC_B - 1, last=True)
        dve.memset(stat[:, 96:108], 1.0).then_inc(root_in, 1)
        dve.wait_ge(x_again, 32)
        dve.wait_ge(route_in, 16)
        did(dve.tensor_copy(ranks[:, 0:2 * P], route[:, 0:2 * P]))
        for n in range(DC + 5):
            if n in (4, 8, 12, 16):
                t = n // 4 - 1
                dve.wait_ge(zT_turned, 32 + 4 * t + 6)
                for k, (t0, m) in enumerate(CHUNKS):
                    xt = z[0:m, k, t * TILE:(t + 1) * TILE]
                    dve.tensor_tensor(xt, PS[0:m, 2 + k, :], xt, ALU.add).then_inc(wo_moved, 1)
            if n >= 5:
                c = n - 5
                dve.wait_ge(x1_turned, c + 1)
                dve.tensor_scalar(x1T[:, c, :], PS[:, 6 + c % 2, 0:TOK], ln2T[:, c:c + 1], None,
                                  ALU.mult).then_inc(x1_moved, 1)
        dve.wait_ge(squares, 3 + 12)
        did(dve.tensor_reduce(stat[:, 0:3], stat[:, 96:108].rearrange("p (k t) -> p k t", t=4), AX.X, ALU.add))
        settle()
        dve.tensor_scalar(stat[:, 4:7], stat[:, 0:3], 1.0 / D, EPS, ALU.mult, ALU.add).then_inc(root_in, 1)

        step(dve.memset(R, 0.0))
        dve.wait_ge(roots, 6)
        step(dve.reciprocal(stat[:, 8:11], stat[:, 4:7]))

        def col(c, n=1):
            return R[:, c:c + 3 * n].rearrange("p (k n) -> p k n", n=n)

        dve.wait_ge(lgT_done, 1)
        L = col(0, 20)
        for k, (t0, m) in enumerate(CHUNKS):
            did(dve.scalar_tensor_tensor(L[0:m, k, :], PS[0:m, 6, 20 * k:20 * k + 20], stat[0:m, 8 + k:9 + k],
                                         rb[0:m], ALU.mult, ALU.add))
        settle()
        lg, le = L[:, :, 0:4], L[:, :, 4:20]
        expg, oh, leg, top, work, m1, m2 = col(60, 4), col(72, 4), col(84, 4), col(96, 4), col(108, 4), col(120), col(123)
        best, tmp3, ge, gate4 = col(126), col(129), col(132), col(136, 4)
        valid = route[:, 5 * P + 3:5 * P + 6].unsqueeze(2)
        tokens = route[:, 5 * P:5 * P + 3].unsqueeze(2)
        order = route[:, 5 * P + 9:5 * P + 13].unsqueeze(1).to_broadcast([P, 3, 4])
        spare = route[:, 5 * P + 6:5 * P + 9]

        def wide(v):
            return v.to_broadcast([P, 3, 4])

        def first_of(dst, src, most):
            step(dve.tensor_tensor(dst, src, wide(most), ALU.is_equal))
            step(dve.tensor_tensor(dst, dst, order, ALU.mult))
            step(dve.tensor_reduce(best, dst, AX.X, ALU.max))
            step(dve.tensor_tensor(dst, dst, wide(best), ALU.is_equal))

        step(dve.tensor_reduce(m1, lg, AX.X, ALU.max))
        first_of(oh, lg, m1)
        dve.tensor_tensor(oh, oh, valid.to_broadcast([P, 3, 4]), ALU.mult).then_inc(oh_ready, 1)
        dve.wait_ge(oh_ready, 1)
        dve.tensor_copy(ranks[:, 2 * P:], R[:, 72:84]).then_inc(oh_ready, 1)
        dve.tensor_tensor(expg, lg, wide(m1), ALU.subtract).then_inc(exp_in, 1)
        rank, pos = col(148, 4), col(220)
        rh = R[:, 292:328].rearrange("p (k n) -> p k n", n=12)
        dve.wait_ge(oh_ready, 1)
        did(dve.tensor_tensor(rh[:, :, 0:4], oh, tokens.to_broadcast([P, 3, 4]), ALU.mult))
        did(dve.tensor_copy(rh[:, :, 4:8], oh))
        did(dve.tensor_tensor(rh[:, :, 8:12], oh, wide(stat[:, 8:11].unsqueeze(2)), ALU.mult))
        dve.wait_ge(rank_done, 1)
        step(dve.tensor_tensor(rank, PS[:, 7, 0:12].rearrange("p (k n) -> p k n", n=4), oh, ALU.mult))
        did(dve.tensor_reduce(R[:, 224:225], PS[:, 7, 12:16], AX.X, ALU.max))
        step(dve.tensor_reduce(pos, rank, AX.X, ALU.add))

        def slots(c):
            for k in range(3):
                dve.tensor_scalar(Pm[:, c, k, :], route[:, (2 + c) * P:(3 + c) * P], R[:, 220 + k:221 + k], None,
                                  ALU.is_equal).then_inc(pm_ready, 1)

        def rows_of(c):
            got, miss = R[:, 328 + 12 * c:340 + 12 * c], R[:, 208 + 4 * c:212 + 4 * c]
            step(dve.tensor_copy(got, PS[:, 4 if c else 6, 64 + 12 * c:76 + 12 * c]))
            step(dve.tensor_scalar(miss, got[:, 4:8], -1.0, 1.0, ALU.mult, ALU.add))
            step(dve.tensor_scalar(miss, miss, spare[:, 0:1], None, ALU.mult))
            step(dve.tensor_tensor(miss, miss, got[:, 0:4], ALU.add))
            step(dve.tensor_copy(pidx[:, 14 + 4 * c:18 + 4 * c], miss))
            dve.tensor_copy(pidx[:, 4 * c:4 * c + 4], got[:, 0:4]).then_inc(rows_ready, 1)
            did(dve.tensor_copy(GT[:, 4 * c:4 * c + 4, 4], got[:, 8:12]))

        for c in range(PASSES):
            slots(c)
        step(dve.memset(pidx[:, 12:14], 0))
        step(dve.memset(GT, 0.0))
        dve.wait_ge(idx_done, 1)
        rows_of(0)
        step(dve.tensor_tensor(leg, le[:, :, 0:4], wide(oh[:, :, 0:1]), ALU.mult))
        for g in range(1, 4):
            step(dve.tensor_tensor(work, le[:, :, 4 * g:4 * g + 4], wide(oh[:, :, g:g + 1]), ALU.mult))
            step(dve.tensor_tensor(leg, leg, work, ALU.add))
        step(dve.tensor_reduce(m1, leg, AX.X, ALU.max))
        first_of(top, leg, m1)
        step(dve.tensor_scalar(work, top, NEG, None, ALU.mult))
        step(dve.tensor_tensor(leg, leg, work, ALU.add))
        step(dve.tensor_reduce(m2, leg, AX.X, ALU.max))
        first_of(work, leg, m2)
        dve.tensor_tensor(ge, m2, m1, ALU.subtract).then_inc(exp_in, 1)
        def quarter_out(n, r, bank):
            dve.tensor_tensor(HTG[n][:, 4 * r:4 * r + 4, :], PS[:, bank, :].rearrange("p (c t) -> p c t", c=4),
                              ln2T[:, 4 * r:4 * r + 4].unsqueeze(2).to_broadcast([P, 4, P]),
                              ALU.mult).then_inc(htg_moved, 1)

        dve.wait_ge(expd, 2)
        step(dve.tensor_reduce(m1, expg, AX.X, ALU.add))
        step(dve.tensor_scalar(tmp3, ge, 1.0, None, ALU.add))
        step(dve.tensor_tensor(m1, m1, tmp3, ALU.mult))
        step(dve.reciprocal(m1, m1))
        step(dve.tensor_tensor(m2, m1, ge, ALU.mult))
        step(dve.tensor_tensor(gate4, top, wide(m1), ALU.mult))
        step(dve.tensor_tensor(work, work, wide(m2), ALU.mult))
        step(dve.tensor_tensor(gate4, gate4, work, ALU.add))
        rg = R[:, 232:280].rearrange("p (k g v) -> p k g v", g=NG, v=4)
        for g in range(NG):
            did(dve.tensor_tensor(rg[:, :, g, :], gate4, wide(oh[:, :, g:g + 1]), ALU.mult))
        settle()
        dve.memset(stat[:, 110:111], 0.0).then_inc(gates_ready, 1)
        dve.wait_ge(gathered[0], 16)
        dve.tensor_scalar(HN, XG[0], GT[:, 0, 4:5], None, ALU.mult).then_inc(hn_ready, 1)
        for r, bank in enumerate(FIRST_BANKS):
            dve.wait_ge(htg_turned, r + 1)
            quarter_out(0, r, bank)

        def rows_in(it, n, ahead):
            dve.wait_ge(gathered[n], it * 16 + 16 * (ahead + 1))
            dve.wait_ge(htg_turned, it * 8 + 4 * (n + 2 * ahead))
            scaled_rows(n, it * 2 + (n + 2 * ahead), it * 2 + (n + 2 * ahead + 1))

        def scaled_rows(n, group, nth):
            dve.tensor_copy(GS[n].unsqueeze(1), GT[:, bass.ds(group, 1), :]).then_inc(gs_ready, 1)
            dve.wait_ge(gs_ready, nth)
            dve.tensor_scalar(HN, XG[n], GS[n][:, 4:5], None, ALU.mult).then_inc(hn_ready, 1)

        dve.wait_ge(idx_done, 2 * PASSES)
        for c in range(1, PASSES):
            rows_of(c)
        for c in range(PASSES):
            did(dve.tensor_copy(GT[:, 4 * c:4 * c + 4, 0:4],
                                PS[:, 3, 64 + 16 * c:80 + 16 * c].rearrange("p (g v) -> p g v", v=4)))
        settle()
        dve.tensor_copy(GS[0].unsqueeze(1), GT[:, 0:1, :]).then_inc(gs_ready, 1)
        dve.sem_inc(out_rows, 4)
        dve.tensor_copy(pidx[:, 28:29], R[:, 224:225]).then_inc(idx_ready, 1)
        dve.wait_ge(idx_ready, 1)

        def experts(it):
            def turned_out(j):
                dve.wait_ge(htg_turned, it * 8 + (j + 5))
                quarter_out(1 - j // 4, j % 4, 7)

            def hidden(k):
                dve.wait_ge(sil_ready, it * 8 + (k + 1))
                dve.wait_ge(up_done, it * 8 + (k + 2))
                if k:
                    dve.wait_ge(hidT_done, it * 8 + k)
                dve.scalar_tensor_tensor(HID, SIL, GS[k // 4][:, k % 4:k % 4 + 1], PS[:, 1, :],
                                         ALU.mult, ALU.mult).then_inc(hid_ready, 1)

            def rows_out(n):
                for q in range(4):
                    if q < 3:
                        dve.wait_ge(down_part, it * 6 + (3 * n + q + 1))
                    else:
                        dve.wait_ge(down_done, it * 8 + (4 * n + 5))
                    v = XG[n][:, q * TILE:(q + 1) * TILE]
                    dve.tensor_tensor(v, PS[:, 3 + q, :], v, ALU.add).then_inc(out_rows, 1)

            rows_in(it, 1, 0)
            for k in range(8):
                if k % 4 == 3:
                    turned_out(k - 1)
                hidden(k)
                if k == 4:
                    rows_out(0)
                if k % 4:
                    if k == 5:
                        rows_in(it, 0, 1)
                    turned_out((k - 1, k - 1, k)[k % 4 - 1])
            rows_out(1)

        with dve.Fori(0, 2) as it:
            experts(it)
        most = dve.value_load(pidx[0:1, 28:29], min_val=0, max_val=TOK)
        with dve.If(most > P):
            with dve.Fori(1, PASSES) as c:
                with dve.Fori(0, 2) as j:
                    experts(c * 2 + j)


_OUTS = [("y", (TOK + P, D)), ("k_prompt", (1, 1, SEQ, H, HD)), ("v_prompt", (1, 1, SEQ, H, HD)),
         ("pool_prompt", (1, 1, BUF, PW)), ("k_sample", (1, DEC_B, DEC_T, H, HD)),
         ("v_sample", (1, DEC_B, DEC_T, H, HD)), ("pool_sample", (1, DEC_B, BUF, PW))]


def small_inputs(i):
    s = np.zeros((P, 588), np.float32)
    s[:, 0:16] = i["ln1_w"][0].reshape(DC, P).T
    s[:, 16:32] = i["ln2_w"][0].reshape(DC, P).T
    s[:, 32:96] = i["q_norm_w"][0][None]
    s[:, 96:160] = i["k_norm_w"][0][None]
    s[:, 160:168] = i["pool_scale"][0].reshape(8, P).T
    s[:, 168:488].reshape(P, DC, 20)[:, :, 0:4] = i["w_router_group"][0].reshape(DC, P, 4).transpose(1, 0, 2)
    s[:, 168:488].reshape(P, DC, 20)[:, :, 4:20] = i["w_router_expert"][0].reshape(DC, P, 16).transpose(1, 0, 2)
    s[:, 488:492] = i["b_router_group"][0][None]
    s[:, 492:508] = i["b_router_expert"][0][None]
    rel = i["rel_bias"]
    for t in range(4):
        s[32 * t:32 * t + 32, 508 + 16 * t:524 + 16 * t] = rel.reshape(NB, 8, 2).transpose(0, 2, 1).reshape(NB, 16)
    s[0:32, 572:588] = rel
    s[32, 572:588] = 1.0
    return s


def kernel(**inputs):
    import concourse.bacc as _bacc
    from concourse.bass_utils import run_bass_kernel_spmd as _run

    inputs = {k: np.asarray(v) for k, v in inputs.items()}
    nc = _bacc.Bacc("TRN2", target_bir_lowering=False, num_devices=1)
    arrays, a, o = {}, {}, {}
    given = {n: inputs[n] for n in ("x_prompt", "x_sample", "cache_k", "cache_v", "state_pool", "w_in", "w_pool",
                                    "w_o", "w_gate", "w_up", "w_down")}
    given["small"] = small_inputs(inputs)
    given.update(shape_constants())
    for name, v in given.items():
        v = np.ascontiguousarray(v)
        arrays[f"in_{name}"] = v
        a[name] = nc.dram_tensor(f"in_{name}", v.shape, mybir.dt.from_np(v.dtype), kind="ExternalInput").ap()
    for name, shape in _OUTS:
        o[name] = nc.dram_tensor(f"out_{name}", shape, F32, kind="ExternalOutput").ap()
    hybrid_layer(nc, a, o)
    r = _run(nc, [arrays], core_ids=[0]).results[0]
    y = r["out_y"]
    return (y[0:SEQ].reshape(1, SEQ, D), y[SEQ:TOK].reshape(DEC_B, DEC_T, D),
            r["out_k_prompt"], r["out_v_prompt"], r["out_pool_prompt"],
            r["out_k_sample"], r["out_v_sample"], r["out_pool_sample"])
```
